# Optimizing a Trainium2 kernel written in Bass

```python
import jax
import jax.numpy as jnp
from jax import lax

D_MODEL = 1024
BATCH = 1
SEQ = 256
DEPTH = 2
DEC_BATCH = 1
DEC_SEQ = 64
PAST_LEN = 512

CHUNK = 64
N_A = DEPTH // 2
N_B = DEPTH - N_A
RW_HEAD = 64
RW_HEADS = D_MODEL // RW_HEAD
LORA_W = 64
LORA_A = 64
LORA_G = 160
N_MU = 6
GN_EPS = 64e-5
HEAD_DIM = 64
N_HEADS = D_MODEL // HEAD_DIM
N_KV = N_HEADS // 4
Q_PER_KV = N_HEADS // N_KV
WINDOW = 128
WIN_CHUNKS = WINDOW // CHUNK
ROPE_DIM = HEAD_DIM // 4
ROPE_THETA = 500000.0
ATT_SCALE = HEAD_DIM ** -0.5
N_GROUPS = 4
EXP_PER_GROUP = 8
N_EXPERTS = N_GROUPS * EXP_PER_GROUP
TOP_K = 2
D_EXPERT = D_MODEL // 4
RMS_EPS = 1e-6
NEG_INF = -1e30

kernel_name = 'yoco_rwkv7_swa_sink_hmoe_stream_step'

def rmsnorm(x, g):
    xf = x.astype(jnp.float32)
    y = xf * lax.rsqrt(jnp.mean(xf * xf, axis=-1, keepdims=True) + RMS_EPS)
    return (y * g.astype(jnp.float32)).astype(x.dtype)

def modulate(h, shift, scale):
    return h * (1 + scale[:, None, :]) + shift[:, None, :]

def rope_partial(x, pos):
    half = ROPE_DIM // 2
    inv = jnp.power(jnp.float32(ROPE_THETA), -jnp.arange(half, dtype=jnp.float32) * (2.0 / ROPE_DIM))
    ang = pos[:, None] * inv[None, :]
    cos = jnp.cos(ang)[None, :, None, :]
    sin = jnp.sin(ang)[None, :, None, :]
    xr = x[..., :ROPE_DIM].astype(jnp.float32)
    x1, x2 = xr[..., :half], xr[..., half:]
    rot = jnp.concatenate([x1 * cos - x2 * sin, x2 * cos + x1 * sin], axis=-1)
    return jnp.concatenate([rot.astype(x.dtype), x[..., ROPE_DIM:]], axis=-1)

def wkv_step(state, inp):
    r, w, k, v, a, b = inp
    sa = jnp.einsum('bhvk,bhk->bhv', state, a)
    state = state * w[:, :, None, :] + sa[..., None] * b[:, :, None, :] + v[..., None] * k[:, :, None, :]
    return state, jnp.einsum('bhvk,bhk->bhv', state, r)

def rwkv7_time_mix(h, prev_x, prev_wkv, p, l):
    B, S, D = h.shape
    shifted = jnp.concatenate([prev_x[:, None, :].astype(h.dtype), h[:, :-1]], axis=1)
    xm = h[:, :, None, :] + (shifted - h)[:, :, None, :] * p['rw_mu'][l].astype(h.dtype)
    rkv = jnp.einsum('bsnd,nde->bsne', xm[:, :, :3], p['rw_w_rkv'][l])
    r, k, v = rkv[:, :, 0], rkv[:, :, 1], rkv[:, :, 2]
    xw, xa, xg = xm[:, :, 3], xm[:, :, 4], xm[:, :, 5]
    w_log = -jax.nn.softplus(-(p['rw_w0'][l] + jnp.tanh(xw @ p['rw_w1'][l]) @ p['rw_w2'][l])) - 0.5
    a = jax.nn.sigmoid(p['rw_a0'][l] + (xa @ p['rw_a1'][l]) @ p['rw_a2'][l])
    g = jax.nn.sigmoid(xg @ p['rw_g1'][l]) @ p['rw_g2'][l]

    def heads(t):
        return t.reshape(B, S, RW_HEADS, RW_HEAD).astype(jnp.float32)

    kk = heads(k * p['rw_k_k'][l])
    kk = kk * lax.rsqrt(jnp.maximum(jnp.sum(kk * kk, axis=-1, keepdims=True), 1e-24))
    k = k * (1 + (a - 1) * p['rw_k_a'][l])
    decay = jnp.exp(-jnp.exp(heads(w_log)))
    rh, kh, vh, ah = heads(r), heads(k), heads(v), heads(a)
    xs = tuple(jnp.moveaxis(t, 1, 0) for t in (rh, decay, kh, vh, -kk, kk * ah))
    final, ys = lax.scan(wkv_step, prev_wkv.astype(jnp.float32), xs)
    y = jnp.moveaxis(ys, 0, 1)
    mu = jnp.mean(y, axis=-1, keepdims=True)
    var = jnp.mean(jnp.square(y - mu), axis=-1, keepdims=True)
    y = ((y - mu) * lax.rsqrt(var + GN_EPS)).reshape(B, S, D) * p['rw_lnx_w'][l].astype(jnp.float32) + p['rw_lnx_b'][l].astype(jnp.float32)
    bonus = jnp.sum(rh * kh * p['rw_r_k'][l].astype(jnp.float32), axis=-1, keepdims=True) * vh
    out = ((y + bonus.reshape(B, S, D)) * g.astype(jnp.float32)).astype(h.dtype) @ p['rw_w_o'][l]
    return out, h[:, -1], final.astype(prev_wkv.dtype)

def hier_moe(h, p, l):
    wg, we = p['moe_w_group'][l], p['moe_w_expert'][l]
    w_gu, w_down = p['moe_w_gu'][l], p['moe_w_down'][l]

    def per_sequence(t):
        S = t.shape[0]
        lg = (t @ wg).astype(jnp.float32)
        gi = jnp.argmax(lg, axis=-1)
        gp = jnp.take_along_axis(jax.nn.softmax(lg, axis=-1), gi[:, None], axis=1)[:, 0]
        le = (t @ we).astype(jnp.float32).reshape(S, N_GROUPS, EXP_PER_GROUP)
        le = jnp.take_along_axis(le, gi[:, None, None], axis=1)[:, 0]
        tv, ti = lax.top_k(jax.nn.softmax(le, axis=-1), TOP_K)
        tw = tv / jnp.sum(tv, axis=-1, keepdims=True) * gp[:, None]
        eidx = gi[:, None] * EXP_PER_GROUP + ti
        cw = jnp.sum(jax.nn.one_hot(eidx, N_EXPERTS, dtype=jnp.float32) * tw[..., None], axis=1)
        gu = jnp.einsum('sd,edf->sef', t, w_gu)
        hid = jax.nn.silu(gu[..., :D_EXPERT]) * gu[..., D_EXPERT:] * cw[..., None].astype(t.dtype)
        return jnp.einsum('sef,efd->sd', hid, w_down)

    return lax.map(per_sequence, h)

def shared_kv(x, c, pos, p):
    mod = jax.nn.silu(c) @ p['kv_ada_w'] + p['kv_ada_b']
    shift, scale = jnp.split(mod, 2, axis=-1)
    h = modulate(rmsnorm(x, p['kv_norm_g']), shift, scale)
    B, S, _ = x.shape
    kv = (h @ p['w_kv'] + p['b_kv']).reshape(B, S, 2, N_KV, HEAD_DIM)
    return rope_partial(kv[:, :, 0], pos), kv[:, :, 1]

def sink_probs(s, sink, mask):
    if mask is not None:
        s = jnp.where(mask, s, NEG_INF)
    m = jnp.maximum(jnp.max(s, axis=-1, keepdims=True), sink)
    e = jnp.exp(s - m)
    return e / (jnp.sum(e, axis=-1, keepdims=True) + jnp.exp(sink - m))

def banded_window_attn(q, k, v, sinks):
    B, S, H, hd = q.shape
    NC = S // CHUNK
    qc = q.reshape(B, NC, CHUNK, N_KV, Q_PER_KV, hd)

    def band(t):
        tc = t.reshape(B, NC, CHUNK, N_KV, hd)
        tp = jnp.pad(tc, ((0, 0), (WIN_CHUNKS, 0), (0, 0), (0, 0), (0, 0)))
        return jnp.concatenate([tp[:, i:i + NC] for i in range(WIN_CHUNKS + 1)], axis=2)

    kb, vb = band(k), band(v)
    s = jnp.einsum('bnqkgd,bnskd->bnkgqs', qc, kb).astype(jnp.float32) * ATT_SCALE
    slot_chunk = jnp.arange(NC)[:, None] - WIN_CHUNKS + jnp.arange((WIN_CHUNKS + 1) * CHUNK)[None, :] // CHUNK
    mask = (slot_chunk >= 0)[None, :, None, None, None, :]
    sink = sinks.astype(jnp.float32).reshape(N_KV, Q_PER_KV)[None, None, :, :, None, None]
    probs = sink_probs(s, sink, mask)
    o = jnp.einsum('bnkgqs,bnskd->bnqkgd', probs.astype(vb.dtype), vb)
    return o.reshape(B, S, H * hd)

def recent_window_attn(q, k_all, v_all, sinks):
    B, T, H, hd = q.shape
    qg = q.reshape(B, T, N_KV, Q_PER_KV, hd)
    s = jnp.einsum('btkgd,bskd->bkgts', qg, k_all).astype(jnp.float32) * ATT_SCALE
    sink = sinks.astype(jnp.float32).reshape(N_KV, Q_PER_KV)[None, :, :, None, None]
    probs = sink_probs(s, sink, None)
    o = jnp.einsum('bkgts,bskd->btkgd', probs.astype(v_all.dtype), v_all)
    return o.reshape(B, T, H * hd)

def window_attn(h, pos, k, v, past_k, past_v, p, j):
    B, S, _ = h.shape
    q = (h @ p['at_w_q'][j] + p['at_b_q'][j]).reshape(B, S, N_HEADS, HEAD_DIM)
    q = rope_partial(q, pos)
    if past_k is None:
        o = banded_window_attn(q, k, v, p['at_sinks'][j])
    else:
        k_all = jnp.concatenate([past_k.astype(k.dtype), k], axis=1)
        v_all = jnp.concatenate([past_v.astype(v.dtype), v], axis=1)
        o = recent_window_attn(q, k_all, v_all, p['at_sinks'][j])
    return o @ p['at_w_o'][j] + p['at_b_o'][j]

def run_trunk(x, c, pos, prev_x, prev_wkv, past_k, past_v, p):
    cs = jax.nn.silu(c)
    new_x, new_wkv = [], []
    k = v = None
    for l in range(DEPTH):
        mod = cs @ p['ada_w'][l] + p['ada_b'][l]
        sh1, sc1, g1, sh2, sc2, g2 = jnp.split(mod, 6, axis=-1)
        if l >= N_A and k is None:
            k, v = shared_kv(x, c, pos, p)
        h = modulate(rmsnorm(x, p['norm_g'][l, 0]), sh1, sc1)
        if l < N_A:
            y, last_x, st = rwkv7_time_mix(h, prev_x[l], prev_wkv[l], p, l)
            new_x.append(last_x)
            new_wkv.append(st)
        else:
            y = window_attn(h, pos, k, v, past_k, past_v, p, l - N_A)
        x = x + g1[:, None, :] * y
        h = modulate(rmsnorm(x, p['norm_g'][l, 1]), sh2, sc2)
        x = x + g2[:, None, :] * hier_moe(h, p, l)
    return rmsnorm(x, p['final_norm_g']), jnp.stack(new_x), jnp.stack(new_wkv), k, v

def setup_inputs(seed: int = 0) -> dict:
    key = jax.random.key(seed)
    ks = iter(jax.random.split(key, 64))
    f32 = jnp.float32

    def nrm(shape, scale):
        return jax.random.normal(next(ks), shape, f32) * scale

    D = D_MODEL
    cache_rows = min(WINDOW, PAST_LEN)
    HQ = N_HEADS * HEAD_DIM
    KVW = 2 * N_KV * HEAD_DIM
    return {
        'x_prompt': nrm((BATCH, SEQ, D), 1.0),
        'x_sample': nrm((DEC_BATCH, DEC_SEQ, D), 1.0),
        'state_shift': nrm((N_A, DEC_BATCH, D), 1.0),
        'state_wkv': nrm((N_A, DEC_BATCH, RW_HEADS, RW_HEAD, RW_HEAD), 0.05),
        'cache_k': nrm((DEC_BATCH, cache_rows, N_KV, HEAD_DIM), 1.0),
        'cache_v': nrm((DEC_BATCH, cache_rows, N_KV, HEAD_DIM), 1.0),
        'c_prompt': nrm((BATCH, D), 1.0),
        'c_sample': nrm((DEC_BATCH, D), 1.0),
        'ada_w': nrm((DEPTH, D, 6 * D), 0.5 * D ** -0.5),
        'ada_b': nrm((DEPTH, 6 * D), 0.02),
        'norm_g': 1.0 + nrm((DEPTH, 2, D), 0.05),
        'rw_mu': jax.random.uniform(next(ks), (N_A, N_MU, D), f32),
        'rw_w_rkv': nrm((N_A, 3, D, D), D ** -0.5),
        'rw_w0': nrm((N_A, D), 0.5) - 1.0,
        'rw_w1': nrm((N_A, D, LORA_W), D ** -0.5),
        'rw_w2': nrm((N_A, LORA_W, D), 0.1 * LORA_W ** -0.5),
        'rw_a0': nrm((N_A, D), 0.1),
        'rw_a1': nrm((N_A, D, LORA_A), D ** -0.5),
        'rw_a2': nrm((N_A, LORA_A, D), 0.1 * LORA_A ** -0.5),
        'rw_g1': nrm((N_A, D, LORA_G), D ** -0.5),
        'rw_g2': nrm((N_A, LORA_G, D), LORA_G ** -0.5),
        'rw_k_k': 0.85 + nrm((N_A, D), 0.05),
        'rw_k_a': 1.0 + nrm((N_A, D), 0.05),
        'rw_r_k': nrm((N_A, RW_HEADS, RW_HEAD), 0.1),
        'rw_lnx_w': 1.0 + nrm((N_A, D), 0.05),
        'rw_lnx_b': nrm((N_A, D), 0.02),
        'rw_w_o': nrm((N_A, D, D), D ** -0.5),
        'kv_ada_w': nrm((D, 2 * D), 0.5 * D ** -0.5),
        'kv_ada_b': nrm((2 * D,), 0.02),
        'kv_norm_g': 1.0 + nrm((D,), 0.05),
        'w_kv': nrm((D, KVW), D ** -0.5),
        'b_kv': nrm((KVW,), 0.02),
        'at_w_q': nrm((N_B, D, HQ), D ** -0.5),
        'at_b_q': nrm((N_B, HQ), 0.02),
        'at_sinks': nrm((N_B, N_HEADS), 0.5),
        'at_w_o': nrm((N_B, HQ, D), HQ ** -0.5),
        'at_b_o': nrm((N_B, D), 0.02),
        'moe_w_group': nrm((DEPTH, D, N_GROUPS), D ** -0.5),
        'moe_w_expert': nrm((DEPTH, D, N_EXPERTS), D ** -0.5),
        'moe_w_gu': nrm((DEPTH, N_EXPERTS, D, 2 * D_EXPERT), D ** -0.5),
        'moe_w_down': nrm((DEPTH, N_EXPERTS, D_EXPERT, D), D_EXPERT ** -0.5),
        'final_norm_g': 1.0 + nrm((D,), 0.05),
    }

def reference(x_prompt, x_sample, state_shift, state_wkv, cache_k, cache_v, c_prompt, c_sample,
              ada_w, ada_b, norm_g, rw_mu, rw_w_rkv, rw_w0, rw_w1, rw_w2, rw_a0, rw_a1, rw_a2,
              rw_g1, rw_g2, rw_k_k, rw_k_a, rw_r_k, rw_lnx_w, rw_lnx_b, rw_w_o,
              kv_ada_w, kv_ada_b, kv_norm_g, w_kv, b_kv,
              at_w_q, at_b_q, at_sinks, at_w_o, at_b_o,
              moe_w_group, moe_w_expert, moe_w_gu, moe_w_down, final_norm_g):
    p = dict(ada_w=ada_w, ada_b=ada_b, norm_g=norm_g, rw_mu=rw_mu, rw_w_rkv=rw_w_rkv,
             rw_w0=rw_w0, rw_w1=rw_w1, rw_w2=rw_w2, rw_a0=rw_a0, rw_a1=rw_a1, rw_a2=rw_a2,
             rw_g1=rw_g1, rw_g2=rw_g2, rw_k_k=rw_k_k, rw_k_a=rw_k_a, rw_r_k=rw_r_k,
             rw_lnx_w=rw_lnx_w, rw_lnx_b=rw_lnx_b, rw_w_o=rw_w_o,
             kv_ada_w=kv_ada_w, kv_ada_b=kv_ada_b, kv_norm_g=kv_norm_g, w_kv=w_kv, b_kv=b_kv,
             at_w_q=at_w_q, at_b_q=at_b_q, at_sinks=at_sinks, at_w_o=at_w_o, at_b_o=at_b_o,
             moe_w_group=moe_w_group, moe_w_expert=moe_w_expert, moe_w_gu=moe_w_gu,
             moe_w_down=moe_w_down, final_norm_g=final_norm_g)
    B, S, _ = x_prompt.shape
    T = x_sample.shape[1]
    pos_p = jnp.arange(S, dtype=jnp.float32)
    pos_s = PAST_LEN + jnp.arange(T, dtype=jnp.float32)
    zero_x = jnp.zeros((N_A, B, D_MODEL), x_prompt.dtype)
    zero_wkv = jnp.zeros((N_A, B, RW_HEADS, RW_HEAD, RW_HEAD), state_wkv.dtype)
    y_prompt, p_shift, p_wkv, p_k, p_v = run_trunk(x_prompt, c_prompt, pos_p, zero_x, zero_wkv, None, None, p)
    y_sample, s_shift, s_wkv, s_k, s_v = run_trunk(x_sample, c_sample, pos_s, state_shift, state_wkv, cache_k, cache_v, p)
    keep = min(WINDOW, S)
    return (y_prompt, y_sample, p_shift, p_wkv, p_k[:, S - keep:], p_v[:, S - keep:], s_shift, s_wkv, s_k, s_v)


_drawn_inputs = setup_inputs


def setup_inputs(seed=0):
    import zlib

    import numpy as np

    out = dict(_drawn_inputs(seed))
    spreads = {}
    factors = {'state_wkv': 7.31,
     'rw_w1': 3.571,
     'rw_w2': 3.448,
     'rw_k_k': 7.641,
     'rw_lnx_w': 4.483,
     'rw_lnx_b': 17.46,
     'b_kv': 2.761,
     'at_b_q': 64.0,
     'at_sinks': 21.921,
     'at_b_o': 6.42,
     'cache_k': 3.064}
    for name, (base, spread) in spreads.items():
        noise = np.random.default_rng([zlib.crc32(name.encode()), seed]).standard_normal(out[name].shape)
        drawn = base * np.exp(spread * noise) if base else spread * noise
        out[name] = jnp.asarray(drawn.astype(out[name].dtype))
    for name, factor in factors.items():
        out[name] = (out[name] * factor).astype(out[name].dtype)
    return out
```

```python
from contextlib import ExitStack

import numpy as np

import concourse.bass as bass
from concourse import mybir

F32 = mybir.dt.float32
I32 = mybir.dt.int32
ALU = mybir.AluOpType
ACT = mybir.ActivationFunctionType
AX = mybir.AxisListType

P = 128
D = 1024
C = D // P
SEQ, DEC = 256, 64
T = SEQ + DEC
CH = 64
NCH = T // CH
HD = 64
HEADS = D // HD
NKV = 4
ROPE = HD // 4
PAST = 512
EXP, GROUPS, EPG = 32, 4, 8
FE = D // 4
SLOTS = 64
LW, LA, LG = 64, 64, 160
RMS_EPS = 1e-6
GN_EPS = 64e-5
DECAY = float(np.exp(-0.5))
SCALE = HD ** -0.5
TILES = [(0, 128), (128, 128), (256, 64)]
SEQS = [(0, 0, SEQ), (1, SEQ, DEC)]

VEC_GROUPS = [
    [("c_prompt", 8), ("c_sample", 8), ("norm_g", 32), ("rw_mu", 48), ("rw_w0", 8), ("rw_a0", 8), ("rw_k_k", 8),
     ("rw_k_a", 8)],
    [("ada_b", 96), ("kv_ada_b", 16), ("rw_r_k", 8), ("rw_lnx_w", 8)],
    [("rw_lnx_b", 8), ("kv_norm_g", 8), ("at_b_q", 8), ("at_b_o", 8), ("final_norm_g", 8), ("b_kv", 4),
     ("state_shift", 8)],
]
VCOL = {}
for _g, _rows in enumerate(VEC_GROUPS):
    _o = P * _g
    for _n, _k in _rows:
        VCOL[_n] = _o
        _o += _k

CONST = [("ident", 128), ("ones", 128), ("triu", 128), ("selh", 128), ("iota", 64), ("i64", 64)]
WKVC = [("maskA", 128), ("lev", 6 * 64), ("lev1n", 64), ("scan", T), ("selb", 1024)]
ATTC = [("cos", T), ("sin", T), ("ropep", 128), ("swap", 128)]


def offsets(table):
    out, o = {}, 0
    for n, k in table:
        out[n] = (o, k)
        o += k
    return out, o


CO, CN = offsets(CONST)
WO, WN = offsets(WKVC)
AO, AN = offsets(ATTC)


def constants():
    p = np.arange(P)
    c = np.zeros((P, CN), np.float32)

    def put(a, off, name, v):
        o, k = off[name]
        a[:v.shape[0], o:o + k] = v

    put(c, CO, "ident", np.eye(P))
    put(c, CO, "ones", np.ones((P, P)))
    put(c, CO, "triu", (p[:, None] <= p[None, :]))
    m = np.arange(P)
    put(c, CO, "selh", ((m % 16)[None, :] == 2 * (m // 16)[None, :] + (p // HD)[:, None]))
    put(c, CO, "iota", np.broadcast_to(np.arange(1, 65), (P, 64)))
    put(c, CO, "i64", ((p % 64)[:, None] == np.arange(64)[None, :]))
    w = np.zeros((P, WN), np.float32)
    s, t = (p % 64)[:, None], np.arange(64)[None, :]
    put(w, WO, "maskA", np.concatenate([s < t, s <= t], 1))
    lev = []
    for l in range(1, 7):
        b = 1 << l
        lev.append((s // b == t // b) & (s % b < b // 2) & (t % b >= b // 2))
    put(w, WO, "lev", np.concatenate(lev, 1))
    put(w, WO, "lev1n", (s // 2 == t // 2) & (t % 2 == 0) & (s % 2 == 1))
    put(w, WO, "scan", np.broadcast_to(np.arange(T) % CH != 0, (P, T)))
    q = np.arange(1024)
    put(w, WO, "selb", (np.arange(16)[:, None] == (2 * (q // P) + (q % P) // HD)[None, :]))
    a = np.zeros((P, AN), np.float32)
    half = ROPE // 2
    inv = np.power(np.float32(500000.0), -np.arange(half, dtype=np.float32) * np.float32(2.0 / ROPE)).astype(np.float32)
    pos = np.concatenate([np.arange(SEQ), PAST + np.arange(DEC)]).astype(np.float32)
    ang = (pos[None, :] * inv[:, None]).astype(np.float32)
    d = p % HD
    cos, sin = np.ones((P, T), np.float32), np.zeros((P, T), np.float32)
    cos[d < ROPE] = np.cos(ang)[d[d < ROPE] % half]
    sin[d < ROPE] = np.sin(ang)[d[d < ROPE] % half]
    put(a, AO, "cos", cos)
    put(a, AO, "sin", sin)
    rp = np.zeros((P, P), np.float32)
    for h in (0, HD):
        for j in range(half):
            rp[h + half + j, h + j] = -1.0
            rp[h + j, h + half + j] = 1.0
    put(a, AO, "ropep", rp)
    put(a, AO, "swap", (p[:, None] == (p[None, :] + HD) % P))
    return {"const_all": c, "const_wkv": w, "const_att": a}


class Counts:

    def __init__(self):
        self.at, self.bank = {}, {}


class Engine:

    def __init__(self, eng, name, sems, known, seen):
        self.e, self.name, self.sems, self.known, self.seen = eng, name, sems, known, seen
        self.n, self.waited = 0, {}

    def did(self, ins, *keys):
        ins.then_inc(self.sems[self.name], 1)
        self.n += 1
        for k in keys:
            self.seen.at[k] = (self.name, self.n)

    def wait(self, *key):
        if self.known is None:
            return
        who, n = self.known.at[key]
        if self.waited.get(who, 0) < n:
            self.waited[who] = n
            self.e.wait_ge(self.sems[who], n)

    def settle(self):
        if self.n and self.waited.get(self.name, 0) < self.n:
            self.waited[self.name] = self.n
            self.e.wait_ge(self.sems[self.name], self.n)


class Banks:

    def __init__(self, pe, ps):
        self.pe, self.ps, self.n, self.owner = pe, ps, 0, [None] * 8

    def open(self, *key):
        b = self.n % 8
        self.n += 1
        if self.owner[b] is not None:
            self.pe.wait("read", *self.owner[b])
        self.owner[b] = key
        self.pe.seen.bank[key] = b
        return self.ps[b]


def build(nc, i, o, known, seen):
    ctx = ExitStack()
    with ctx:
        def sb(name, shape, dt=F32):
            return ctx.enter_context(nc.sbuf_tensor(name, shape, dt))

        def sem(name):
            return ctx.enter_context(nc.semaphore(name))

        ps = [ctx.enter_context(nc.psum_tensor(f"bank{b}", [P, 512], F32)) for b in range(8)]
        SLOT = 6144
        B = C * T
        xt_ = sb("x_res", [P, B])
        ring = sb("ring", [P, 4 * SLOT])
        work = sb("work", [P, 8 * B])
        const = sb("const", [P, CN])
        cph = sb("const_phase", [P, max(WN, AN)])
        vec = sb("vec", [P, 3 * P])
        cs = sb("cs", [P, C, 32])
        mod = sb("mod", [P, 2, 2, 48])
        kvmod = sb("kvmod", [P, 2, 16])
        coef = sb("coef", [P, 2, C])
        rstd = sb("rstd", [P, T])
        state = sb("state", [P, 2, C, HD])
        dend = sb("dend", [P, C, NCH])
        sink = sb("sink", [P, C])
        att = sb("att", [P, 6, C])
        bog = sb("bog", [P, 2, C])
        passes = sb("passes", [P, 4], I32)
        small = sb("small", [P, 16])

        names = ["pe_done", "act_done", "dve_done", "pool_done"]
        sems = {n: sem(n) for n in names}
        ring_in = [sem(f"ring_in{s}") for s in range(4)]
        in_sems = {n: sem(n) for n in ("const_in", "vec_in", "x_in", "wkvc_in", "attc_in", "sink_in", "cache_in",
                                       "swkv_in", "router_in0", "router_in1", "out_written")}
        moe_sems = [{n: sem(f"{n}{l}") for n in (
            "gu_in0", "gu_in1", "gu_in2", "gu_in3", "dn_in0", "dn_in1", "dn_in2", "dn_in3",
            "pos_ready", "sel_ready", "selT_made", "selT_ready", "xe_made", "xe_ready",
            "gu_made", "silu_ready", "h_ready", "hT_made", "hT_ready", "down_made", "down_ready",
            "y_made", "y_added")} for l in range(2)]

        def cst(n, rows=P):
            a, k = CO[n]
            return const[0:rows, a:a + k]

        def wcst(n, rows=P):
            a, k = WO[n]
            return cph[0:rows, a:a + k]

        def acst(n):
            a, k = AO[n]
            return cph[:, a:a + k]

        def vcol(n, c, k=1):
            return vec[:, VCOL[n] + c:VCOL[n] + c + k]

        def slot(s, n=SLOT):
            return ring[:, s * SLOT:s * SLOT + n]

        def w512(s):
            return slot(s, 4096).rearrange("p (c n) -> p c n", c=C)

        def buf(t, off=0):
            return t[:, off:off + B].rearrange("p (c t) -> p c t", c=C)

        x = buf(xt_)
        E = [buf(work, B * n) for n in range(8)]
        Fb = [buf(ring, 2 * SLOT + B * n) for n in range(4)]
        G = [buf(ring, B * n) for n in range(4)]
        h0, diff, xm = E[0], E[1], [E[2], E[3]]
        sig, aa, kb, vb, gb, kk, rr, tmp = Fb[0], Fb[1], Fb[2], E[5], E[4], E[6], E[7], Fb[3]
        nrm, bonus, cum, dec = E[0], E[1], E[2], E[3]
        dinv = E[0]
        arb, aak, ark, tt, nt, tmat, wmat, nl = E[0], E[2], E[3], Fb[0], Fb[3], G[0], G[1], G[2]
        ar = work[:, 6 * B:8 * B].rearrange("p (b c t) -> p b c t", b=2, c=C)
        off = [0]

        def wk(n):
            a = off[0]
            off[0] += n
            return work[:, a:a + n]

        hT = wk(B).rearrange("p (c t) -> p c t", c=C)
        htok = wk(3 * D).rearrange("p (j d) -> p j d", j=3)
        ysum = wk(B).rearrange("p (c t) -> p c t", c=C)
        xe = wk(2 * C * P).rearrange("p (u c s) -> p u c s", u=2, c=C)
        dslot = wk(2 * D).rearrange("p (u d) -> p u d", u=2)
        silu = wk(2 * FE).rearrange("p (u f) -> p u f", u=2)
        hid = wk(2 * FE).rearrange("p (u f) -> p u f", u=2)
        hidT = wk(2 * 2 * P).rearrange("p (u f s) -> p u f s", u=2, f=2)
        sel = wk(2 * 3 * P).rearrange("p (u j s) -> p u j s", u=2, j=3)
        selw = wk(2 * 3 * P).rearrange("p (u j s) -> p u j s", u=2, j=3)
        selT = wk(2 * T).rearrange("p (u t) -> p u t", u=2)
        router = wk(C * 36).rearrange("p (c n) -> p c n", c=C)
        lg = wk(3 * 36).rearrange("p (j n) -> p j n", j=3)
        cw = wk(3 * EXP).rearrange("p (j e) -> p j e", j=3)
        msk = wk(3 * EXP).rearrange("p (j e) -> p j e", j=3)
        posn = wk(3 * EXP).rearrange("p (j e) -> p j e", j=3)
        rt = wk(40 * 12).rearrange("p (n k) -> p n k", n=40)
        g48 = wk(3 * 4 * 8).rearrange("p (j g e) -> p j g e", j=3, g=4)
        hkv, haq, q, qt, oT = E[1], E[5], E[6], E[7], E[5]
        kT = work[:, 2 * B:2 * B + 4 * 448].rearrange("p (v t) -> p v t", v=4)
        a3 = 3 * B
        vT = work[:, a3:a3 + 640].rearrange("p (c t) -> p c t", c=2)
        kraw = work[:, a3 + 640:a3 + 1280].rearrange("p (c t) -> p c t", c=2)
        krot = work[:, a3 + 1280:a3 + 1920].rearrange("p (c t) -> p c t", c=2)
        ktok = work[:, a3 + 1920:a3 + 2176]
        v64 = work[0:64, 4 * B:4 * B + 7 * 256].rearrange("p (n d) -> p n d", n=7)
        k64 = work[0:64, 4 * B + 1792:4 * B + 2560].rearrange("p (n d) -> p n d", n=3)
        prob = work[:, 0:1536].rearrange("p (c s) -> p c s", c=C)
        pT = work[0:64, 1536:1536 + 3072].rearrange("p (w c s) -> p w c s", w=3, c=C)
        ytok = work[:, 2 * B:2 * B + 3 * D].rearrange("p (j d) -> p j d", j=3)
        xtok = work[:, 0:3 * D].rearrange("p (j d) -> p j d", j=3)
        rows = work[:, 2 * B:2 * B + 3 * P].rearrange("p (g d) -> p g d", g=3)
        modrow = work[:, 6 * B:6 * B + 1536].rearrange("p (b n) -> p b n", b=3)
        tail1, tail3 = 10240, 22528
        rhs_u = ring[:, tail1:tail1 + 1024].rearrange("p (b c k) -> p b c k", b=2, c=C)
        swin = ring[:, tail1 + 1024:tail1 + 1536].rearrange("p (c k) -> p c k", c=C)
        shiftT = ring[:, tail1 + 1536:tail1 + 1792]
        lows = {"w": ring[0:64, tail3:tail3 + T], "a": ring[0:64, tail3 + T:tail3 + 2 * T],
                "g": ring[:, tail3 + 2 * T:tail3 + 3 * T], "g1": ring[0:32, tail3 + 3 * T:tail3 + 4 * T]}
        head16 = ring[0:16, tail3 + 4 * T:tail3 + 5 * T]
        head16b = ring[0:16, tail3 + 5 * T:tail3 + 6 * T]
        swo = ring[:, 2 * SLOT + 3 * B:2 * SLOT + 3 * B + 1024].rearrange("p (r c k) -> p r c k", r=2, c=C)

        def sq_buf(tag):
            return E[7]

        def seen_bank(key):
            return (known or seen).bank.get(key, 0)

        def bc(ap, n):
            return ap.unsqueeze(2).broadcast_to([ap.shape[0], ap.shape[1], n])

        def bmid(ap, n):
            return ap.unsqueeze(1).broadcast_to([ap.shape[0], n, ap.shape[1]])

        ring_plan, ring_at, got = [], {}, [0] * 4

        def plan(name, s, parts):
            got[s] += 16 * parts
            ring_at[name] = (s, got[s])
            ring_plan.append(name)

        for c in range(C):
            plan(("ada", 0, c), c % 4, 1)
        plan(("lora1",), 0, 3)
        plan(("lora2",), 1, 4)
        for n in (0, 1, 2):
            for hf in range(2):
                plan(("rkv", n, hf), hf, 1)
        for hf in range(2):
            plan(("wo", hf), hf, 1)
        for m, cnt in enumerate((3, 3, 2)):
            plan(("kvada", m), m, 1)
        for c in range(C):
            plan(("ada", 1, c), (c + 3) % 4, 1)
        plan(("wkv",), 3, 1)
        for hf in range(2):
            plan(("wq", hf), hf, 1)
        for hf in range(2):
            plan(("ao", hf), 2 + hf, 1)

        def arrived(en, *name):
            s, n = ring_at[name]
            en.e.wait_ge(ring_in[s], n)
            return s

        block = ctx.enter_context(nc.Block())
        rank = {"n": 0}

        @block.sync
        def _(eng):
            sp = Engine(eng, "sp", sems, known, seen)
            mine = {}

            def load(name, pairs):
                s, _n = ring_at[name]
                if mine.get(s) is not None:
                    sp.wait("used", *mine[s])
                mine[s] = name
                for dst, src in pairs:
                    eng.dma_start(dst, src).then_inc(ring_in[s], 16)

            def ada_load(l, c):
                s, _n = ring_at[("ada", l, c)]
                load(("ada", l, c), [(slot(s), i["ada_w"][l, c * P:(c + 1) * P, :])])

            def half(name, w, hf):
                s, _n = ring_at[name]
                load(name, [(w512(s), w[:, 512 * hf:512 * (hf + 1)].rearrange("(c p) n -> p c n", p=P))])

            def moe_gu(l, s, e):
                eng.dma_start(slot(s, 4096).rearrange("p (c n) -> p c n", c=C),
                              i["moe_w_gu"][l, bass.ds(e, 1)].rearrange("a (c p) n -> p (a c) n", p=P)
                              ).then_inc(moe_sems[l][f"gu_in{s}"], 16)

            def moe_dn(l, s, e):
                eng.dma_start(ring[:, s * SLOT + 4096:(s + 1) * SLOT].rearrange("p (f n) -> p f n", f=2),
                              i["moe_w_down"][l, bass.ds(e, 1)].rearrange("a (f p) n -> p (a f) n", p=P)
                              ).then_inc(moe_sems[l][f"dn_in{s}"], 16)

            def moe_loads(l):
                S = moe_sems[l]
                for s in range(4):
                    if mine.get(s) is not None:
                        sp.wait("used", *mine[s])
                    if l == 0:
                        sp.wait("mix out")
                        eng.wait_ge(in_sems["out_written"], 64)
                    moe_gu(l, s, s)
                    moe_dn(l, s, s)
                    mine[s] = None

                def again(gu, dn, e):
                    for u in range(2):
                        eng.wait_ge(S["gu_made"], gu + u)
                        for v in range(2):
                            moe_gu(l, 2 * u + v, e + 2 * u + v)
                        eng.wait_ge(S["down_made"], dn + 2 * u)
                        for v in range(2):
                            moe_dn(l, 2 * u + v, e + 2 * u + v)

                with eng.Fori(0, EXP // 4 - 1) as k:
                    again(2 * k + 1, 4 * k + 2, 4 * k + 4)
                sp.wait("passes", l)
                extra = eng.value_load(passes[0:1, 2 * l + 1:2 * l + 2], min_val=0, max_val=4)
                with eng.If(extra > 0):
                    with eng.Fori(0, extra) as p:
                        with eng.Fori(0, EXP // 4) as k:
                            again(16 * p + 2 * k + 15, 32 * p + 4 * k + 30, 4 * k)
                if l == 0:
                    eng.wait_ge(S["down_made"], 32 * extra + 32)

            for c in range(C):
                ada_load(0, c)
            load(("lora1",), [
                (slot(0, 512).rearrange("p (c n) -> p c n", c=C), i["rw_w1"][0].rearrange("(c p) n -> p c n", p=P)),
                (ring[:, 512:1024].rearrange("p (c n) -> p c n", c=C),
                 i["rw_a1"][0].rearrange("(c p) n -> p c n", p=P)),
                (ring[:, 1024:1024 + C * LG].rearrange("p (c n) -> p c n", c=C),
                 i["rw_g1"][0].rearrange("(c p) n -> p c n", p=P))])
            load(("lora2",), [
                (ring[0:64, SLOT:SLOT + 1024], i["rw_w2"][0]), (ring[0:64, SLOT + 1024:SLOT + 2048], i["rw_a2"][0]),
                (ring[:, SLOT + 2048:SLOT + 3072], i["rw_g2"][0, 0:P]),
                (ring[0:32, SLOT + 3072:SLOT + 4096], i["rw_g2"][0, P:LG])])
            for n in range(3):
                for hf in range(2):
                    half(("rkv", n, hf), i["rw_w_rkv"][0, n], hf)
            sp.wait("inverses")
            for hf in range(2):
                half(("wo", hf), i["rw_w_o"][0], hf)
            moe_loads(0)
            for m, (a, cnt) in enumerate(((0, 3), (3, 3), (6, 2))):
                load(("kvada", m), [(slot(m, 2048 * cnt).rearrange("p (c n) -> p c n", c=cnt),
                                     i["kv_ada_w"][a * P:(a + cnt) * P].rearrange("(c p) n -> p c n", p=P))])
            for c in range(C):
                ada_load(1, c)
            half(("wkv",), i["w_kv"], 0)
            for hf in range(2):
                half(("wq", hf), i["at_w_q"][0], hf)
            for hf in range(2):
                half(("ao", hf), i["at_w_o"][0], hf)
            moe_loads(1)

        @block.gpsimd
        def _(eng):
            pl = Engine(eng, "pool_done", sems, known, seen)
            outs = [0]

            def put(dst, src):
                eng.dma_start(dst, src).then_inc(in_sems["out_written"], 16)
                outs[0] += 16

            eng.dma_start(const[:, :], i["const_all"]).then_inc(in_sems["const_in"], 16)
            pl.did(eng.memset(rows[:, 2, :], 0.0), "rows zeroed")
            pl.settle()
            n = 0
            for g, group in enumerate(VEC_GROUPS):
                r = 0
                for name, k in group:
                    a = i[name]
                    src = a.rearrange(" ".join("abcdef"[:len(a.shape)]) + " -> (" + " ".join("abcdef"[:len(a.shape)])
                                      + ")").rearrange("(r d) -> r d", d=P)
                    eng.dma_start(rows[r:r + k, g, :], src).then_inc(in_sems["vec_in"], 16)
                    r += k
                    n += 16
            rank["vec"] = n
            for j in range(2):
                eng.dma_start(xtok[:, j, :], i["x_prompt"][0, j * P:(j + 1) * P]).then_inc(in_sems["x_in"], 16)
            eng.dma_start(xtok[0:64, 2, :], i["x_sample"][0]).then_inc(in_sems["x_in"], 16)
            eng.dma_start(cph[:, 0:WN], i["const_wkv"]).then_inc(in_sems["wkvc_in"], 16)
            for h in range(2):
                eng.dma_start(sink[64 * h:64 * h + 64, :],
                              i["at_sinks"][0].rearrange("(c h) -> h c", h=2)[h:h + 1, :].broadcast_to([64, C]),
                              allow_slow_non_contiguous=True).then_inc(in_sems["sink_in"], 16)
            pl.wait("shift row")
            put(o[2][0, 0].rearrange("(c p) -> c p", p=P), shiftT[0:C, 0:P])
            put(o[6][0, 0].rearrange("(c p) -> c p", p=P), shiftT[0:C, P:2 * P])
            pl.wait("wkv ready")
            eng.dma_start(swin, i["state_wkv"][0, 0].rearrange("(c h) v k -> (h v) c k", h=2)
                          ).then_inc(in_sems["swkv_in"], 16)
            for r, n_out in ((0, 3), (1, 7)):
                pl.wait("swout ready", r)
                put(o[n_out][0, 0].rearrange("(c h) v k -> (h v) c k", h=2), swo[:, r])
            eng.dma_start(cph[:, 0:AN], i["const_att"]).then_inc(in_sems["attc_in"], 16)
            pl.wait("x mixed", 0)

            def load_router(l):
                eng.dma_start(router[:, :, 0:GROUPS], i["moe_w_group"][l].rearrange("(c p) n -> p c n", p=P)
                              ).then_inc(in_sems[f"router_in{l}"], 16)
                eng.dma_start(router[:, :, GROUPS:36], i["moe_w_expert"][l].rearrange("(c p) n -> p c n", p=P)
                              ).then_inc(in_sems[f"router_in{l}"], 16)

            load_router(0)
            pl.wait("x moe", 0)
            eng.dma_start(ktok, i["cache_k"][0].rearrange("t n d -> t (n d)")).then_inc(in_sems["cache_in"], 16)
            eng.dma_start(v64[:, 4:6, :], i["cache_v"][0].rearrange("(w t) n d -> t w (n d)", w=2)
                          ).then_inc(in_sems["cache_in"], 16)
            pl.wait("k64")
            for r, (n_out, w) in enumerate(((4, 0), (4, 1), (8, 2))):
                t0 = 64 * w if n_out == 4 else 0
                put(o[n_out][0, t0:t0 + 64].rearrange("t n d -> t (n d)"), k64[:, w, :])
            pl.wait("v64")
            for n_out, w, t0 in ((5, 2, 0), (5, 3, 64), (9, 6, 0)):
                put(o[n_out][0, t0:t0 + 64].rearrange("t n d -> t (n d)"), v64[:, w, :])
            pl.wait("x mixed", 1)
            load_router(1)
            for j in range(3):
                pl.wait("ytok", j)
                if j < 2:
                    put(o[0][0, j * P:(j + 1) * P], ytok[:, j, :])
                else:
                    put(o[1][0], ytok[0:64, 2, :])
            eng.wait_ge(in_sems["out_written"], outs[0])

        @block.tensor
        def _(eng):
            pe = Engine(eng, "pe_done", sems, known, seen)
            bank = Banks(pe, ps)
            ident = cst("ident")

            def mm(out, l, r, start, stop, **kw):
                return eng.matmul(out, l, r, start=start, stop=stop, **kw)

            def full(ins, *key):
                pe.did(ins, key)

            def adaln(tag, ready, loads, ncol):
                nb = ncol // 512
                banks = [bank.open(tag, b) for b in range((nb + 3) // 4)]
                for name, s_c0, cnt in loads:
                    s = arrived(pe, *name)
                    w = slot(s, cnt * ncol).rearrange("p (c n) -> p c n", c=cnt)
                    for cc in range(cnt):
                        c = s_c0 + cc
                        for n in range(nb):
                            jq = n % 4
                            ins = mm(banks[n // 4][32 * jq:32 * jq + 32, :], cs[:, c, :],
                                     w[:, cc, 512 * n:512 * (n + 1)], c == 0, c == C - 1,
                                     tile_position=(0, 32 * jq))
                    pe.did(ins, ("used",) + name, (tag,))

            def turn_mod(tag, nbk):
                pe.wait(tag + " rows")
                for b in range(nbk):
                    pb = bank.open(tag + "T", b)
                    for qd in range(4):
                        ins = eng.transpose(pb[:, 128 * qd:128 * qd + 128], modrow[:, b, 128 * qd:128 * qd + 128],
                                            ident)
                    full(ins, tag + "T", b)

            def mean_square(tag):
                pb = bank.open("ms", tag)
                for c in range(C):
                    if c % 2 == 0:
                        pe.wait("squares", tag, c // 2)
                    ins = mm(pb[:, 0:T], cst("ones"), sq_buf(tag)[:, c, :], c == 0, c == C - 1)
                full(ins, "ms", tag)

            def project(tag, nout, src, wname, cols, acc=C):
                for m in range(nout):
                    s = arrived(pe, *wname(m // 4))
                    pb = bank.open(tag, m)
                    for c in range(C):
                        ins = mm(pb[:, 0:T], w512(s)[:, c, 128 * (m % 4):128 * (m % 4) + 128], src[:, c, :], c == 0,
                                 c == C - 1)
                    keys = [(tag, m)]
                    if m % 4 == 3 or m == nout - 1:
                        keys.append(("used",) + wname(m // 4))
                    pe.did(ins, *keys)

            def head_sums(tag, src):
                pb = bank.open(tag, 0)
                for c in range(C):
                    ins = mm(pb[0:16, 0:T], cst("selh")[:, 16 * c:16 * c + 16], src[:, c, :], c == 0, c == C - 1)
                full(ins, tag, 0)

            def head_spread(tag, src16):
                for c in range(C):
                    pb = bank.open(tag, c)
                    full(mm(pb[:, 0:T], wcst("selb", 16)[:, P * c:P * (c + 1)], src16, True, True), tag, c)

            eng.wait_ge(in_sems["const_in"], 16)
            eng.wait_ge(in_sems["vec_in"], 16 * sum(len(g) for g in VEC_GROUPS))
            pb = bank.open("vec")
            for g in range(3):
                ins = eng.transpose(pb[:, P * g:P * (g + 1)], rows[:, g, :], ident)
            full(ins, "vec")
            eng.wait_ge(in_sems["x_in"], 48)
            for c in range(C):
                pb = bank.open("xT", c)
                for j, (t0, k) in enumerate(TILES):
                    ins = eng.transpose(pb[:, t0:t0 + k], xtok[0:k, j, P * c:P * (c + 1)], ident[0:k, 0:k])
                full(ins, "xT", c)
            pe.wait("cs")
            adaln("ada0", None, [(("ada", 0, c), c, 1) for c in range(C)], 6144)
            turn_mod("ada0", 3)

            mean_square("A0")
            pe.wait("h", "A0")
            pb = bank.open("shift")
            ins = eng.transpose(pb[0:C, 0:128], h0[:, :, SEQ - 1], ident)
            ins = eng.transpose(pb[0:C, 128:256], h0[:, :, T - 1], ident)
            full(ins, "shift")
            s = arrived(pe, "lora1")
            for n, (key, a, k) in enumerate((("w", 0, LW), ("a", 512, LA), ("g", 1024, LG))):
                w = ring[:, a:a + C * k].rearrange("p (c n) -> p c n", c=C)
                parts = [(0, k)] if k <= 128 else [(0, 128), (128, k - 128)]
                pe.wait("xm", 3 + n)
                for m, (c0, kk_) in enumerate(parts):
                    pb = bank.open("low", key, m)
                    for c in range(C):
                        ins = mm(pb[0:kk_, 0:T], w[:, c, c0:c0 + kk_], xm[(3 + n) % 2][:, c, :], c == 0, c == C - 1)
                    pe.did(ins, ("low", key, m), ("xm used", 3 + n))
            seen.at[("used", "lora1")] = seen.at[("low", "g", 1)]
            s = arrived(pe, "lora2")
            w2 = ring[0:64, SLOT:SLOT + 1024]
            a2 = ring[0:64, SLOT + 1024:SLOT + 2048]
            g2a = ring[:, SLOT + 2048:SLOT + 3072]
            g2b = ring[0:32, SLOT + 3072:SLOT + 4096]
            for key, w in (("w", w2), ("a", a2)):
                pe.wait("low ready", key, 0)
                for c in range(C):
                    pb = bank.open("up", key, c)
                    full(mm(pb[:, 0:T], w[:, P * c:P * (c + 1)], lows[key], True, True), "up", key, c)
            pe.wait("low ready", "g", 1)
            for c in range(C):
                pb = bank.open("up", "g", c)
                mm(pb[:, 0:T], g2a[:, P * c:P * (c + 1)], lows["g"], True, False)
                ins = mm(pb[:, 0:T], g2b[:, P * c:P * (c + 1)], lows["g1"], False, True)
                pe.did(ins, ("up", "g", c), ("used", "lora2"))
            for n in range(3):
                pe.wait("xm", n)
                project(("rkv", n), C, xm[n % 2], lambda hf, n=n: ("rkv", n, hf), 512)
                seen.at[("xm used", n)] = (pe.name, pe.n)
            pe.wait("kk squares")
            head_sums("kk sum", nrm)
            pe.wait("kk rstd")
            head_spread("kk rstd all", head16)
            pe.wait("rk")
            head_sums("bonus sum", tmp)
            pe.wait("bonus 16")
            head_spread("bonus all", head16b)
            pe.wait("wkv ready")
            i64 = cst("i64")

            def per_head(pb, cols, terms, c, last=True):
                for h in range(2):
                    r = slice(64 * h, 64 * h + 64)
                    for k, (l, m) in enumerate(terms):
                        ins = mm(pb[r, cols], l[r], m[r], k == 0, k == len(terms) - 1)
                return ins

            for j in range(NCH):
                t = slice(CH * j, CH * (j + 1))
                for nm, st in (("b", aa), ("k", kb)):
                    for hf in range(2):
                        pb = bank.open("A" + nm, j, hf)
                        for cc in range(4):
                            c = 4 * hf + cc
                            for h in range(2):
                                r = slice(64 * h, 64 * h + 64)
                                ins = mm(pb[r, P * cc:P * cc + P].rearrange("p (b t) -> p b t", b=2), st[r, c, t],
                                         ar[r, :, c, t], True, True)
                        full(ins, "A" + nm, j, hf)
                pb = bank.open("N1", j)
                for c in range(C):
                    ins = per_head(pb, slice(64 * c, 64 * c + 64), [(kk[:, c, t], aa[:, c, t])], c)
                full(ins, "N1", j)
                for nm, st in (("v", vb), ("b", aa), ("k", kb)):
                    pb = bank.open("tok" + nm, j)
                    for c in range(C):
                        ins = per_head(pb, slice(64 * c, 64 * c + 64), [(st[:, c, t], i64)], c)
                    full(ins, "tok" + nm, j)
            for l in range(2, 7):
                for j in range(NCH):
                    t = slice(CH * j, CH * (j + 1))
                    pe.wait("level", l, j)
                    pb = bank.open("W", l, j)
                    for c in range(C):
                        ins = per_head(pb, slice(64 * c, 64 * c + 64), [(nl[:, c, t], tmat[:, c, t])], c)
                    full(ins, "W", l, j)
                for j in range(NCH):
                    t = slice(CH * j, CH * (j + 1))
                    pe.wait("W ready", l, j)
                    pb = bank.open("TT", l, j)
                    for c in range(C):
                        ins = per_head(pb, slice(64 * c, 64 * c + 64), [(wmat[:, c, t], tt[:, c, t])], c)
                    full(ins, "TT", l, j)
                    if l < 6:
                        pb = bank.open("TW", l, j)
                        for c in range(C):
                            ins = per_head(pb, slice(64 * c, 64 * c + 64), [(tt[:, c, t], wmat[:, c, t])], c)
                        full(ins, "TW", l, j)
            eng.wait_ge(in_sems["swkv_in"], 16)
            pb = bank.open("s0")
            for c in range(C):
                ins = per_head(pb, slice(64 * c, 64 * c + 64), [(swin[:, c, :], i64)], c)
            full(ins, "s0")
            for j in (0, 4, 1, 2, 3):
                r_ = 1 if j == 4 else 0
                t = slice(CH * j, CH * (j + 1))
                pe.wait("state", j)
                pe.wait("T ready", j)
                pb = bank.open("RHS", j)
                for c in range(C):
                    ins = per_head(pb, slice(64 * c, 64 * c + 64),
                                   [(kk[:, c, t], state[:, r_, c, :]), (aak[:, c, t], vb[:, c, t])], c)
                full(ins, "RHS", j)
                pe.wait("RHS ready", j)
                pb = bank.open("U", j)
                for c in range(C):
                    ins = per_head(pb, slice(64 * c, 64 * c + 64), [(tt[:, c, t], rhs_u[:, 0, c, :])], c)
                full(ins, "U", j)
                pe.wait("U ready", j)
                pb = bank.open("S", j)
                for c in range(C):
                    ins = per_head(pb, slice(64 * c, 64 * c + 64),
                                   [(aa[:, c, t], rhs_u[:, 1, c, :]), (kb[:, c, t], vb[:, c, t])], c)
                full(ins, "S", j)
                pb = bank.open("Y", j)
                for c in range(C):
                    ins = per_head(pb, slice(64 * c, 64 * c + 64),
                                   [(state[:, r_, c, :], rr[:, c, t]), (rhs_u[:, 1, c, :], arb[:, c, t]),
                                    (vb[:, c, t], ark[:, c, t])], c)
                full(ins, "Y", j)
            for r_ in range(2):
                pe.wait("final state", r_)
                pb = bank.open("sout", r_)
                for c in range(C):
                    ins = per_head(pb, slice(64 * c, 64 * c + 64), [(state[:, r_, c, :], i64)], c)
                full(ins, "sout", r_)
            pe.wait("y all")
            head_sums("y sum", rr)
            pe.wait("y mean")
            head_spread("y mean all", head16)
            pe.wait("yc squares")
            head_sums("yc sum", E[0])
            pe.wait("y rstd")
            head_spread("y rstd all", head16)
            pe.wait("mix out")
            project("wo", C, rr, lambda hf: ("wo", hf), 512)

            def moe(l):
                S = moe_sems[l]
                mean_square(f"B{l}")
                pe.wait("h", f"B{l}")
                for j, (t0, k) in enumerate(TILES):
                    for hf in range(2):
                        pb = bank.open("htok", l, j, hf)
                        for cc in range(4):
                            ins = eng.transpose(pb[0:k, P * cc:P * cc + P], hT[:, 4 * hf + cc, t0:t0 + k], ident)
                        full(ins, "htok", l, j, hf)
                eng.wait_ge(in_sems[f"router_in{l}"], 32)
                pb = bank.open("logits", l)
                for j, (t0, k) in enumerate(TILES):
                    for c in range(C):
                        ins = mm(pb[0:k, 36 * j:36 * j + 36], hT[:, c, t0:t0 + k], router[:, c, :], c == 0,
                                 c == C - 1)
                full(ins, "logits", l)
                pe.wait("mask", l)
                pb = bank.open("rank", l)
                for j in range(3):
                    for jj in range(j + 1):
                        ins = mm(pb[:, EXP * j:EXP * j + EXP], cst("triu") if jj == j else cst("ones"),
                                 msk[:, jj, :], jj == 0, jj == j)
                for jj in range(3):
                    ins = mm(pb[:, 96:96 + EXP], cst("ones"), msk[:, jj, :], jj == 0, jj == 2)
                full(ins, "rank", l)
                pe.wait("passes", l)
                for b in range(8):
                    if bank.owner[b] is not None:
                        pe.wait("read", *bank.owner[b])
                nb = eng.value_load(passes[0:1, 2 * l:2 * l + 1], min_val=1, max_val=5)
                with eng.Fori(0, nb) as p:
                    with eng.Fori(0, EXP // 4) as k_:
                        k = 8 * p + k_
                        for u in range(2):
                            eng.wait_ge(S["sel_ready"], 2 * k + u + 1)
                            if u == 1:
                                eng.wait_ge(S["selT_ready"], 2 * k + 1)
                            for j, (t0, kt) in enumerate(TILES):
                                ins = eng.transpose(ps[0][:, t0:t0 + kt], selw[0:kt, u, j, :], ident[0:kt, 0:kt])
                            ins.then_inc(S["selT_made"], 1)
                            for hf in range(2):
                                if u == 1:
                                    eng.wait_ge(S["xe_ready"], 4 * k + hf + 1)
                                for cc in range(4):
                                    c = 4 * hf + cc
                                    for j, (t0, kt) in enumerate(TILES):
                                        ins = mm(ps[1 + hf][:, P * cc:P * cc + P], htok[0:kt, j, P * c:P * c + P],
                                                 sel[0:kt, u, j, :], j == 0, j == 2)
                                ins.then_inc(S["xe_made"], 1)
                        for u in range(2):
                            for v in range(2):
                                eng.wait_ge(S[f"gu_in{2 * u + v}"], 16 * k + 16)
                            for c in range(C):
                                if c % 4 == 0:
                                    eng.wait_ge(S["xe_ready"], 4 * k + 2 * u + c // 4 + 1)
                                for v in range(2):
                                    ins = mm(ps[3 + 4 * u][64 * v:64 * v + 64, :], xe[:, u, c, 64 * v:64 * v + 64],
                                             w512(2 * u + v)[:, c, :], c == 0, c == C - 1)
                            ins.then_inc(S["gu_made"], 1)
                        for u in range(2):
                            eng.wait_ge(S["h_ready"], 2 * k + u + 1)
                            if u == 0:
                                eng.wait_ge(S["selT_ready"], 2 * k + 2)
                            for f in range(2):
                                ins = eng.transpose(ps[0][:, P * f:P * f + P], hid[:, u, P * f:P * f + P], ident)
                            ins.then_inc(S["hT_made"], 1)
                            eng.wait_ge(S["hT_ready"], 2 * k + u + 1)
                            for v in range(2):
                                eng.wait_ge(S[f"dn_in{2 * u + v}"], 16 * k + 16)
                            for n in range(2):
                                if u == 1:
                                    eng.wait_ge(S["down_ready"], 4 * k + n + 1)
                                for f in range(2):
                                    for v in range(2):
                                        s = 2 * u + v
                                        w = ring[:, s * SLOT + 4096:(s + 1) * SLOT]
                                        ins = mm(ps[4 + n][64 * v:64 * v + 64, :], hidT[:, u, f, 64 * v:64 * v + 64],
                                                 w[:, D * f + 512 * n:D * f + 512 * n + 512], f == 0, f == 1)
                                ins.then_inc(S["down_made"], 1)
                        for c in range(C):
                            pb = ps[(6, 1, 7, 2)[c % 4]]
                            if c % 4 == 0:
                                eng.wait_ge(S["down_ready"], 4 * k + 3 + c // 4)
                            if c >= 4:
                                eng.wait_ge(S["y_added"], 8 * k + c - 3)
                            for u in range(2):
                                ins = mm(pb[:, 0:T], dslot[:, u, P * c:P * c + P], selT[:, u, :], u == 0, u == 1)
                            ins.then_inc(S["y_made"], 1)
                pe.wait("x moe", l)

            moe(0)

            adaln("kvada", None, [(("kvada", m), a, cnt) for m, (a, cnt) in enumerate(((0, 3), (3, 3), (6, 2)))], 2048)
            turn_mod("kvada", 1)
            mean_square("A1")
            adaln("ada1", None, [(("ada", 1, c), c, 1) for c in range(C)], 6144)
            turn_mod("ada1", 3)
            pe.wait("h", "KV")
            project("kv", 4, hkv, lambda hf: ("wkv",), 512)
            eng.wait_ge(in_sems["attc_in"], 16)
            for c in range(2):
                pe.wait("kraw", c)
                pb = bank.open("krot", c)
                full(mm(pb[:, 0:T], acst("ropep"), kraw[:, c, :], True, True), "krot", c)
            eng.wait_ge(in_sems["cache_in"], 32)
            pb = bank.open("kcache")
            for c in range(2):
                ins = eng.transpose(pb[:, P * c:P * c + P], ktok[:, P * c:P * c + P], ident)
            full(ins, "kcache")
            pe.wait("kT whole")
            for c in range(2):
                pb = bank.open("kswap", c)
                full(mm(pb[:, 0:448], acst("swap"), kT[:, c, :], True, True), "kswap", c)
            pe.wait("vT", 1)
            for w, t0 in enumerate((0, 64, 128, 192, 256)):
                pb = bank.open("v64", w)
                for c in range(2):
                    ins = eng.transpose(pb[0:64, P * c:P * c + P], vT[:, c, t0:t0 + 64], ident)
                full(ins, "v64", w)
            for w, t0 in enumerate((128, 192, 384)):
                pb = bank.open("k64", w)
                for c in range(2):
                    ins = eng.transpose(pb[0:64, P * c:P * c + P], kT[:, c, t0:t0 + 64], ident)
                full(ins, "k64", w)
            pe.wait("h", "A1")
            project("q", C, haq, lambda hf: ("wq", hf), 512)
            for c in range(C):
                pe.wait("qraw", c)
                pb = bank.open("qrot", c)
                full(mm(pb[:, 0:T], acst("ropep"), q[:, c, :], True, True), "qrot", c)
            pe.wait("kswapped", 1)
            for n in range(NCH):
                t0 = CH * n
                lo, hi = (max(0, n - 2) * CH, (n + 1) * CH) if n < 4 else (256, 448)
                W = hi - lo
                for b in range(4):
                    pe.wait("q ready", 2 * b + 1)
                    pb = bank.open("score", n, b)
                    for cc in range(2):
                        c = 2 * b + cc
                        g = c // 2
                        for h in range(2):
                            var = 0 if g % 2 == h else 2
                            r = slice(64 * h, 64 * h + 64)
                            ins = mm(pb[r, 256 * cc:256 * cc + W], q[r, c, t0:t0 + CH], kT[r, var + g // 2, lo:hi],
                                     True, True)
                    full(ins, "score", n, b)
                for w in range(W // CH):
                    for hf in range(2):
                        pe.wait("prob", n, 4 * hf + 3)
                        pb = bank.open("pT", n, w, hf)
                        for cc in range(4):
                            ins = eng.transpose(pb[0:64, P * cc:P * cc + P], prob[:, 4 * hf + cc, CH * w:CH * w + CH],
                                                ident)
                        full(ins, "pT", n, w, hf)
                pe.wait("v64")
                pe.wait("pT ready", n)
                pb = bank.open("o", n)
                first = max(0, n - 2) if n < 4 else 4
                for g in range(NKV):
                    for h in range(2):
                        for w in range(W // CH):
                            ins = mm(pb[64 * h:64 * h + 64, P * g:P * g + P].rearrange("p (c s) -> p c s", c=2),
                                     v64[:, first + w, 64 * g:64 * g + 64],
                                     pT[:, w, 2 * g:2 * g + 2, 64 * h:64 * h + 64], w == 0, w == W // CH - 1)
                full(ins, "o", n)
            pe.wait("oT", NCH - 1)
            project("ao", C, oT, lambda hf: ("ao", hf), 512)
            moe(1)
            mean_square("F")
            pe.wait("h", "F")
            for j, (t0, k) in enumerate(TILES):
                for hf in range(2):
                    pb = bank.open("ytok", j, hf)
                    for cc in range(4):
                        ins = eng.transpose(pb[0:k, P * cc:P * cc + P], E[1][:, 4 * hf + cc, t0:t0 + k], ident)
                    full(ins, "ytok", j, hf)

        @block.scalar
        def _(eng):
            ac = Engine(eng, "act_done", sems, known, seen)

            def pk(*key):
                ac.wait(*key)
                return ps[seen_bank(key)]

            def act(out, in_, f, *keys, **kw):
                ac.did(eng.activation(out, in_, f, **kw), *keys)

            def squares(tag):
                ac.wait("x for", tag)
                for b in range(4):
                    act(sq_buf(tag)[:, 2 * b:2 * b + 2, :], x[:, 2 * b:2 * b + 2, :], ACT.Square,
                        ("squares", tag, b))

            def root(tag):
                ac.wait("ms ready", tag)
                act(rstd[:, :], rstd[:, :], ACT.Sqrt, ("root", tag))

            ac.wait("vec ready")
            act(small[:, 0:16], vcol("c_prompt", 0, 16), ACT.Silu, ("silu c",))
            squares("A0")
            ac.wait("ada0")
            for b in range(3):
                act(modrow[:, b, :], ps[seen_bank(("ada0", b))][:, :], ACT.Copy, ("read", "ada0", b), ("ada0 rows",))
            root("A0")
            pb = pk("shift")
            act(shiftT[0:C, :], pb[0:C, 0:256], ACT.Copy, ("read", "shift"), ("shift row",))
            act(lows["w"], pk("low", "w", 0)[0:64, 0:T], ACT.Tanh, ("read", "low", "w", 0), ("low ready", "w", 0))
            act(lows["a"], pk("low", "a", 0)[0:64, 0:T], ACT.Copy, ("read", "low", "a", 0), ("low ready", "a", 0))
            act(lows["g"], pk("low", "g", 0)[:, 0:T], ACT.Sigmoid, ("read", "low", "g", 0), ("low ready", "g", 0))
            act(lows["g1"], pk("low", "g", 1)[0:32, 0:T], ACT.Sigmoid, ("read", "low", "g", 1), ("low ready", "g", 1))
            for key, dst, v in (("w", sig, "rw_w0"), ("a", aa, "rw_a0")):
                for c in range(C):
                    act(dst[:, c, :], pk("up", key, c)[:, 0:T], ACT.Sigmoid, ("read", "up", key, c), (key + " ready",),
                        bias=vcol(v, c))
            for c in range(C):
                act(gb[:, c, :], pk("up", "g", c)[:, 0:T], ACT.Copy, ("read", "up", "g", c))
            for n, dst in ((0, rr), (1, kb), (2, vb)):
                for c in range(C):
                    act(dst[:, c, :], pk(("rkv", n), c)[:, 0:T], ACT.Copy, ("read", ("rkv", n), c), ("rkv ready", n))
            ac.wait("kk raw")
            act(nrm[:, :, :], kk[:, :, :], ACT.Square, ("kk squares",))
            ac.wait("kk ms")
            act(head16, head16, ACT.Sqrt, ("kk root",))
            ac.wait("cum")
            act(dec[:, :, :], cum[:, :, :], ACT.Exp, ("dec",), scale=-DECAY)
            ac.wait("dm arg")
            act(sig[:, :, :], sig[:, :, :], ACT.Exp, ("dm",), scale=-DECAY)
            ac.wait("kk done")
            act(dinv[:, :, :], cum[:, :, :], ACT.Exp, ("dinv",), scale=DECAY)
            for j in range(NCH):
                t = slice(CH * j, CH * (j + 1))
                for nm, dst in (("v", vb), ("b", aa), ("k", kb)):
                    pb = pk("tok" + nm, j)
                    act(dst[:, :, t], pb[:, :].rearrange("p (c t) -> p c t", c=C), ACT.Copy,
                        ("read", "tok" + nm, j), ("tok ready", j))
            for l in range(2, 7):
                for j in range(NCH):
                    t = slice(CH * j, CH * (j + 1))
                    pb = pk("W", l, j)
                    act(wmat[:, :, t], pb[:, :].rearrange("p (c t) -> p c t", c=C), ACT.Copy,
                        ("read", "W", l, j), ("W ready", l, j))
            pb = pk("s0")
            act(state[:, 1], pb[:, :].rearrange("p (c t) -> p c t", c=C), ACT.Copy, ("read", "s0"), ("state", 4))
            for j in (0, 4, 1, 2, 3):
                pb = pk("RHS", j)
                act(rhs_u[:, 0], pb[:, :].rearrange("p (c t) -> p c t", c=C), ACT.Copy, ("read", "RHS", j),
                    ("RHS ready", j))
                pb = pk("U", j)
                act(rhs_u[:, 1], pb[:, :].rearrange("p (c t) -> p c t", c=C), ACT.Copy, ("read", "U", j),
                    ("U ready", j))
                pb = pk("Y", j)
                act(rr[:, :, CH * j:CH * (j + 1)], pb[:, :].rearrange("p (c t) -> p c t", c=C), ACT.Copy,
                    ("read", "Y", j), ("y all",))
            for r_ in range(2):
                pb = pk("sout", r_)
                act(swo[:, r_], pb[:, :].rearrange("p (c t) -> p c t", c=C), ACT.Copy, ("read", "sout", r_),
                    ("swout ready", r_), ("read", "swout", r_))
            ac.wait("yc")
            act(E[0][:, :, :], rr[:, :, :], ACT.Square, ("yc squares",))
            ac.wait("y var")
            act(head16, head16, ACT.Sqrt, ("y root",))

            def moe(l):
                S = moe_sems[l]
                squares(f"B{l}")
                root(f"B{l}")
                for j, (t0, k) in enumerate(TILES):
                    for hf in range(2):
                        act(htok[0:k, j, 512 * hf:512 * hf + 512], pk("htok", l, j, hf)[0:k, :], ACT.Copy,
                            ("read", "htok", l, j, hf), ("htok ready", l))
                ac.wait("group max", l)
                ac.wait("top2", l)
                act(rt[:, 6:9, 0:4], rt[:, 3:6, 0:4], ACT.Exp)
                act(rt[:, 36, 0:3], rt[:, 35, 0:3], ACT.Exp, ("route exp", l))
                ac.wait("passes", l)
                eng.wait_ge(in_sems["out_written"], (64, 160)[l])
                nb = eng.value_load(passes[0:1, 2 * l:2 * l + 1], min_val=1, max_val=5)
                with eng.Fori(0, nb) as p:
                    with eng.Fori(0, EXP // 4) as k_:
                        k = 8 * p + k_
                        for u in range(2):
                            eng.wait_ge(S["selT_made"], 2 * k + u + 1)
                            eng.activation(selT[:, u, :], ps[0][:, 0:T], ACT.Copy).then_inc(S["selT_ready"], 1)
                            for hf in range(2):
                                eng.wait_ge(S["xe_made"], 4 * k + 2 * u + hf + 1)
                                eng.activation(xe[:, u, 4 * hf:4 * hf + 4, :],
                                               ps[1 + hf][:, :].rearrange("p (c s) -> p c s", c=4),
                                               ACT.Copy).then_inc(S["xe_ready"], 1)
                        for u in range(2):
                            eng.wait_ge(S["gu_made"], 2 * k + u + 1)
                            eng.activation(silu[:, u, :], ps[3 + 4 * u][:, 0:FE], ACT.Silu).then_inc(S["silu_ready"], 1)
                        for u in range(2):
                            for n in range(2):
                                eng.wait_ge(S["down_made"], 4 * k + 2 * u + n + 1)
                                eng.activation(dslot[:, u, 512 * n:512 * n + 512], ps[4 + n][:, :],
                                               ACT.Copy).then_inc(S["down_ready"], 1)
                ac.wait("x moe", l)

            moe(0)
            squares("A1")
            ac.wait("kvada")
            act(modrow[:, 0, :], ps[seen_bank(("kvada", 0))][:, :], ACT.Copy, ("read", "kvada", 0), ("kvada rows",))
            root("A1")
            ac.wait("ada1")
            ac.wait("kvadaT", 0)
            for b in range(3):
                act(modrow[:, b, :], ps[seen_bank(("ada1", b))][:, :], ACT.Copy, ("read", "ada1", b), ("ada1 rows",))
            for c in range(4):
                dst = kraw[:, c, :] if c < 2 else vT[:, c - 2, :]
                act(dst, pk("kv", c)[:, 0:T], ACT.Identity, ("read", "kv", c), ("kraw", c) if c < 2 else ("vT", c - 2),
                    bias=vcol("b_kv", c))
            act(kT[:, 0:2, 256:384], pk("kcache")[:, 0:256].rearrange("p (c t) -> p c t", c=2), ACT.Copy,
                ("read", "kcache"), ("kcache ready",))
            for c in range(2):
                act(kT[:, 2 + c, :], pk("kswap", c)[:, 0:448], ACT.Copy, ("read", "kswap", c), ("kswapped", c))
            for w in range(5):
                act(v64[:, w if w < 4 else 6, :], pk("v64", w)[0:64, 0:256], ACT.Copy, ("read", "v64", w), ("v64",))
            for w in range(3):
                act(k64[:, w, :], pk("k64", w)[0:64, 0:256], ACT.Copy, ("read", "k64", w), ("k64",))
            for c in range(C):
                act(q[:, c, :], pk("q", c)[:, 0:T], ACT.Identity, ("read", "q", c), ("qraw", c),
                    bias=vcol("at_b_q", c))
            for n in range(NCH):
                W = min(n + 1, 3) * CH if n < 4 else 192
                for b in range(4):
                    ac.wait("row max", n, b)
                    for cc in range(2):
                        c = 2 * b + cc
                        act(prob[:, c, 0:W], ps[seen_bank(("score", n, b))][:, 256 * cc:256 * cc + W], ACT.Exp,
                            ("read", "score", n, b), ("exp", n, c), bias=att[:, 1, c:c + 1], scale=SCALE,
                            accum_out=att[:, 2, c:c + 1])
                act(att[:, 3, :], att[:, 4, :], ACT.Exp, ("sink exp", n))
                for w in range(W // CH):
                    for hf in range(2):
                        act(pT[:, w, 4 * hf:4 * hf + 4, :],
                            pk("pT", n, w, hf)[0:64, :].rearrange("p (c s) -> p c s", c=4), ACT.Copy,
                            ("read", "pT", n, w, hf), ("pT ready", n))
                act(oT[:, :, CH * n:CH * (n + 1)], pk("o", n)[:, :].rearrange("p (c t) -> p c t", c=C), ACT.Copy,
                    ("read", "o", n), ("oT", n))
            moe(1)
            squares("F")
            root("F")
            for j, (t0, k) in enumerate(TILES):
                for hf in range(2):
                    act(ytok[0:k, j, 512 * hf:512 * hf + 512], pk("ytok", j, hf)[0:k, :], ACT.Copy,
                        ("read", "ytok", j, hf), ("ytok", j))

        @block.vector
        def _(eng):
            ve = Engine(eng, "dve_done", sems, known, seen)

            def pk(*key):
                ve.wait(*key)
                return ps[seen_bank(key)]

            def op(ins, *keys):
                ve.did(ins, *keys)

            def tt_(out, a, b, o_, *keys):
                op(eng.tensor_tensor(out, a, b, o_), *keys)

            def ts(out, a, s1, s2, o1, o2, *keys):
                op(eng.tensor_scalar(out, a, s1, s2, o1, o2), *keys)

            def stt(out, a, s_, b, o1, o2, *keys):
                op(eng.scalar_tensor_tensor(out, a, s_, b, o1, o2), *keys)

            M, A_ = ALU.mult, ALU.add

            op(eng.memset(cs[:, :, :], 0.0))
            op(eng.memset(state[:, 0], 0.0), ("state", 0))
            op(eng.tensor_copy(vec[:, :], pk("vec")[:, 0:3 * P]), ("read", "vec"), ("vec ready",))
            ve.wait("silu c")
            for r in range(2):
                op(eng.tensor_copy(cs[:, :, r], small[:, 8 * r:8 * r + 8]), ("cs",))
            for c in range(C):
                op(eng.tensor_copy(x[:, c, :], pk("xT", c)[:, 0:T]), ("read", "xT", c), ("x for", "A0"))

            def turned(tag, dst, bias, nbk):
                for b in range(nbk):
                    pb = pk(tag + "T", b)
                    v = pb[:, :].rearrange("p (q j r) -> p r q j", q=4, j=4)
                    for r in range(2):
                        out = dst(r)[:, 16 * b:16 * b + 16].rearrange("p (j q) -> p q j", q=4)
                        bi = vec[:, bias + 16 * b:bias + 16 * b + 16].rearrange("p (j q) -> p q j", q=4)
                        tt_(out, v[:, r], bi, A_, ("read", tag + "T", b), (tag + " ready",))
                ve.settle()

            def rms(tag):
                ts(rstd[:, :], pk("ms", tag)[:, 0:T], 1.0 / D, RMS_EPS, M, A_, ("read", "ms", tag), ("ms ready", tag))
                ve.wait("root", tag)
                op(eng.reciprocal(rstd[:, :], rstd[:, :]))

            def modulated(tag, src, dst, g, md, sh, sc):
                if md is not None:
                    for r in range(2):
                        ts(coef[:, r, :], md(r)[:, sc:sc + C], 1.0, None, A_, ALU.bypass)
                    ve.settle()
                    for r in range(2):
                        tt_(coef[:, r, :], coef[:, r, :], g, M)
                    ve.settle()
                for c in range(C):
                    if md is None:
                        ts(dst[:, c, :], src[:, c, :], g[:, c:c + 1], None, M, ALU.bypass, ("h", tag))
                    else:
                        for r, t0, k in SEQS:
                            ts(dst[:, c, t0:t0 + k], src[:, c, t0:t0 + k], coef[:, r, c:c + 1],
                               md(r)[:, sh + c:sh + c + 1], M, A_, ("h", tag))
                ve.settle()

            def mdl(l):
                return lambda r: mod[:, l, r, :]

            def gated(tag, l, gate, *key):
                for c in range(C):
                    pb = pk(*key, c)
                    for r, t0, k in SEQS:
                        stt(x[:, c, t0:t0 + k], pb[:, t0:t0 + k], mod[:, l, r, gate + c:gate + c + 1],
                            x[:, c, t0:t0 + k], M, A_, ("read",) + key + (c,), *tag)
                ve.settle()

            turned("ada0", lambda r: mod[:, 0, r, :], VCOL["ada_b"], 3)
            rms("A0")
            ve.settle()
            tt_(h0[:, :, :], x[:, :, :], bmid(rstd[:, :], C), M)
            ve.settle()
            modulated("A0", h0, h0, vcol("norm_g", 0, C), mdl(0), 0, 8)
            tt_(diff[:, :, 1:T], h0[:, :, 0:T - 1], h0[:, :, 1:T], ALU.subtract)
            ve.settle()
            ts(diff[:, :, 0], h0[:, :, 0], -1.0, None, M, ALU.bypass)
            tt_(diff[:, :, SEQ], vcol("state_shift", 0, C), h0[:, :, SEQ], ALU.subtract)
            ve.settle()
            order = (3, 4, 5, 0, 1, 2)
            for k, n in enumerate(order):
                if k >= 2:
                    prev = [m for m in order[:k] if m % 2 == n % 2][-1:]
                    if prev:
                        ve.wait("xm used", prev[0])
                for c in range(C):
                    stt(xm[n % 2][:, c, :], diff[:, c, :], vcol("rw_mu", 8 * n + c), h0[:, c, :], M, A_, ("xm", n))
            ve.wait("rkv ready", 1)
            ve.wait("a ready")
            eng.wait_ge(in_sems["wkvc_in"], 16)
            tt_(kk[:, :, :], kb[:, :, :], bc(vcol("rw_k_k", 0, C), T), M, ("kk raw",))
            stt(tmp[:, :, :], aa[:, :, :], -1.0, bc(vcol("rw_k_a", 0, C), T), A_, M)
            ve.settle()
            stt(kb[:, :, :], tmp[:, :, :], 1.0, kb[:, :, :], A_, M)
            ve.settle()
            ve.wait("w ready")
            ve.wait("xm used", 2)
            for c in range(C):
                op(eng.tensor_tensor_scan(cum[:, c, :], wcst("scan"), sig[:, c, :], 0.0, M, A_), ("cum",))
            ve.settle()
            tt_(sig[:, :, :], cum[:, :, :], sig[:, :, :], ALU.subtract, ("dm arg",))
            ts(head16, pk("kk sum", 0)[0:16, 0:T], 1e-24, None, ALU.max, ALU.bypass, ("read", "kk sum", 0),
               ("kk ms",))
            ve.wait("kk root")
            op(eng.reciprocal(head16, head16), ("kk rstd",))
            tt_(tmp[:, :, :], rr[:, :, :], kb[:, :, :], M)
            ve.settle()
            tt_(tmp[:, :, :], tmp[:, :, :], bc(vcol("rw_r_k", 0, C), T), M, ("rk",))
            for c in range(C):
                tt_(kk[:, c, :], kk[:, c, :], pk("kk rstd all", c)[:, 0:T], M, ("read", "kk rstd all", c), ("kk done",))
            op(eng.tensor_copy(head16b, pk("bonus sum", 0)[0:16, 0:T]), ("read", "bonus sum", 0), ("bonus 16",))
            ve.settle()
            tt_(aa[:, :, :], kk[:, :, :], aa[:, :, :], M)
            ve.wait("dm")
            ve.settle()
            stt(kk[:, :, :], kk[:, :, :], -1.0, sig[:, :, :], M, M)
            ve.wait("dec")
            tt_(rr[:, :, :], rr[:, :, :], dec[:, :, :], M)
            op(eng.tensor_copy(dend[:, :, :], dec[:, :, CH - 1:T:CH]))
            ve.wait("rkv ready", 2)
            for c in range(C):
                tt_(bonus[:, c, :], vb[:, c, :], pk("bonus all", c)[:, 0:T], M, ("read", "bonus all", c))
            ve.wait("dinv")
            tt_(aa[:, :, :], aa[:, :, :], dinv[:, :, :], M)
            tt_(kb[:, :, :], kb[:, :, :], dinv[:, :, :], M, ("wkv ready",))
            ve.settle()
            for j in range(NCH):
                t = slice(CH * j, CH * (j + 1))
                for nm, strict, incl in (("b", nt, arb), ("k", aak, ark)):
                    for hf in range(2):
                        pb = pk("A" + nm, j, hf)[:, :].rearrange("p (c b t) -> p c b t", c=4, b=2)
                        cs4 = slice(4 * hf, 4 * hf + 4)
                        tt_(strict[:, cs4, t], pb[:, :, 0, :], bmid(wcst("maskA")[:, 0:64], 4), M)
                        tt_(incl[:, cs4, t], pb[:, :, 1, :], bmid(wcst("maskA")[:, 64:128], 4), M,
                            ("read", "A" + nm, j, hf))
                pb = pk("N1", j)[:, :].rearrange("p (c t) -> p c t", c=C)
                ve.settle()
                tt_(tmat[:, :, t], pb, bmid(wcst("lev1n"), C), M, ("read", "N1", j))
                tt_(tt[:, :, t], nt[:, :, t], bmid(wcst("lev")[:, 0:64], C), M)
                ve.settle()
                tt_(tmat[:, :, t], tmat[:, :, t], bmid(cst("i64"), C), A_)
                tt_(tt[:, :, t], tt[:, :, t], bmid(cst("i64"), C), A_)
                tt_(nl[:, :, t], nt[:, :, t], bmid(wcst("lev")[:, 64:128], C), M, ("level", 2, j))
                ve.settle()
            for l in range(2, 7):
                for j in range(NCH):
                    t = slice(CH * j, CH * (j + 1))
                    pb = pk("TT", l, j)[:, :].rearrange("p (c t) -> p c t", c=C)
                    if l < 6:
                        ve.wait("TW", l, j)
                    tt_(tt[:, :, t], tt[:, :, t], pb, A_, ("read", "TT", l, j), ("T ready", j), ("inverses",))
                    if l < 6:
                        pb = pk("TW", l, j)[:, :].rearrange("p (c t) -> p c t", c=C)
                        tt_(tmat[:, :, t], tmat[:, :, t], pb, A_, ("read", "TW", l, j))
                        tt_(nl[:, :, t], nt[:, :, t], bmid(wcst("lev")[:, 64 * l:64 * l + 64], C), M,
                            ("level", l + 1, j))
            ve.settle()
            for j in (0, 4, 1, 2, 3):
                r_ = 1 if j == 4 else 0
                pb = pk("S", j)[:, :].rearrange("p (c t) -> p c t", c=C)
                ve.wait("Y", j)
                tt_(state[:, r_], state[:, r_], pb, A_, ("read", "S", j))
                ve.settle()
                keys = [("state", j + 1)] if j < 3 else [("final state", 0 if j == 3 else 1)]
                tt_(state[:, r_], state[:, r_], bc(dend[:, :, j], HD), M, *keys)
            ve.wait("y all")
            ts(head16, pk("y sum", 0)[0:16, 0:T], 1.0 / HD, None, M, ALU.bypass, ("read", "y sum", 0), ("y mean",))
            for c in range(C):
                tt_(rr[:, c, :], rr[:, c, :], pk("y mean all", c)[:, 0:T], ALU.subtract, ("read", "y mean all", c),
                    ("yc",))
            ts(head16, pk("yc sum", 0)[0:16, 0:T], 1.0 / HD, GN_EPS, M, A_, ("read", "yc sum", 0), ("y var",))
            ve.wait("y root")
            op(eng.reciprocal(head16, head16), ("y rstd",))
            for c in range(C):
                tt_(rr[:, c, :], rr[:, c, :], pk("y rstd all", c)[:, 0:T], M, ("read", "y rstd all", c))
            ve.settle()
            for c in range(C):
                ts(rr[:, c, :], rr[:, c, :], vcol("rw_lnx_w", c), vcol("rw_lnx_b", c), M, A_)
            ve.settle()
            tt_(rr[:, :, :], rr[:, :, :], bonus[:, :, :], A_)
            ve.settle()
            tt_(rr[:, :, :], rr[:, :, :], gb[:, :, :], M, ("mix out",))
            gated([("x mixed", 0), ("x for", "B0")], 0, 16, "wo")

            def moe(l):
                S = moe_sems[l]
                rms(f"B{l}")
                ve.settle()
                if l == 1:
                    pass
                tt_(hT[:, :, :], x[:, :, :], bmid(rstd[:, :], C), M)
                ve.settle()
                modulated(f"B{l}", hT, hT, vcol("norm_g", 16 * l + 8, C), mdl(l), 24, 32)
                op(eng.memset(ysum[:, :, :], 0.0))
                op(eng.memset(lg[:, :, :], 0.0))
                ve.settle()
                pb = pk("logits", l)
                for j, (t0, k) in enumerate(TILES):
                    op(eng.tensor_copy(lg[0:k, j, :], pb[0:k, 36 * j:36 * j + 36]), ("read", "logits", l))
                ve.settle()
                R = lambda a, n=8: rt[:, a:a + 3, 0:n]
                g4 = lg[:, :, 0:4]
                e32 = lg[:, :, 4:36].rearrange("p j (g e) -> p j g e", g=4)
                sc_ = lambda a: rt[:, a, 0:3]
                down = cst("iota")

                def first_one(dst, key, src, mx, n):
                    tt_(R(key, n), src, bc(mx, n), ALU.is_equal)
                    ve.settle()
                    for a in range(n):
                        ts(rt[:, key:key + 3, a], rt[:, key:key + 3, a], float(n - a), None, M, ALU.bypass)
                    ve.settle()
                    op(eng.tensor_reduce(sc_(39), R(key, n), AX.X, ALU.max))
                    ve.settle()
                    tt_(R(dst, n), R(key, n), bc(sc_(39), n), ALU.is_equal)
                    ve.settle()

                op(eng.tensor_reduce(sc_(30), g4, AX.X, ALU.max))
                ve.settle()
                tt_(R(3, 4), g4, bc(sc_(30), 4), ALU.subtract, ("group max", l))
                first_one(12, 9, g4, sc_(30), 4)
                for g in range(4):
                    tt_(g48[:, :, g, :], e32[:, :, g, :], bc(rt[:, 12:15, g], 8), M)
                ve.settle()
                tt_(R(15), g48[:, :, 0, :], g48[:, :, 1, :], A_)
                tt_(R(18), g48[:, :, 2, :], g48[:, :, 3, :], A_)
                ve.settle()
                tt_(R(15), R(15), R(18), A_)
                ve.settle()
                op(eng.tensor_reduce(sc_(33), R(15), AX.X, ALU.max))
                ve.settle()
                first_one(21, 18, R(15), sc_(33), 8)
                stt(R(24), R(21), -3e38, R(15), M, A_)
                ve.settle()
                op(eng.tensor_reduce(sc_(34), R(24), AX.X, ALU.max))
                ve.settle()
                tt_(sc_(35), sc_(34), sc_(33), ALU.subtract, ("top2", l))
                first_one(27, 18, R(24), sc_(34), 8)
                ve.wait("route exp", l)
                op(eng.tensor_reduce(sc_(37), rt[:, 6:9, 0:4], AX.X, A_))
                ts(sc_(38), sc_(36), 1.0, None, A_, ALU.bypass)
                ve.settle()
                tt_(sc_(38), sc_(38), sc_(37), M)
                ve.settle()
                op(eng.reciprocal(sc_(38), sc_(38)))
                ve.settle()
                tt_(sc_(37), sc_(38), sc_(36), M)
                ve.settle()
                tt_(R(15), R(21), bc(sc_(38), 8), M)
                tt_(R(18), R(27), bc(sc_(37), 8), M)
                tt_(R(24), R(21), R(27), A_)
                ve.settle()
                tt_(R(15), R(15), R(18), A_)
                ve.settle()
                for g in range(4):
                    tt_(cw[:, :, 8 * g:8 * g + 8], R(15), bc(rt[:, 12:15, g], 8), M)
                    tt_(msk[:, :, 8 * g:8 * g + 8], R(24), bc(rt[:, 12:15, g], 8), M)
                ve.settle()
                op(eng.memset(msk[64:128, 2, :], 0.0), ("mask", l))
                pb = pk("rank", l)
                tt_(posn[:, :, :], pb[:, 0:96].rearrange("p (j e) -> p j e", j=3), msk[:, :, :], M)
                op(eng.tensor_reduce(small[:, 0:1], pb[:, 96:96 + EXP], AX.X, ALU.max), ("read", "rank", l))
                ve.settle()
                for a in range(4):
                    ts(small[:, 1 + a:2 + a], small[:, 0:1], float(SLOTS * (a + 1)), None, ALU.is_gt, ALU.bypass)
                ve.settle()
                op(eng.tensor_reduce(small[:, 5:6], small[:, 1:5], AX.X, A_))
                ve.settle()
                ts(passes[:, 2 * l:2 * l + 1], small[:, 5:6], 1.0, None, A_, ALU.bypass)
                op(eng.tensor_copy(passes[:, 2 * l + 1:2 * l + 2], small[:, 5:6]), ("passes", l))
                ve.settle()
                eng.memset(small[:, 8:9], 0.0).then_inc(S["pos_ready"], 1)
                nb = eng.value_load(passes[0:1, 2 * l:2 * l + 1], min_val=1, max_val=5)
                ve.wait("htok ready", l)
                with eng.Fori(0, nb) as p:
                    with eng.Fori(0, EXP // 4) as k_:
                        k = 8 * p + k_
                        eng.wait_ge(S["pos_ready"], p + 1)
                        for u in range(2):
                            for v in range(2):
                                for j, (t0, kt) in enumerate(TILES):
                                    e = 4 * k_ + 2 * u + v
                                    a = slice(64 * v, 64 * v + 64)
                                    eng.tensor_scalar(sel[0:kt, u, j, a], cst("iota", kt), posn[0:kt, j, bass.ds(e, 1)],
                                                      None, ALU.is_equal, ALU.bypass)
                                    ins = eng.tensor_scalar(selw[0:kt, u, j, a], cst("iota", kt),
                                                            posn[0:kt, j, bass.ds(e, 1)], cw[0:kt, j, bass.ds(e, 1)],
                                                            ALU.is_equal, M)
                            ins.then_inc(S["sel_ready"], 1)
                        for u in range(2):
                            eng.wait_ge(S["silu_ready"], 2 * k + u + 1)
                            eng.tensor_tensor(hid[:, u, :], silu[:, u, :], ps[3 + 4 * u][:, FE:2 * FE],
                                              M).then_inc(S["h_ready"], 1)
                            eng.wait_ge(S["hT_made"], 2 * k + u + 1)
                            eng.tensor_copy(hidT[:, u], ps[0][:, 0:2 * P].rearrange("p (f s) -> p f s", f=2)
                                            ).then_inc(S["hT_ready"], 1)
                        for c in range(C):
                            eng.wait_ge(S["y_made"], 8 * k + c + 1)
                            eng.tensor_tensor(ysum[:, c, :], ysum[:, c, :], ps[(6, 1, 7, 2)[c % 4]][:, 0:T],
                                              A_).then_inc(S["y_added"], 1)
                    eng.tensor_scalar(posn[:, :, :], posn[:, :, :], -float(SLOTS), None, A_, ALU.bypass
                                      ).then_inc(S["pos_ready"], 1)
                eng.wait_ge(S["y_added"], 64 * nb)
                for c in range(C):
                    for r, t0, k in SEQS:
                        stt(x[:, c, t0:t0 + k], ysum[:, c, t0:t0 + k], mod[:, l, r, 40 + c:40 + c + 1],
                            x[:, c, t0:t0 + k], M, A_, ("x moe", l), ("x for", "A1" if l == 0 else "F"))
                ve.settle()

            moe(0)
            turned("kvada", lambda r: kvmod[:, r, :], VCOL["kv_ada_b"], 1)
            rms("A1")
            ve.settle()
            tt_(E[0][:, :, :], x[:, :, :], bmid(rstd[:, :], C), M)
            ve.settle()
            modulated("KV", E[0], hkv, vcol("kv_norm_g", 0, C), lambda r: kvmod[:, r, :], 0, 8)
            turned("ada1", lambda r: mod[:, 1, r, :], VCOL["ada_b"] + 48, 3)
            modulated("A1", E[0], haq, vcol("norm_g", 16, C), mdl(1), 0, 8)
            for r in range(2):
                tt_(bog[:, r, :], vcol("at_b_o", 0, C), mod[:, 1, r, 16:24], M)
            eng.wait_ge(in_sems["attc_in"], 16)
            for c in range(2):
                tt_(krot[:, c, :], acst("sin"), pk("krot", c)[:, 0:T], M, ("read", "krot", c))
                tt_(kraw[:, c, :], kraw[:, c, :], acst("cos"), M)
                ve.settle()
                tt_(kT[:, c, 0:SEQ], kraw[:, c, 0:SEQ], krot[:, c, 0:SEQ], A_)
                tt_(kT[:, c, 384:448], kraw[:, c, SEQ:T], krot[:, c, SEQ:T], A_)
            ve.settle()
            ve.wait("kcache ready")
            ts(small[:, 8:9], small[:, 0:1], 0.0, None, M, ALU.bypass, ("kT whole",))
            for c in range(C):
                tt_(qt[:, c, :], acst("sin"), pk("qrot", c)[:, 0:T], M, ("read", "qrot", c))
                tt_(q[:, c, :], q[:, c, :], acst("cos"), M)
                ve.settle()
                tt_(q[:, c, :], q[:, c, :], qt[:, c, :], A_, ("q ready", c))
            eng.wait_ge(in_sems["sink_in"], 32)
            for n in range(NCH):
                W = min(n + 1, 3) * CH if n < 4 else 192
                for b in range(4):
                    cc = slice(2 * b, 2 * b + 2)
                    pb = pk("score", n, b)
                    if n:
                        ve.wait("sink exp", n - 1)
                    op(eng.tensor_reduce(att[:, 0, cc], pb[:, :].rearrange("p (c s) -> p c s", c=2)[:, :, 0:W], AX.X,
                                         ALU.max))
                    ve.settle()
                    stt(att[:, 1, cc], att[:, 0, cc], SCALE, sink[:, cc], M, ALU.max)
                    ve.settle()
                    ts(att[:, 1, cc], att[:, 1, cc], -1.0, None, M, ALU.bypass)
                    ve.settle()
                    tt_(att[:, 4, cc], sink[:, cc], att[:, 1, cc], A_, ("row max", n, b))
                ve.wait("sink exp", n)
                tt_(att[:, 5, :], att[:, 2, :], att[:, 3, :], A_)
                ve.settle()
                op(eng.reciprocal(att[:, 5, :], att[:, 5, :]))
                ve.settle()
                for c in range(C):
                    ts(prob[:, c, 0:W], prob[:, c, 0:W], att[:, 5, c:c + 1], None, M, ALU.bypass, ("prob", n, c))
            for c in range(C):
                pb = pk("ao", c)
                for r, t0, k in SEQS:
                    ts(qt[:, c, t0:t0 + k], pb[:, t0:t0 + k], mod[:, 1, r, 16 + c:17 + c], bog[:, r, c:c + 1], M, A_,
                       ("read", "ao", c))
            ve.settle()
            tt_(x[:, :, :], x[:, :, :], qt[:, :, :], A_, ("x mixed", 1), ("x for", "B1"))
            ve.settle()
            moe(1)
            rms("F")
            ve.settle()
            tt_(E[0][:, :, :], x[:, :, :], bmid(rstd[:, :], C), M)
            ve.settle()
            modulated("F", E[0], E[1], vcol("final_norm_g", 0, C), None, 0, 0)


NAMES = ['x_prompt', 'x_sample', 'state_shift', 'state_wkv', 'cache_k', 'cache_v', 'c_prompt', 'c_sample', 'ada_w',
         'ada_b', 'norm_g', 'rw_mu', 'rw_w_rkv', 'rw_w0', 'rw_w1', 'rw_w2', 'rw_a0', 'rw_a1', 'rw_a2', 'rw_g1',
         'rw_g2', 'rw_k_k', 'rw_k_a', 'rw_r_k', 'rw_lnx_w', 'rw_lnx_b', 'rw_w_o', 'kv_ada_w', 'kv_ada_b', 'kv_norm_g',
         'w_kv', 'b_kv', 'at_w_q', 'at_b_q', 'at_sinks', 'at_w_o', 'at_b_o', 'moe_w_group', 'moe_w_expert',
         'moe_w_gu', 'moe_w_down', 'final_norm_g']
OUTS = [(1, SEQ, D), (1, DEC, D), (1, 1, D), (1, 1, HEADS, HD, HD), (1, 128, NKV, HD), (1, 128, NKV, HD), (1, 1, D),
        (1, 1, HEADS, HD, HD), (1, DEC, NKV, HD), (1, DEC, NKV, HD)]


def kernel(**inputs):
    import concourse.bacc as bacc
    from concourse.bass_utils import run_bass_kernel_spmd as run

    arrays = {n: np.ascontiguousarray(inputs[n]) for n in NAMES}
    arrays.update(constants())

    def program(known):
        nc = bacc.Bacc("TRN2", target_bir_lowering=False, num_devices=1)
        i = {n: nc.dram_tensor(f"in_{n}", a.shape, mybir.dt.from_np(a.dtype), kind="ExternalInput").ap()
             for n, a in arrays.items()}
        o = [nc.dram_tensor(f"out_{k}", s, F32, kind="ExternalOutput").ap() for k, s in enumerate(OUTS)]
        seen = Counts()
        build(nc, i, o, known, seen)
        return nc, seen

    _, counts = program(None)
    nc, _ = program(counts)
    r = run(nc, [{f"in_{n}": a for n, a in arrays.items()}], core_ids=[0])
    return tuple(r.results[0][f"out_{k}"] for k in range(len(OUTS)))
```

```python
from contextlib import ExitStack

import numpy as np

import concourse.bass as bass
from concourse import mybir

F32 = mybir.dt.float32
I32 = mybir.dt.int32
ALU = mybir.AluOpType
ACT = mybir.ActivationFunctionType
AX = mybir.AxisListType

P = 128
D = 1024
C = D // P
SEQ, DEC = 256, 64
T = SEQ + DEC
CH = 64
NCH = T // CH
HD = 64
HEADS = D // HD
NKV = 4
ROPE = HD // 4
PAST = 512
EXP, GROUPS, EPG = 32, 4, 8
FE = D // 4
SLOTS = 64
LW, LA, LG = 64, 64, 160
RMS_EPS = 1e-6
GN_EPS = 64e-5
DECAY = float(np.exp(-0.5))
SCALE = HD ** -0.5
TILES = [(0, 128), (128, 128), (256, 64)]
SEQS = [(0, 0, SEQ), (1, SEQ, DEC)]

VEC_GROUPS = [
    [("c_prompt", 8), ("c_sample", 8), ("norm_g", 32), ("rw_mu", 48), ("rw_w0", 8), ("rw_a0", 8), ("rw_k_k", 8),
     ("rw_k_a", 8)],
    [("ada_b", 96), ("kv_ada_b", 16), ("rw_r_k", 8), ("rw_lnx_w", 8)],
    [("rw_lnx_b", 8), ("kv_norm_g", 8), ("at_b_q", 8), ("at_b_o", 8), ("final_norm_g", 8), ("b_kv", 4),
     ("state_shift", 8)],
]
VCOL = {}
for _g, _rows in enumerate(VEC_GROUPS):
    _o = P * _g
    for _n, _k in _rows:
        VCOL[_n] = _o
        _o += _k

CONST = [("ident", 128), ("ones", 128), ("triu", 128), ("selh", 128), ("iota", 64), ("i64", 64)]
WKVC = [("maskA", 128), ("lev", 6 * 64), ("lev1n", 64), ("scan", T), ("selb", 1024)]
ATTC = [("cos", T), ("sin", T), ("ropep", 128), ("swap", 128)]


def offsets(table):
    out, o = {}, 0
    for n, k in table:
        out[n] = (o, k)
        o += k
    return out, o


CO, CN = offsets(CONST)
WO, WN = offsets(WKVC)
AO, AN = offsets(ATTC)


def constants():
    p = np.arange(P)
    c = np.zeros((P, CN), np.float32)

    def put(a, off, name, v):
        o, k = off[name]
        a[:v.shape[0], o:o + k] = v

    put(c, CO, "ident", np.eye(P))
    put(c, CO, "ones", np.ones((P, P)))
    put(c, CO, "triu", (p[:, None] <= p[None, :]))
    m = np.arange(P)
    put(c, CO, "selh", ((m % 16)[None, :] == 2 * (m // 16)[None, :] + (p // HD)[:, None]))
    put(c, CO, "iota", np.broadcast_to(np.arange(1, 65), (P, 64)))
    put(c, CO, "i64", ((p % 64)[:, None] == np.arange(64)[None, :]))
    w = np.zeros((P, WN), np.float32)
    s, t = (p % 64)[:, None], np.arange(64)[None, :]
    put(w, WO, "maskA", np.concatenate([s < t, s <= t], 1))
    lev = []
    for l in range(1, 7):
        b = 1 << l
        lev.append((s // b == t // b) & (s % b < b // 2) & (t % b >= b // 2))
    put(w, WO, "lev", np.concatenate(lev, 1))
    put(w, WO, "lev1n", (s // 2 == t // 2) & (t % 2 == 0) & (s % 2 == 1))
    put(w, WO, "scan", np.broadcast_to(np.arange(T) % CH != 0, (P, T)))
    q = np.arange(1024)
    put(w, WO, "selb", (np.arange(16)[:, None] == (2 * (q // P) + (q % P) // HD)[None, :]))
    a = np.zeros((P, AN), np.float32)
    half = ROPE // 2
    inv = np.power(np.float32(500000.0), -np.arange(half, dtype=np.float32) * np.float32(2.0 / ROPE)).astype(np.float32)
    pos = np.concatenate([np.arange(SEQ), PAST + np.arange(DEC)]).astype(np.float32)
    ang = (pos[None, :] * inv[:, None]).astype(np.float32)
    d = p % HD
    cos, sin = np.ones((P, T), np.float32), np.zeros((P, T), np.float32)
    cos[d < ROPE] = np.cos(ang)[d[d < ROPE] % half]
    sin[d < ROPE] = np.sin(ang)[d[d < ROPE] % half]
    put(a, AO, "cos", cos)
    put(a, AO, "sin", sin)
    rp = np.zeros((P, P), np.float32)
    for h in (0, HD):
        for j in range(half):
            rp[h + half + j, h + j] = -1.0
            rp[h + j, h + half + j] = 1.0
    put(a, AO, "ropep", rp)
    put(a, AO, "swap", (p[:, None] == (p[None, :] + HD) % P))
    return {"const_all": c, "const_wkv": w, "const_att": a}


MODS = [("ada_w", 0, 1, "ada_b"), ("ada_w", 0, 2, "ada_b"), ("kv_ada_w", None, 0, "kv_ada_b"), ("ada_w", 1, 0, "ada_b"),
        ("ada_w", 1, 1, "ada_b"), ("ada_w", 1, 2, "ada_b")]
MSTEPS = C * len(MODS)
A_STEPS = 4


def steps_of_level(l):
    first = A_STEPS * NCH + NCH * (l - 2)
    return range(first, first + NCH)


def step_of_state(n):
    return A_STEPS * NCH + NCH * 5 + n


def mods_done(steps):
    return [n // C for n in steps if n % C == C - 1 and n < MSTEPS]


def mods_turned(steps):
    return [n // C - 1 for n in steps if n % C == 1 and C < n <= MSTEPS + 1]


class Counts:

    def __init__(self):
        self.at, self.bank = {}, {}


class Engine:

    def __init__(self, eng, name, sems, known, seen):
        self.e, self.name, self.sems, self.known, self.seen = eng, name, sems, known, seen
        self.n, self.waited = 0, {}

    def did(self, ins, *keys):
        ins.then_inc(self.sems[self.name], 1)
        self.n += 1
        for k in keys:
            self.seen.at[k] = (self.name, self.n)

    def wait(self, *key):
        if self.known is None:
            return
        who, n = self.known.at[key]
        if self.waited.get(who, 0) < n:
            self.waited[who] = n
            self.e.wait_ge(self.sems[who], n)

    def settle(self):
        if self.n and self.waited.get(self.name, 0) < self.n:
            self.waited[self.name] = self.n
            self.e.wait_ge(self.sems[self.name], self.n)


class Banks:

    def __init__(self, pe, ps):
        self.pe, self.ps, self.n, self.owner, self.held = pe, ps, 0, [None] * 8, None

    def hold(self, *key):
        self.held = None
        pb = self.open(*key)
        self.held = (self.n - 1) % 8
        return pb

    def open(self, *key):
        if self.n % 8 == self.held:
            self.n += 1
        b = self.n % 8
        self.n += 1
        if self.owner[b] is not None:
            self.pe.wait("read", *self.owner[b])
        self.owner[b] = key
        self.pe.seen.bank[key] = b
        return self.ps[b]


def build(nc, i, o, known, seen):
    ctx = ExitStack()
    with ctx:
        def sb(name, shape, dt=F32):
            return ctx.enter_context(nc.sbuf_tensor(name, shape, dt))

        def sem(name):
            return ctx.enter_context(nc.semaphore(name))

        ps = [ctx.enter_context(nc.psum_tensor(f"bank{b}", [P, 512], F32)) for b in range(8)]
        SLOT = 6144
        B = C * T
        xt_ = sb("x_res", [P, B])
        ring = sb("ring", [P, 4 * SLOT])
        work = sb("work", [P, 8 * B])
        const = sb("const", [P, CN])
        cph = sb("const_phase", [P, max(WN, AN)])
        vec = sb("vec", [P, 3 * P])
        cs = sb("cs", [P, C, 32])
        mod = sb("mod", [P, 2, 2, 48])
        kvmod = sb("kvmod", [P, 2, 16])
        coef = sb("coef", [P, 2, C])
        rstd = sb("rstd", [P, T])
        state = sb("state", [P, 2, C, HD])
        dend = sb("dend", [P, C, NCH])
        sink = sb("sink", [P, C])
        att = sb("att", [P, 6, C])
        bog = sb("bog", [P, 2, C])
        passes = sb("passes", [P, 4], I32)
        small = sb("small", [P, 16])

        names = ["pe_done", "act_done", "dve_done", "pool_done"]
        sems = {n: sem(n) for n in names}
        ring_in = [sem(f"ring_in{s}") for s in range(4)]
        in_sems = {n: sem(n) for n in ("const_in", "vec_in", "x_in", "wkvc_in", "attc_in", "sink_in", "cache_in",
                                       "swkv_in", "router_in0", "router_in1", "out_written", "modw_in0", "modw_in1")}
        moe_sems = [{n: sem(f"{n}{l}") for n in (
            "gu_in0", "gu_in1", "gu_in2", "gu_in3", "dn_in0", "dn_in1", "dn_in2", "dn_in3",
            "pos_ready", "sel_ready", "selT_made", "selT_ready", "xe_made", "xe_ready",
            "gu_made", "silu_ready", "h_ready", "hT_made", "hT_ready", "down_made", "down_ready",
            "y_made", "y_added")} for l in range(2)]

        def cst(n, rows=P):
            a, k = CO[n]
            return const[0:rows, a:a + k]

        def wcst(n, rows=P):
            a, k = WO[n]
            return cph[0:rows, a:a + k]

        def acst(n):
            a, k = AO[n]
            return cph[:, a:a + k]

        def vcol(n, c, k=1):
            return vec[:, VCOL[n] + c:VCOL[n] + c + k]

        def slot(s, n=SLOT):
            return ring[:, s * SLOT:s * SLOT + n]

        def w512(s):
            return slot(s, 4096).rearrange("p (c n) -> p c n", c=C)

        def buf(t, off=0):
            return t[:, off:off + B].rearrange("p (c t) -> p c t", c=C)

        x = buf(xt_)
        E = [buf(work, B * n) for n in range(8)]
        Fb = [buf(ring, 2 * SLOT + B * n) for n in range(4)]
        G = [buf(ring, B * n) for n in range(4)]
        h0, diff, xm = E[0], E[1], [E[2], E[3]]
        sig, aa, kb, vb, gb, kk, rr, tmp = Fb[0], Fb[1], Fb[2], E[5], E[4], E[6], E[7], Fb[3]
        nrm, bonus, cum, dec = E[0], E[1], E[2], E[3]
        dinv = E[0]
        arb, aak, ark, tt, nt, tmat, wmat, nl = E[0], E[2], E[3], Fb[0], Fb[3], G[0], G[1], G[2]
        ar = work[:, 6 * B:8 * B].rearrange("p (b c t) -> p b c t", b=2, c=C)
        off = [0]

        def wk(n):
            a = off[0]
            off[0] += n
            return work[:, a:a + n]

        hT = wk(B).rearrange("p (c t) -> p c t", c=C)
        htok = wk(3 * D).rearrange("p (j d) -> p j d", j=3)
        ysum = wk(B).rearrange("p (c t) -> p c t", c=C)
        xe = wk(2 * C * P).rearrange("p (u c s) -> p u c s", u=2, c=C)
        dslot = wk(2 * D).rearrange("p (u d) -> p u d", u=2)
        silu = wk(2 * FE).rearrange("p (u f) -> p u f", u=2)
        hid = wk(2 * FE).rearrange("p (u f) -> p u f", u=2)
        hidT = wk(2 * 2 * P).rearrange("p (u f s) -> p u f s", u=2, f=2)
        sel = wk(2 * 3 * P).rearrange("p (u j s) -> p u j s", u=2, j=3)
        selw = wk(2 * 3 * P).rearrange("p (u j s) -> p u j s", u=2, j=3)
        selT = wk(2 * T).rearrange("p (u t) -> p u t", u=2)
        router = wk(C * 36).rearrange("p (c n) -> p c n", c=C)
        lg = wk(3 * 36).rearrange("p (j n) -> p j n", j=3)
        cw = wk(3 * EXP).rearrange("p (j e) -> p j e", j=3)
        msk = wk(3 * EXP).rearrange("p (j e) -> p j e", j=3)
        posn = wk(3 * EXP).rearrange("p (j e) -> p j e", j=3)
        rt = wk(40 * 12).rearrange("p (n k) -> p n k", n=40)
        g48 = wk(3 * 4 * 8).rearrange("p (j g e) -> p j g e", j=3, g=4)
        hkv, haq, q, qt, oT = E[1], E[5], E[6], E[7], E[5]
        kT = work[:, 2 * B:2 * B + 4 * 448].rearrange("p (v t) -> p v t", v=4)
        a3 = 3 * B
        vT = work[:, a3:a3 + 640].rearrange("p (c t) -> p c t", c=2)
        kraw = work[:, a3 + 640:a3 + 1280].rearrange("p (c t) -> p c t", c=2)
        krot = work[:, a3 + 1280:a3 + 1920].rearrange("p (c t) -> p c t", c=2)
        ktok = work[:, a3 + 1920:a3 + 2176]
        v64 = work[0:64, 4 * B:4 * B + 7 * 256].rearrange("p (n d) -> p n d", n=7)
        k64 = work[0:64, 4 * B + 1792:4 * B + 2560].rearrange("p (n d) -> p n d", n=3)
        prob = work[:, 0:1536].rearrange("p (c s) -> p c s", c=C)
        pT = work[0:64, 1536:1536 + 3072].rearrange("p (w c s) -> p w c s", w=3, c=C)
        ytok = work[:, 2 * B:2 * B + 3 * D].rearrange("p (j d) -> p j d", j=3)
        xtok = work[:, 0:3 * D].rearrange("p (j d) -> p j d", j=3)
        rows = work[:, 2 * B:2 * B + 3 * P].rearrange("p (g d) -> p g d", g=3)
        tail1, tail3 = 10240, 22528
        rhs_u = ring[:, tail1:tail1 + 1024].rearrange("p (b c k) -> p b c k", b=2, c=C)
        swin = ring[:, tail1 + 1024:tail1 + 1536].rearrange("p (c k) -> p c k", c=C)
        shiftT = ring[:, tail1 + 1536:tail1 + 1792]
        mw = [ring[:, 3 * B:3 * B + 2048], ring[:, tail3:tail3 + 2048]]
        modrow = [ring[:, 3 * B + 2048:3 * B + 2560], work[:, 6 * B:6 * B + 512]]
        lows = {"w": ring[0:64, tail3:tail3 + T], "a": ring[0:64, tail3 + T:tail3 + 2 * T],
                "g": ring[:, tail3 + 2 * T:tail3 + 3 * T], "g1": ring[0:32, tail3 + 3 * T:tail3 + 4 * T]}
        head16 = ring[0:16, tail3 + 4 * T:tail3 + 5 * T]
        head16b = ring[0:16, tail3 + 5 * T:tail3 + 6 * T]
        swo = ring[:, 2 * SLOT + 3 * B:2 * SLOT + 3 * B + 1024].rearrange("p (r c k) -> p r c k", r=2, c=C)

        def sq_buf(tag):
            return E[7]

        def seen_bank(key):
            return (known or seen).bank.get(key, 0)

        def bc(ap, n):
            return ap.unsqueeze(2).broadcast_to([ap.shape[0], ap.shape[1], n])

        def bmid(ap, n):
            return ap.unsqueeze(1).broadcast_to([ap.shape[0], n, ap.shape[1]])

        ring_plan, ring_at, got = [], {}, [0] * 4

        def plan(name, s, parts):
            got[s] += 16 * parts
            ring_at[name] = (s, got[s])
            ring_plan.append(name)

        for m in range(4):
            plan(("ada", m), m, 1)
        plan(("lora1",), 0, 3)
        plan(("lora2",), 1, 4)
        for n in (0, 1, 2):
            for hf in range(2):
                plan(("rkv", n, hf), hf, 1)
        for hf in range(2):
            plan(("wo", hf), hf, 1)
        plan(("wkv",), 0, 1)
        for hf in range(2):
            plan(("wq", hf), 1 + hf, 1)
        plan(("ao", 0), 3, 1)
        plan(("ao", 1), 0, 1)

        def arrived(en, *name):
            s, n = ring_at[name]
            en.e.wait_ge(ring_in[s], n)
            return s

        def vec_loads(eng, which):
            n = 0
            for g, group in enumerate(VEC_GROUPS):
                r = 0
                for name, k in group:
                    letters = " ".join("abcdef"[:len(i[name].shape)])
                    src = i[name].rearrange(f"{letters} -> ({letters})").rearrange("(r d) -> r d", d=P)
                    if n % 2 == which:
                        eng.dma_start(rows[r:r + k, g, :], src).then_inc(in_sems["vec_in"], 16)
                    r += k
                    n += 1

        block = ctx.enter_context(nc.Block())

        @block.sync
        def _(eng):
            sp = Engine(eng, "sp", sems, known, seen)
            mine = {}

            def load(name, pairs):
                s, _n = ring_at[name]
                if mine.get(s) is not None:
                    sp.wait("used", *mine[s])
                mine[s] = name
                for dst, src in pairs:
                    eng.dma_start(dst, src).then_inc(ring_in[s], 16)

            def half(name, w, hf):
                s, _n = ring_at[name]
                load(name, [(w512(s), w[:, 512 * hf:512 * (hf + 1)].rearrange("(c p) n -> p c n", p=P))])

            def moe_gu(l, s, e):
                eng.dma_start(slot(s, 4096).rearrange("p (c n) -> p c n", c=C),
                              i["moe_w_gu"][l, bass.ds(e, 1)].rearrange("a (c p) n -> p (a c) n", p=P)
                              ).then_inc(moe_sems[l][f"gu_in{s}"], 16)

            def moe_dn(l, s, e):
                eng.dma_start(ring[:, s * SLOT + 4096:(s + 1) * SLOT].rearrange("p (f n) -> p f n", f=2),
                              i["moe_w_down"][l, bass.ds(e, 1)].rearrange("a (f p) n -> p (a f) n", p=P)
                              ).then_inc(moe_sems[l][f"dn_in{s}"], 16)

            def moe_loads(l):
                S = moe_sems[l]
                for s in range(4):
                    if mine.get(s) is not None:
                        sp.wait("used", *mine[s])
                    if l == 0:
                        sp.wait("mix out")
                        eng.wait_ge(in_sems["out_written"], 64)
                    moe_gu(l, s, s)
                    moe_dn(l, s, s)
                    mine[s] = None

                def again(gu, dn, e):
                    for u in range(2):
                        eng.wait_ge(S["gu_made"], gu + u)
                        for v in range(2):
                            moe_gu(l, 2 * u + v, e + 2 * u + v)
                    for u in range(2):
                        eng.wait_ge(S["down_made"], dn + 2 * u)
                        for v in range(2):
                            moe_dn(l, 2 * u + v, e + 2 * u + v)

                with eng.Fori(0, EXP // 4 - 1) as k:
                    again(2 * k + 1, 4 * k + 2, 4 * k + 4)
                sp.wait("passes", l)
                extra = eng.value_load(passes[0:1, 2 * l + 1:2 * l + 2], min_val=0, max_val=4)
                with eng.If(extra > 0):
                    with eng.Fori(0, extra) as p:
                        with eng.Fori(0, EXP // 4) as k:
                            again(16 * p + 2 * k + 15, 32 * p + 4 * k + 30, 4 * k)
                return extra

            sp.wait("rows zeroed")
            vec_loads(eng, 0)
            for m in range(4):
                load(("ada", m), [(w512(m).rearrange("p (c k) n -> p c (k n)", c=2),
                                   i["ada_w"][0, 2 * m * P:(2 * m + 2) * P, 0:2048]
                                   .rearrange("(c p) n -> p c n", p=P))])
            load(("lora1",), [
                (slot(0, 512).rearrange("p (c n) -> p c n", c=C), i["rw_w1"][0].rearrange("(c p) n -> p c n", p=P)),
                (ring[:, 512:1024].rearrange("p (c n) -> p c n", c=C),
                 i["rw_a1"][0].rearrange("(c p) n -> p c n", p=P)),
                (ring[:, 1024:1024 + C * LG].rearrange("p (c n) -> p c n", c=C),
                 i["rw_g1"][0].rearrange("(c p) n -> p c n", p=P))])
            load(("lora2",), [
                (ring[0:64, SLOT:SLOT + 1024], i["rw_w2"][0]), (ring[0:64, SLOT + 1024:SLOT + 2048], i["rw_a2"][0]),
                (ring[:, SLOT + 2048:SLOT + 3072], i["rw_g2"][0, 0:P]),
                (ring[0:32, SLOT + 3072:SLOT + 4096], i["rw_g2"][0, P:LG])])
            for n in range(3):
                for hf in range(2):
                    half(("rkv", n, hf), i["rw_w_rkv"][0, n], hf)
            for n in range(MSTEPS):
                w, l, blk, _b = MODS[n // C]
                src = i[w] if l is None else i[w][l]
                if n >= 2:
                    sp.wait("mod used", n - 2)
                elif n == 1:
                    sp.wait("bonus all", C - 1)
                else:
                    sp.wait("used", "rkv", 2, 1)
                eng.dma_start(mw[n % 2], src[P * (n % C):P * (n % C) + P, 2048 * blk:2048 * (blk + 1)]
                              ).then_inc(in_sems[f"modw_in{n % 2}"], 16)
            sp.wait("mod used", MSTEPS - 1)
            sp.wait("modT", len(MODS) - 1)
            sp.wait("inverses")
            for hf in range(2):
                half(("wo", hf), i["rw_w_o"][0], hf)
            extra = moe_loads(0)
            for name, w, hf, n in ((("wkv",), i["w_kv"], 0, 30), (("wq", 0), i["at_w_q"][0], 0, 30),
                                   (("wq", 1), i["at_w_q"][0], 1, 32), (("ao", 0), i["at_w_o"][0], 0, 32)):
                eng.wait_ge(moe_sems[0]["down_made"], 32 * extra + n)
                half(name, w, hf)
            half(("ao", 1), i["at_w_o"][0], 1)
            moe_loads(1)

        @block.gpsimd
        def _(eng):
            pl = Engine(eng, "pool_done", sems, known, seen)
            outs = [0]

            def put(dst, src):
                eng.dma_start(dst, src).then_inc(in_sems["out_written"], 16)
                outs[0] += 16

            pl.did(eng.memset(rows[:, 2, :], 0.0), ("rows zeroed",))
            eng.dma_start(const[:, :], i["const_all"]).then_inc(in_sems["const_in"], 16)
            for j in range(2):
                eng.dma_start(xtok[:, j, :], i["x_prompt"][0, j * P:(j + 1) * P]).then_inc(in_sems["x_in"], 16)
            eng.dma_start(xtok[0:64, 2, :], i["x_sample"][0]).then_inc(in_sems["x_in"], 16)
            eng.dma_start(cph[:, 0:WN], i["const_wkv"]).then_inc(in_sems["wkvc_in"], 16)
            for h in range(2):
                eng.dma_start(sink[64 * h:64 * h + 64, :],
                              i["at_sinks"][0].rearrange("(c h) -> h c", h=2)[h:h + 1, :].broadcast_to([64, C]),
                              allow_slow_non_contiguous=True).then_inc(in_sems["sink_in"], 16)
            pl.wait("shift row")
            put(o[2][0, 0].rearrange("(c p) -> c p", p=P), shiftT[0:C, 0:P])
            put(o[6][0, 0].rearrange("(c p) -> c p", p=P), shiftT[0:C, P:2 * P])
            pl.wait("wkv ready")
            eng.dma_start(swin, i["state_wkv"][0, 0].rearrange("(c h) v k -> (h v) c k", h=2)
                          ).then_inc(in_sems["swkv_in"], 16)
            for r, n_out in ((0, 3), (1, 7)):
                pl.wait("swout ready", r)
                put(o[n_out][0, 0].rearrange("(c h) v k -> (h v) c k", h=2), swo[:, r])
            eng.dma_start(cph[:, 0:AN], i["const_att"]).then_inc(in_sems["attc_in"], 16)
            pl.wait("x mixed", 0)

            def load_router(l):
                eng.dma_start(router[:, :, 0:GROUPS], i["moe_w_group"][l].rearrange("(c p) n -> p c n", p=P)
                              ).then_inc(in_sems[f"router_in{l}"], 16)
                eng.dma_start(router[:, :, GROUPS:36], i["moe_w_expert"][l].rearrange("(c p) n -> p c n", p=P)
                              ).then_inc(in_sems[f"router_in{l}"], 16)

            load_router(0)
            pl.wait("x moe", 0)
            eng.dma_start(ktok, i["cache_k"][0].rearrange("t n d -> t (n d)")).then_inc(in_sems["cache_in"], 16)
            eng.dma_start(v64[:, 4:6, :], i["cache_v"][0].rearrange("(w t) n d -> t w (n d)", w=2)
                          ).then_inc(in_sems["cache_in"], 16)
            pl.wait("k64")
            for r, (n_out, w) in enumerate(((4, 0), (4, 1), (8, 2))):
                t0 = 64 * w if n_out == 4 else 0
                put(o[n_out][0, t0:t0 + 64].rearrange("t n d -> t (n d)"), k64[:, w, :])
            pl.wait("v64")
            for n_out, w, t0 in ((5, 2, 0), (5, 3, 64), (9, 6, 0)):
                put(o[n_out][0, t0:t0 + 64].rearrange("t n d -> t (n d)"), v64[:, w, :])
            pl.wait("x mixed", 1)
            load_router(1)
            for j in range(3):
                pl.wait("ytok", j)
                if j < 2:
                    put(o[0][0, j * P:(j + 1) * P], ytok[:, j, :])
                else:
                    put(o[1][0], ytok[0:64, 2, :])
            eng.wait_ge(in_sems["out_written"], outs[0])

        @block.tensor
        def _(eng):
            pe = Engine(eng, "pe_done", sems, known, seen)
            bank = Banks(pe, ps)
            ident = cst("ident")

            def mm(out, l, r, start, stop, **kw):
                return eng.matmul(out, l, r, start=start, stop=stop, **kw)

            def full(ins, *key):
                pe.did(ins, key)

            def mod_rows(pb, c, w):
                for n in range(4):
                    ins = mm(pb[32 * n:32 * n + 32, :], cs[:, c, :], w[:, 512 * n:512 * n + 512], c == 0, c == C - 1,
                             tile_position=(0, 32 * n))
                return ins

            def mod_turn(g):
                pe.wait("mod rows", g)
                pb = bank.open("modT", g)
                for qd in range(4):
                    ins = eng.transpose(pb[:, 128 * qd:128 * qd + 128], modrow[g < 0][:, 128 * qd:128 * qd + 128], ident)
                full(ins, "modT", g)

            def mod_step(n):
                for g in mods_turned([n]):
                    mod_turn(g)
                if n < MSTEPS:
                    g, c = divmod(n, C)
                    if c == 0:
                        bank.hold("mod", g)
                    eng.wait_ge(in_sems[f"modw_in{n % 2}"], 16 * (n // 2 + 1))
                    pe.did(mod_rows(ps[seen_bank(("mod", g))], c, mw[n % 2]), ("mod used", n), ("mod", g))
                elif n == MSTEPS:
                    bank.held = None

            def mean_square(tag):
                pb = bank.open("ms", tag)
                for c in range(C):
                    if c % 2 == 0:
                        pe.wait("squares", tag, c // 2)
                    ins = mm(pb[:, 0:T], cst("ones"), sq_buf(tag)[:, c, :], c == 0, c == C - 1)
                full(ins, "ms", tag)

            def project(tag, nout, src, wname, cols, acc=C):
                for m in range(nout):
                    s = arrived(pe, *wname(m // 4))
                    pb = bank.open(tag, m)
                    for c in range(C):
                        ins = mm(pb[:, 0:T], w512(s)[:, c, 128 * (m % 4):128 * (m % 4) + 128], src[:, c, :], c == 0,
                                 c == C - 1)
                    keys = [(tag, m)]
                    if m % 4 == 3 or m == nout - 1:
                        keys.append(("used",) + wname(m // 4))
                    pe.did(ins, *keys)

            def head_sums(tag, src):
                pb = bank.open(tag, 0)
                for c in range(C):
                    ins = mm(pb[0:16, 0:T], cst("selh")[:, 16 * c:16 * c + 16], src[:, c, :], c == 0, c == C - 1)
                full(ins, tag, 0)

            def head_spread(tag, src16):
                for c in range(C):
                    pb = bank.open(tag, c)
                    full(mm(pb[:, 0:T], wcst("selb", 16)[:, P * c:P * (c + 1)], src16, True, True), tag, c)

            eng.wait_ge(in_sems["const_in"], 16)
            eng.wait_ge(in_sems["vec_in"], 16 * sum(len(g) for g in VEC_GROUPS))
            pb = bank.open("vec")
            for g in range(3):
                ins = eng.transpose(pb[:, P * g:P * (g + 1)], rows[:, g, :], ident)
            full(ins, "vec")
            eng.wait_ge(in_sems["x_in"], 48)
            for c in range(C):
                pb = bank.open("xT", c)
                for j, (t0, k) in enumerate(TILES):
                    ins = eng.transpose(pb[:, t0:t0 + k], xtok[0:k, j, P * c:P * (c + 1)], ident[0:k, 0:k])
                full(ins, "xT", c)
            pe.wait("cs")
            pb = bank.open("mod", -1)
            for m in range(4):
                s = arrived(pe, "ada", m)
                for c in range(2):
                    ins = mod_rows(pb, 2 * m + c, slot(s, 4096)[:, 2048 * c:2048 * c + 2048])
                pe.did(ins, ("used", "ada", m), ("mod", -1))
            mod_turn(-1)

            mean_square("A0")
            pe.wait("h", "A0")
            pb = bank.open("shift")
            ins = eng.transpose(pb[0:C, 0:128], h0[:, :, SEQ - 1], ident)
            ins = eng.transpose(pb[0:C, 128:256], h0[:, :, T - 1], ident)
            full(ins, "shift")
            s = arrived(pe, "lora1")
            for n, (key, a, k) in enumerate((("w", 0, LW), ("a", 512, LA), ("g", 1024, LG))):
                w = ring[:, a:a + C * k].rearrange("p (c n) -> p c n", c=C)
                parts = [(0, k)] if k <= 128 else [(0, 128), (128, k - 128)]
                pe.wait("xm", 3 + n)
                for m, (c0, kk_) in enumerate(parts):
                    pb = bank.open("low", key, m)
                    for c in range(C):
                        ins = mm(pb[0:kk_, 0:T], w[:, c, c0:c0 + kk_], xm[(3 + n) % 2][:, c, :], c == 0, c == C - 1)
                    pe.did(ins, ("low", key, m), ("xm used", 3 + n))
            seen.at[("used", "lora1")] = seen.at[("low", "g", 1)]
            s = arrived(pe, "lora2")
            w2 = ring[0:64, SLOT:SLOT + 1024]
            a2 = ring[0:64, SLOT + 1024:SLOT + 2048]
            g2a = ring[:, SLOT + 2048:SLOT + 3072]
            g2b = ring[0:32, SLOT + 3072:SLOT + 4096]
            for key, w in (("w", w2), ("a", a2)):
                pe.wait("low ready", key, 0)
                for c in range(C):
                    pb = bank.open("up", key, c)
                    full(mm(pb[:, 0:T], w[:, P * c:P * (c + 1)], lows[key], True, True), "up", key, c)
            pe.wait("low ready", "g", 1)
            for c in range(C):
                pb = bank.open("up", "g", c)
                mm(pb[:, 0:T], g2a[:, P * c:P * (c + 1)], lows["g"], True, False)
                ins = mm(pb[:, 0:T], g2b[:, P * c:P * (c + 1)], lows["g1"], False, True)
                pe.did(ins, ("up", "g", c), ("used", "lora2"))
            for n in range(3):
                pe.wait("xm", n)
                project(("rkv", n), C, xm[n % 2], lambda hf, n=n: ("rkv", n, hf), 512)
                seen.at[("xm used", n)] = (pe.name, pe.n)
            pe.wait("kk squares")
            head_sums("kk sum", nrm)
            pe.wait("kk rstd")
            head_spread("kk rstd all", head16)
            pe.wait("rk")
            head_sums("bonus sum", tmp)
            pe.wait("bonus 16")
            head_spread("bonus all", head16b)
            pe.wait("wkv ready")
            i64 = cst("i64")

            def per_head(pb, cols, terms, c, last=True):
                for h in range(2):
                    r = slice(64 * h, 64 * h + 64)
                    for k, (l, m) in enumerate(terms):
                        ins = mm(pb[r, cols], l[r], m[r], k == 0, k == len(terms) - 1)
                return ins

            for j in range(NCH):
                t = slice(CH * j, CH * (j + 1))
                for nm, st in (("b", aa), ("k", kb)):
                    for hf in range(2):
                        pb = bank.open("A" + nm, j, hf)
                        for cc in range(4):
                            c = 4 * hf + cc
                            for h in range(2):
                                r = slice(64 * h, 64 * h + 64)
                                ins = mm(pb[r, P * cc:P * cc + P].rearrange("p (b t) -> p b t", b=2), st[r, c, t],
                                         ar[r, :, c, t], True, True)
                        full(ins, "A" + nm, j, hf)
                    mod_step(A_STEPS * j + "bk".index(nm))
                pb = bank.open("N1", j)
                for c in range(C):
                    ins = per_head(pb, slice(64 * c, 64 * c + 64), [(kk[:, c, t], aa[:, c, t])], c)
                full(ins, "N1", j)
                for nm, st in (("v", vb), ("b", aa), ("k", kb)):
                    pb = bank.open("tok" + nm, j)
                    for c in range(C):
                        ins = per_head(pb, slice(64 * c, 64 * c + 64), [(st[:, c, t], i64)], c)
                    full(ins, "tok" + nm, j)
                    if nm != "b":
                        mod_step(A_STEPS * j + 2 + "vk".index(nm))
            for l in range(2, 7):
                for j in range(NCH):
                    t = slice(CH * j, CH * (j + 1))
                    pe.wait("level", l, j)
                    pb = bank.open("W", l, j)
                    for c in range(C):
                        ins = per_head(pb, slice(64 * c, 64 * c + 64), [(nl[:, c, t], tmat[:, c, t])], c)
                    full(ins, "W", l, j)
                for j in range(NCH):
                    t = slice(CH * j, CH * (j + 1))
                    pe.wait("W ready", l, j)
                    pb = bank.open("TT", l, j)
                    for c in range(C):
                        ins = per_head(pb, slice(64 * c, 64 * c + 64), [(wmat[:, c, t], tt[:, c, t])], c)
                    full(ins, "TT", l, j)
                    if l < 6:
                        pb = bank.open("TW", l, j)
                        for c in range(C):
                            ins = per_head(pb, slice(64 * c, 64 * c + 64), [(tt[:, c, t], wmat[:, c, t])], c)
                        full(ins, "TW", l, j)
                    mod_step(steps_of_level(l)[j])
            eng.wait_ge(in_sems["swkv_in"], 16)
            pb = bank.open("s0")
            for c in range(C):
                ins = per_head(pb, slice(64 * c, 64 * c + 64), [(swin[:, c, :], i64)], c)
            full(ins, "s0")
            for n, j in enumerate((0, 4, 1, 2, 3)):
                r_ = 1 if j == 4 else 0
                t = slice(CH * j, CH * (j + 1))
                pe.wait("state", j)
                pe.wait("T ready", j)
                pb = bank.open("RHS", j)
                for c in range(C):
                    ins = per_head(pb, slice(64 * c, 64 * c + 64),
                                   [(kk[:, c, t], state[:, r_, c, :]), (aak[:, c, t], vb[:, c, t])], c)
                full(ins, "RHS", j)
                pe.wait("RHS ready", j)
                pb = bank.open("U", j)
                for c in range(C):
                    ins = per_head(pb, slice(64 * c, 64 * c + 64), [(tt[:, c, t], rhs_u[:, 0, c, :])], c)
                full(ins, "U", j)
                pe.wait("U ready", j)
                pb = bank.open("S", j)
                for c in range(C):
                    ins = per_head(pb, slice(64 * c, 64 * c + 64),
                                   [(aa[:, c, t], rhs_u[:, 1, c, :]), (kb[:, c, t], vb[:, c, t])], c)
                full(ins, "S", j)
                pb = bank.open("Y", j)
                for c in range(C):
                    ins = per_head(pb, slice(64 * c, 64 * c + 64),
                                   [(state[:, r_, c, :], rr[:, c, t]), (rhs_u[:, 1, c, :], arb[:, c, t]),
                                    (vb[:, c, t], ark[:, c, t])], c)
                full(ins, "Y", j)
                mod_step(step_of_state(n))
            for r_ in range(2):
                pe.wait("final state", r_)
                pb = bank.open("sout", r_)
                for c in range(C):
                    ins = per_head(pb, slice(64 * c, 64 * c + 64), [(state[:, r_, c, :], i64)], c)
                full(ins, "sout", r_)
            pe.wait("y all")
            head_sums("y sum", rr)
            pe.wait("y mean")
            head_spread("y mean all", head16)
            pe.wait("yc squares")
            head_sums("yc sum", E[0])
            pe.wait("y rstd")
            head_spread("y rstd all", head16)
            pe.wait("mix out")
            project("wo", C, rr, lambda hf: ("wo", hf), 512)

            def moe(l):
                S = moe_sems[l]
                mean_square(f"B{l}")
                eng.wait_ge(in_sems[f"router_in{l}"], 32)
                pb = [bank.open("logits", l, j) for j in range(3)]
                for c in range(C):
                    pe.wait("h", f"B{l}", c)
                    for j, (t0, k) in enumerate(TILES):
                        ins = mm(pb[j][0:k, 0:36], hT[:, c, t0:t0 + k], router[:, c, :], c == 0,
                                 c == C - 1)
                pe.did(ins, *[("logits", l, j) for j in range(3)])
                for j, (t0, k) in enumerate(TILES):
                    for hf in range(2):
                        pb = bank.open("htok", l, j, hf)
                        for cc in range(4):
                            ins = eng.transpose(pb[0:k, P * cc:P * cc + P], hT[:, 4 * hf + cc, t0:t0 + k], ident)
                        full(ins, "htok", l, j, hf)
                pe.wait("mask", l)
                pb = bank.open("rank", l)
                for j in range(3):
                    for jj in range(j + 1):
                        ins = mm(pb[:, EXP * j:EXP * j + EXP], cst("triu") if jj == j else cst("ones"),
                                 msk[:, jj, :], jj == 0, jj == j)
                for jj in range(3):
                    ins = mm(pb[:, 96:96 + EXP], cst("ones"), msk[:, jj, :], jj == 0, jj == 2)
                full(ins, "rank", l)
                pe.wait("htok ready", l)
                pe.wait("passes", l)
                for b in range(8):
                    if bank.owner[b] is not None:
                        pe.wait("read", *bank.owner[b])
                nb = eng.value_load(passes[0:1, 2 * l:2 * l + 1], min_val=1, max_val=5)

                def gather(k, u):
                    eng.wait_ge(S["sel_ready"], 2 * k + u + 1)
                    for hf in range(2):
                        if u == 1:
                            eng.wait_ge(S["xe_ready"], 4 * k + hf + 1)
                        for cc in range(4):
                            c = 4 * hf + cc
                            for j, (t0, kt) in enumerate(TILES):
                                ins = mm(ps[1 + hf][:, P * cc:P * cc + P], htok[0:kt, j, P * c:P * c + P],
                                         sel[0:kt, u, j, :], j == 0, j == 2)
                        ins.then_inc(S["xe_made"], 1)

                def hid_turn(k, u):
                    eng.wait_ge(S["h_ready"], 2 * k + u + 1)
                    if u == 0:
                        eng.wait_ge(S["y_added"], 8 * k + 1)
                    else:
                        eng.wait_ge(S["hT_ready"], 2 * k + 1)
                    for f in range(2):
                        ins = eng.transpose(ps[0][:, P * f:P * f + P], hid[:, u, P * f:P * f + P], ident)
                    ins.then_inc(S["hT_made"], 1)

                def down(k, u):
                    eng.wait_ge(S["hT_ready"], 2 * k + u + 1)
                    for v in range(2):
                        eng.wait_ge(S[f"dn_in{2 * u + v}"], 16 * k + 16)
                    for n in range(2):
                        if u == 1:
                            eng.wait_ge(S["down_ready"], 4 * k + n + 1)
                        for f in range(2):
                            for v in range(2):
                                s = 2 * u + v
                                w = ring[:, s * SLOT + 4096:(s + 1) * SLOT]
                                ins = mm(ps[4 + n][64 * v:64 * v + 64, :], hidT[:, u, f, 64 * v:64 * v + 64],
                                         w[:, D * f + 512 * n:D * f + 512 * n + 512], f == 0, f == 1)
                        ins.then_inc(S["down_made"], 1)

                def experts(k, ahead):
                    for u in range(2):
                        eng.wait_ge(S["xe_ready"], 4 * k + 3 + u)
                        for j, (t0, kt) in enumerate(TILES):
                            ins = eng.transpose(ps[1 + u][:, t0:t0 + kt], selw[0:kt, u, j, :], ident[0:kt, 0:kt])
                        ins.then_inc(S["selT_made"], 1)
                    for u in range(2):
                        for v in range(2):
                            eng.wait_ge(S[f"gu_in{2 * u + v}"], 16 * k + 16)
                        if u == 0:
                            eng.wait_ge(S["y_added"], 8 * k)
                        for c in range(C):
                            for v in range(2):
                                ins = mm(ps[3 + 4 * u][64 * v:64 * v + 64, :], xe[:, u, c, 64 * v:64 * v + 64],
                                         w512(2 * u + v)[:, c, :], c == 0, c == C - 1)
                        ins.then_inc(S["gu_made"], 1)
                    hid_turn(k, 0)
                    eng.wait_ge(S["selT_ready"], 2 * k + 2)
                    if ahead:
                        gather(k + 1, 0)
                    hid_turn(k, 1)
                    down(k, 0)
                    down(k, 1)
                    if ahead:
                        gather(k + 1, 1)
                    eng.wait_ge(S["hT_ready"], 2 * k + 2)
                    for c in range(C):
                        pb = ps[(6, 7, 3, 0)[c % 4]]
                        if c % 4 == 0:
                            eng.wait_ge(S["down_ready"], 4 * k + 3 + c // 4)
                        if c >= 4:
                            eng.wait_ge(S["y_added"], 8 * k + c - 2)
                        for u in range(2):
                            ins = mm(pb[:, 0:T], dslot[:, u, P * c:P * c + P], selT[:, u, :], u == 0, u == 1)
                        ins.then_inc(S["y_made"], 1)

                with eng.Fori(0, nb) as p:
                    for u in range(2):
                        gather(8 * p, u)
                    with eng.Fori(0, EXP // 4 - 1) as k_:
                        experts(8 * p + k_, True)
                    experts(8 * p + 7, False)
                pe.wait("x moe", l)

            moe(0)

            mean_square("A1")
            pe.wait("h", "KV")
            project("kv", 4, hkv, lambda hf: ("wkv",), 512)
            eng.wait_ge(in_sems["attc_in"], 16)
            for c in range(2):
                pe.wait("kraw", c)
                pb = bank.open("krot", c)
                full(mm(pb[:, 0:T], acst("ropep"), kraw[:, c, :], True, True), "krot", c)
            eng.wait_ge(in_sems["cache_in"], 32)
            pb = bank.open("kcache")
            for c in range(2):
                ins = eng.transpose(pb[:, P * c:P * c + P], ktok[:, P * c:P * c + P], ident)
            full(ins, "kcache")
            pe.wait("kT whole")
            for c in range(2):
                pb = bank.open("kswap", c)
                full(mm(pb[:, 0:448], acst("swap"), kT[:, c, :], True, True), "kswap", c)
            pe.wait("vT", 1)
            for w, t0 in enumerate((0, 64, 128, 192, 256)):
                pb = bank.open("v64", w)
                for c in range(2):
                    ins = eng.transpose(pb[0:64, P * c:P * c + P], vT[:, c, t0:t0 + 64], ident)
                full(ins, "v64", w)
            for w, t0 in enumerate((128, 192, 384)):
                pb = bank.open("k64", w)
                for c in range(2):
                    ins = eng.transpose(pb[0:64, P * c:P * c + P], kT[:, c, t0:t0 + 64], ident)
                full(ins, "k64", w)
            pe.wait("h", "A1")
            project("q", C, haq, lambda hf: ("wq", hf), 512)
            for c in range(C):
                pe.wait("qraw", c)
                pb = bank.open("qrot", c)
                full(mm(pb[:, 0:T], acst("ropep"), q[:, c, :], True, True), "qrot", c)
            pe.wait("kswapped", 1)
            for n in range(NCH):
                t0 = CH * n
                lo, hi = (max(0, n - 2) * CH, (n + 1) * CH) if n < 4 else (256, 448)
                W = hi - lo
                for b in range(4):
                    pe.wait("q ready", 2 * b + 1)
                    pb = bank.open("score", n, b)
                    for cc in range(2):
                        c = 2 * b + cc
                        g = c // 2
                        for h in range(2):
                            var = 0 if g % 2 == h else 2
                            r = slice(64 * h, 64 * h + 64)
                            ins = mm(pb[r, 256 * cc:256 * cc + W], q[r, c, t0:t0 + CH], kT[r, var + g // 2, lo:hi],
                                     True, True)
                    full(ins, "score", n, b)
                for w in range(W // CH):
                    for hf in range(2):
                        pe.wait("prob", n, 4 * hf + 3)
                        pb = bank.open("pT", n, w, hf)
                        for cc in range(4):
                            ins = eng.transpose(pb[0:64, P * cc:P * cc + P], prob[:, 4 * hf + cc, CH * w:CH * w + CH],
                                                ident)
                        full(ins, "pT", n, w, hf)
                pe.wait("v64")
                pe.wait("pT ready", n)
                pb = bank.open("o", n)
                first = max(0, n - 2) if n < 4 else 4
                for g in range(NKV):
                    for h in range(2):
                        for w in range(W // CH):
                            ins = mm(pb[64 * h:64 * h + 64, P * g:P * g + P].rearrange("p (c s) -> p c s", c=2),
                                     v64[:, first + w, 64 * g:64 * g + 64],
                                     pT[:, w, 2 * g:2 * g + 2, 64 * h:64 * h + 64], w == 0, w == W // CH - 1)
                full(ins, "o", n)
            pe.wait("oT", NCH - 1)
            project("ao", C, oT, lambda hf: ("ao", hf), 512)
            moe(1)
            mean_square("F")
            pe.wait("h", "F")
            for j, (t0, k) in enumerate(TILES):
                for hf in range(2):
                    pb = bank.open("ytok", j, hf)
                    for cc in range(4):
                        ins = eng.transpose(pb[0:k, P * cc:P * cc + P], E[1][:, 4 * hf + cc, t0:t0 + k], ident)
                    full(ins, "ytok", j, hf)

        @block.scalar
        def _(eng):
            ac = Engine(eng, "act_done", sems, known, seen)

            def pk(*key):
                ac.wait(*key)
                return ps[seen_bank(key)]

            def act(out, in_, f, *keys, **kw):
                ac.did(eng.activation(out, in_, f, **kw), *keys)

            def squares(tag):
                ac.wait("x for", tag)
                for b in range(4):
                    act(sq_buf(tag)[:, 2 * b:2 * b + 2, :], x[:, 2 * b:2 * b + 2, :], ACT.Square,
                        ("squares", tag, b))

            def root(tag):
                ac.wait("ms ready", tag)
                act(rstd[:, :], rstd[:, :], ACT.Sqrt, ("root", tag))

            def mod_copy(steps):
                for g in mods_done(steps):
                    pb = pk("mod", g)
                    ac.wait("modT", g - 1)
                    act(modrow[0], pb[:, :], ACT.Copy, ("read", "mod", g), ("mod rows", g))

            ac.wait("rows zeroed")
            vec_loads(eng, 1)
            ac.wait("vec ready")
            act(small[:, 0:16], vcol("c_prompt", 0, 16), ACT.Silu, ("silu c",))
            squares("A0")
            act(modrow[1], pk("mod", -1)[:, :], ACT.Copy, ("read", "mod", -1), ("mod rows", -1))
            root("A0")
            pb = pk("shift")
            act(shiftT[0:C, :], pb[0:C, 0:256], ACT.Copy, ("read", "shift"), ("shift row",))
            act(lows["w"], pk("low", "w", 0)[0:64, 0:T], ACT.Tanh, ("read", "low", "w", 0), ("low ready", "w", 0))
            act(lows["a"], pk("low", "a", 0)[0:64, 0:T], ACT.Copy, ("read", "low", "a", 0), ("low ready", "a", 0))
            act(lows["g"], pk("low", "g", 0)[:, 0:T], ACT.Sigmoid, ("read", "low", "g", 0), ("low ready", "g", 0))
            act(lows["g1"], pk("low", "g", 1)[0:32, 0:T], ACT.Sigmoid, ("read", "low", "g", 1), ("low ready", "g", 1))
            for key, dst, v in (("w", sig, "rw_w0"), ("a", aa, "rw_a0")):
                for c in range(C):
                    act(dst[:, c, :], pk("up", key, c)[:, 0:T], ACT.Sigmoid, ("read", "up", key, c), (key + " ready",),
                        bias=vcol(v, c))
            for c in range(C):
                act(gb[:, c, :], pk("up", "g", c)[:, 0:T], ACT.Copy, ("read", "up", "g", c))
            for n, dst in ((0, rr), (1, kb), (2, vb)):
                for c in range(C):
                    act(dst[:, c, :], pk(("rkv", n), c)[:, 0:T], ACT.Copy, ("read", ("rkv", n), c), ("rkv ready", n))
            ac.wait("kk raw")
            act(nrm[:, :, :], kk[:, :, :], ACT.Square, ("kk squares",))
            ac.wait("kk ms")
            act(head16, head16, ACT.Sqrt, ("kk root",))
            ac.wait("cum")
            act(dec[:, :, :], cum[:, :, :], ACT.Exp, ("dec",), scale=-DECAY)
            ac.wait("dm arg")
            act(sig[:, :, :], sig[:, :, :], ACT.Exp, ("dm",), scale=-DECAY)
            ac.wait("kk done")
            act(dinv[:, :, :], cum[:, :, :], ACT.Exp, ("dinv",), scale=DECAY)
            for j in range(NCH):
                t = slice(CH * j, CH * (j + 1))
                for nm, dst in (("v", vb), ("b", aa), ("k", kb)):
                    pb = pk("tok" + nm, j)
                    act(dst[:, :, t], pb[:, :].rearrange("p (c t) -> p c t", c=C), ACT.Copy,
                        ("read", "tok" + nm, j), ("tok ready", j))
                mod_copy(range(A_STEPS * j, A_STEPS * (j + 1)))
            for l in range(2, 7):
                for j in range(NCH):
                    t = slice(CH * j, CH * (j + 1))
                    pb = pk("W", l, j)
                    act(wmat[:, :, t], pb[:, :].rearrange("p (c t) -> p c t", c=C), ACT.Copy,
                        ("read", "W", l, j), ("W ready", l, j))
                mod_copy(steps_of_level(l))
            pb = pk("s0")
            act(state[:, 1], pb[:, :].rearrange("p (c t) -> p c t", c=C), ACT.Copy, ("read", "s0"), ("state", 4))
            for n, j in enumerate((0, 4, 1, 2, 3)):
                pb = pk("RHS", j)
                act(rhs_u[:, 0], pb[:, :].rearrange("p (c t) -> p c t", c=C), ACT.Copy, ("read", "RHS", j),
                    ("RHS ready", j))
                pb = pk("U", j)
                act(rhs_u[:, 1], pb[:, :].rearrange("p (c t) -> p c t", c=C), ACT.Copy, ("read", "U", j),
                    ("U ready", j))
                pb = pk("Y", j)
                act(rr[:, :, CH * j:CH * (j + 1)], pb[:, :].rearrange("p (c t) -> p c t", c=C), ACT.Copy,
                    ("read", "Y", j), ("y all",))
                mod_copy([step_of_state(n)])
            for r_ in range(2):
                pb = pk("sout", r_)
                act(swo[:, r_], pb[:, :].rearrange("p (c t) -> p c t", c=C), ACT.Copy, ("read", "sout", r_),
                    ("swout ready", r_), ("read", "swout", r_))
            ac.wait("yc")
            act(E[0][:, :, :], rr[:, :, :], ACT.Square, ("yc squares",))
            ac.wait("y var")
            act(head16, head16, ACT.Sqrt, ("y root",))

            def moe(l):
                S = moe_sems[l]
                squares(f"B{l}")
                root(f"B{l}")
                for j, (t0, k) in enumerate(TILES):
                    for hf in range(2):
                        act(htok[0:k, j, 512 * hf:512 * hf + 512], pk("htok", l, j, hf)[0:k, :], ACT.Copy,
                            ("read", "htok", l, j, hf), ("htok ready", l))
                ac.wait("group max", l)
                ac.wait("top2", l)
                act(rt[:, 6:9, 0:4], rt[:, 3:6, 0:4], ACT.Exp)
                act(rt[:, 36, 0:3], rt[:, 35, 0:3], ACT.Exp, ("route exp", l))
                ac.wait("passes", l)
                eng.wait_ge(in_sems["out_written"], (64, 160)[l])
                nb = eng.value_load(passes[0:1, 2 * l:2 * l + 1], min_val=1, max_val=5)

                def gathered(k, u):
                    for hf in range(2):
                        eng.wait_ge(S["xe_made"], 4 * k + 2 * u + hf + 1)
                        eng.activation(xe[:, u, 4 * hf:4 * hf + 4, :],
                                       ps[1 + hf][:, :].rearrange("p (c s) -> p c s", c=4),
                                       ACT.Copy).then_inc(S["xe_ready"], 1)

                def experts(k, ahead):
                    for u in range(2):
                        eng.wait_ge(S["selT_made"], 2 * k + u + 1)
                        eng.activation(selT[:, u, :], ps[1 + u][:, 0:T], ACT.Copy).then_inc(S["selT_ready"], 1)
                    for u in range(2):
                        eng.wait_ge(S["gu_made"], 2 * k + u + 1)
                        eng.activation(silu[:, u, :], ps[3 + 4 * u][:, 0:FE], ACT.Silu).then_inc(S["silu_ready"], 1)
                    if ahead:
                        gathered(k + 1, 0)
                    for u in range(2):
                        for n in range(2):
                            eng.wait_ge(S["down_made"], 4 * k + 2 * u + n + 1)
                            eng.activation(dslot[:, u, 512 * n:512 * n + 512], ps[4 + n][:, :],
                                           ACT.Copy).then_inc(S["down_ready"], 1)
                    if ahead:
                        gathered(k + 1, 1)

                with eng.Fori(0, nb) as p:
                    for u in range(2):
                        gathered(8 * p, u)
                    with eng.Fori(0, EXP // 4 - 1) as k_:
                        experts(8 * p + k_, True)
                    experts(8 * p + 7, False)
                ac.wait("x moe", l)

            moe(0)
            squares("A1")
            root("A1")
            for c in range(4):
                dst = kraw[:, c, :] if c < 2 else vT[:, c - 2, :]
                act(dst, pk("kv", c)[:, 0:T], ACT.Identity, ("read", "kv", c), ("kraw", c) if c < 2 else ("vT", c - 2),
                    bias=vcol("b_kv", c))
            act(kT[:, 0:2, 256:384], pk("kcache")[:, 0:256].rearrange("p (c t) -> p c t", c=2), ACT.Copy,
                ("read", "kcache"), ("kcache ready",))
            for c in range(2):
                act(kT[:, 2 + c, :], pk("kswap", c)[:, 0:448], ACT.Copy, ("read", "kswap", c), ("kswapped", c))
            for w in range(5):
                act(v64[:, w if w < 4 else 6, :], pk("v64", w)[0:64, 0:256], ACT.Copy, ("read", "v64", w), ("v64",))
            for w in range(3):
                act(k64[:, w, :], pk("k64", w)[0:64, 0:256], ACT.Copy, ("read", "k64", w), ("k64",))
            for c in range(C):
                act(q[:, c, :], pk("q", c)[:, 0:T], ACT.Identity, ("read", "q", c), ("qraw", c),
                    bias=vcol("at_b_q", c))
            for n in range(NCH):
                W = min(n + 1, 3) * CH if n < 4 else 192
                for b in range(4):
                    ac.wait("row max", n, b)
                    for cc in range(2):
                        c = 2 * b + cc
                        act(prob[:, c, 0:W], ps[seen_bank(("score", n, b))][:, 256 * cc:256 * cc + W], ACT.Exp,
                            ("read", "score", n, b), ("exp", n, c), bias=att[:, 1, c:c + 1], scale=SCALE,
                            accum_out=att[:, 2, c:c + 1])
                act(att[:, 3, :], att[:, 4, :], ACT.Exp, ("sink exp", n))
                for w in range(W // CH):
                    for hf in range(2):
                        act(pT[:, w, 4 * hf:4 * hf + 4, :],
                            pk("pT", n, w, hf)[0:64, :].rearrange("p (c s) -> p c s", c=4), ACT.Copy,
                            ("read", "pT", n, w, hf), ("pT ready", n))
                act(oT[:, :, CH * n:CH * (n + 1)], pk("o", n)[:, :].rearrange("p (c t) -> p c t", c=C), ACT.Copy,
                    ("read", "o", n), ("oT", n))
            moe(1)
            squares("F")
            root("F")
            for j, (t0, k) in enumerate(TILES):
                for hf in range(2):
                    act(ytok[0:k, j, 512 * hf:512 * hf + 512], pk("ytok", j, hf)[0:k, :], ACT.Copy,
                        ("read", "ytok", j, hf), ("ytok", j))

        @block.vector
        def _(eng):
            ve = Engine(eng, "dve_done", sems, known, seen)

            def pk(*key):
                ve.wait(*key)
                return ps[seen_bank(key)]

            def op(ins, *keys):
                ve.did(ins, *keys)

            def tt_(out, a, b, o_, *keys):
                op(eng.tensor_tensor(out, a, b, o_), *keys)

            def ts(out, a, s1, s2, o1, o2, *keys):
                op(eng.tensor_scalar(out, a, s1, s2, o1, o2), *keys)

            def stt(out, a, s_, b, o1, o2, *keys):
                op(eng.scalar_tensor_tensor(out, a, s_, b, o1, o2), *keys)

            M, A_ = ALU.mult, ALU.add

            op(eng.memset(cs[:, :, :], 0.0))
            op(eng.memset(state[:, 0], 0.0), ("state", 0))
            op(eng.tensor_copy(vec[:, :], pk("vec")[:, 0:3 * P]), ("read", "vec"), ("vec ready",))
            ve.wait("silu c")
            for r in range(2):
                op(eng.tensor_copy(cs[:, :, r], small[:, 8 * r:8 * r + 8]), ("cs",))
            for c in range(C):
                op(eng.tensor_copy(x[:, c, :], pk("xT", c)[:, 0:T]), ("read", "xT", c), ("x for", "A0"))

            def turned(g, dst, bias):
                v = pk("modT", g)[:, :].rearrange("p (q j r) -> p r q j", q=4, j=4)
                for r in range(2):
                    tt_(dst(r).rearrange("p (j q) -> p q j", q=4), v[:, r],
                        vec[:, bias:bias + 16].rearrange("p (j q) -> p q j", q=4), A_, ("read", "modT", g),
                        ("mod ready", g))

            def mods_out(steps):
                for g in mods_turned(steps):
                    _w, l, blk, b = MODS[g]
                    if l is None:
                        turned(g, lambda r: kvmod[:, r, :], VCOL[b])
                    else:
                        turned(g, lambda r: mod[:, l, r, 16 * blk:16 * blk + 16], VCOL[b] + 48 * l + 16 * blk)

            def rms(tag):
                ts(rstd[:, :], pk("ms", tag)[:, 0:T], 1.0 / D, RMS_EPS, M, A_, ("read", "ms", tag), ("ms ready", tag))
                ve.wait("root", tag)
                op(eng.reciprocal(rstd[:, :], rstd[:, :]))

            def modulated(tag, src, dst, g, md, sh, sc):
                if md is not None:
                    for r in range(2):
                        ts(coef[:, r, :], md(r)[:, sc:sc + C], 1.0, None, A_, ALU.bypass)
                    ve.settle()
                    for r in range(2):
                        tt_(coef[:, r, :], coef[:, r, :], g, M)
                    ve.settle()
                for c in range(C):
                    if md is None:
                        ts(dst[:, c, :], src[:, c, :], g[:, c:c + 1], None, M, ALU.bypass, ("h", tag), ("h", tag, c))
                    else:
                        for r, t0, k in SEQS:
                            ts(dst[:, c, t0:t0 + k], src[:, c, t0:t0 + k], coef[:, r, c:c + 1],
                               md(r)[:, sh + c:sh + c + 1], M, A_, ("h", tag), ("h", tag, c))
                ve.settle()

            def mdl(l):
                return lambda r: mod[:, l, r, :]

            def gated(tag, l, gate, *key):
                for c in range(C):
                    pb = pk(*key, c)
                    for r, t0, k in SEQS:
                        stt(x[:, c, t0:t0 + k], pb[:, t0:t0 + k], mod[:, l, r, gate + c:gate + c + 1],
                            x[:, c, t0:t0 + k], M, A_, ("read",) + key + (c,), *tag)
                ve.settle()

            turned(-1, lambda r: mod[:, 0, r, 0:16], VCOL["ada_b"])
            rms("A0")
            ve.settle()
            tt_(h0[:, :, :], x[:, :, :], bmid(rstd[:, :], C), M)
            ve.settle()
            modulated("A0", h0, h0, vcol("norm_g", 0, C), mdl(0), 0, 8)
            tt_(diff[:, :, 1:T], h0[:, :, 0:T - 1], h0[:, :, 1:T], ALU.subtract)
            ve.settle()
            ts(diff[:, :, 0], h0[:, :, 0], -1.0, None, M, ALU.bypass)
            tt_(diff[:, :, SEQ], vcol("state_shift", 0, C), h0[:, :, SEQ], ALU.subtract)
            ve.settle()
            order = (3, 4, 5, 0, 1, 2)
            for k, n in enumerate(order):
                if k >= 2:
                    prev = [m for m in order[:k] if m % 2 == n % 2][-1:]
                    if prev:
                        ve.wait("xm used", prev[0])
                for c in range(C):
                    stt(xm[n % 2][:, c, :], diff[:, c, :], vcol("rw_mu", 8 * n + c), h0[:, c, :], M, A_, ("xm", n))
            ve.wait("rkv ready", 1)
            ve.wait("a ready")
            eng.wait_ge(in_sems["wkvc_in"], 16)
            tt_(kk[:, :, :], kb[:, :, :], bc(vcol("rw_k_k", 0, C), T), M, ("kk raw",))
            stt(tmp[:, :, :], aa[:, :, :], -1.0, bc(vcol("rw_k_a", 0, C), T), A_, M)
            ve.settle()
            stt(kb[:, :, :], tmp[:, :, :], 1.0, kb[:, :, :], A_, M)
            ve.settle()
            ve.wait("w ready")
            ve.wait("xm used", 2)
            for c in range(C):
                op(eng.tensor_tensor_scan(cum[:, c, :], wcst("scan"), sig[:, c, :], 0.0, M, A_), ("cum",))
            ve.settle()
            tt_(sig[:, :, :], cum[:, :, :], sig[:, :, :], ALU.subtract, ("dm arg",))
            ts(head16, pk("kk sum", 0)[0:16, 0:T], 1e-24, None, ALU.max, ALU.bypass, ("read", "kk sum", 0),
               ("kk ms",))
            ve.wait("kk root")
            op(eng.reciprocal(head16, head16), ("kk rstd",))
            tt_(tmp[:, :, :], rr[:, :, :], kb[:, :, :], M)
            ve.settle()
            tt_(tmp[:, :, :], tmp[:, :, :], bc(vcol("rw_r_k", 0, C), T), M, ("rk",))
            for c in range(C):
                tt_(kk[:, c, :], kk[:, c, :], pk("kk rstd all", c)[:, 0:T], M, ("read", "kk rstd all", c), ("kk done",))
            op(eng.tensor_copy(head16b, pk("bonus sum", 0)[0:16, 0:T]), ("read", "bonus sum", 0), ("bonus 16",))
            ve.settle()
            tt_(aa[:, :, :], kk[:, :, :], aa[:, :, :], M)
            ve.wait("dm")
            ve.settle()
            stt(kk[:, :, :], kk[:, :, :], -1.0, sig[:, :, :], M, M)
            ve.wait("dec")
            tt_(rr[:, :, :], rr[:, :, :], dec[:, :, :], M)
            op(eng.tensor_copy(dend[:, :, :], dec[:, :, CH - 1:T:CH]))
            ve.wait("rkv ready", 2)
            for c in range(C):
                tt_(bonus[:, c, :], vb[:, c, :], pk("bonus all", c)[:, 0:T], M, ("read", "bonus all", c))
            ve.wait("dinv")
            tt_(aa[:, :, :], aa[:, :, :], dinv[:, :, :], M)
            tt_(kb[:, :, :], kb[:, :, :], dinv[:, :, :], M, ("wkv ready",))
            ve.settle()
            for j in range(NCH):
                t = slice(CH * j, CH * (j + 1))
                for nm, strict, incl in (("b", nt, arb), ("k", aak, ark)):
                    for hf in range(2):
                        pb = pk("A" + nm, j, hf)[:, :].rearrange("p (c b t) -> p c b t", c=4, b=2)
                        cs4 = slice(4 * hf, 4 * hf + 4)
                        tt_(strict[:, cs4, t], pb[:, :, 0, :], bmid(wcst("maskA")[:, 0:64], 4), M)
                        tt_(incl[:, cs4, t], pb[:, :, 1, :], bmid(wcst("maskA")[:, 64:128], 4), M,
                            ("read", "A" + nm, j, hf))
                pb = pk("N1", j)[:, :].rearrange("p (c t) -> p c t", c=C)
                ve.settle()
                tt_(tmat[:, :, t], pb, bmid(wcst("lev1n"), C), M, ("read", "N1", j))
                tt_(tt[:, :, t], nt[:, :, t], bmid(wcst("lev")[:, 0:64], C), M)
                ve.settle()
                tt_(tmat[:, :, t], tmat[:, :, t], bmid(cst("i64"), C), A_)
                tt_(tt[:, :, t], tt[:, :, t], bmid(cst("i64"), C), A_)
                tt_(nl[:, :, t], nt[:, :, t], bmid(wcst("lev")[:, 64:128], C), M, ("level", 2, j))
                mods_out(range(A_STEPS * j, A_STEPS * (j + 1)))
                ve.settle()
            for l in range(2, 7):
                for j in range(NCH):
                    t = slice(CH * j, CH * (j + 1))
                    pb = pk("TT", l, j)[:, :].rearrange("p (c t) -> p c t", c=C)
                    if l < 6:
                        ve.wait("TW", l, j)
                    tt_(tt[:, :, t], tt[:, :, t], pb, A_, ("read", "TT", l, j), ("T ready", j), ("inverses",))
                    if l < 6:
                        pb = pk("TW", l, j)[:, :].rearrange("p (c t) -> p c t", c=C)
                        tt_(tmat[:, :, t], tmat[:, :, t], pb, A_, ("read", "TW", l, j))
                        tt_(nl[:, :, t], nt[:, :, t], bmid(wcst("lev")[:, 64 * l:64 * l + 64], C), M,
                            ("level", l + 1, j))
                    mods_out([steps_of_level(l)[j]])
            ve.settle()
            for n, j in enumerate((0, 4, 1, 2, 3)):
                r_ = 1 if j == 4 else 0
                pb = pk("S", j)[:, :].rearrange("p (c t) -> p c t", c=C)
                ve.wait("Y", j)
                tt_(state[:, r_], state[:, r_], pb, A_, ("read", "S", j))
                ve.settle()
                keys = [("state", j + 1)] if j < 3 else [("final state", 0 if j == 3 else 1)]
                tt_(state[:, r_], state[:, r_], bc(dend[:, :, j], HD), M, *keys)
                mods_out([step_of_state(n)])
            ve.wait("y all")
            ts(head16, pk("y sum", 0)[0:16, 0:T], 1.0 / HD, None, M, ALU.bypass, ("read", "y sum", 0), ("y mean",))
            for c in range(C):
                tt_(rr[:, c, :], rr[:, c, :], pk("y mean all", c)[:, 0:T], ALU.subtract, ("read", "y mean all", c),
                    ("yc",))
            ts(head16, pk("yc sum", 0)[0:16, 0:T], 1.0 / HD, GN_EPS, M, A_, ("read", "yc sum", 0), ("y var",))
            ve.wait("y root")
            op(eng.reciprocal(head16, head16), ("y rstd",))
            for c in range(C):
                tt_(rr[:, c, :], rr[:, c, :], pk("y rstd all", c)[:, 0:T], M, ("read", "y rstd all", c))
            ve.settle()
            for c in range(C):
                ts(rr[:, c, :], rr[:, c, :], vcol("rw_lnx_w", c), vcol("rw_lnx_b", c), M, A_)
            ve.settle()
            tt_(rr[:, :, :], rr[:, :, :], bonus[:, :, :], A_)
            ve.settle()
            tt_(rr[:, :, :], rr[:, :, :], gb[:, :, :], M, ("mix out",))
            gated([("x mixed", 0), ("x for", "B0")], 0, 16, "wo")

            def moe(l):
                S = moe_sems[l]
                rms(f"B{l}")
                ve.settle()
                tt_(hT[:, :, :], x[:, :, :], bmid(rstd[:, :], C), M)
                ve.settle()
                modulated(f"B{l}", hT, hT, vcol("norm_g", 16 * l + 8, C), mdl(l), 24, 32)
                op(eng.memset(ysum[:, :, :], 0.0))
                op(eng.memset(lg[:, :, :], 0.0))
                ve.settle()
                for j, (t0, k) in enumerate(TILES):
                    op(eng.tensor_copy(lg[0:k, j, :], pk("logits", l, j)[0:k, 0:36]), ("read", "logits", l, j))
                ve.settle()
                R = lambda a, n=8: rt[:, a:a + 3, 0:n]
                g4 = lg[:, :, 0:4]
                e32 = lg[:, :, 4:36].rearrange("p j (g e) -> p j g e", g=4)
                sc_ = lambda a: rt[:, a, 0:3]
                down = cst("iota")

                def first_one(dst, key, src, mx, n):
                    tt_(R(key, n), src, bc(mx, n), ALU.is_equal)
                    ve.settle()
                    for a in range(n):
                        ts(rt[:, key:key + 3, a], rt[:, key:key + 3, a], float(n - a), None, M, ALU.bypass)
                    ve.settle()
                    op(eng.tensor_reduce(sc_(39), R(key, n), AX.X, ALU.max))
                    ve.settle()
                    tt_(R(dst, n), R(key, n), bc(sc_(39), n), ALU.is_equal)
                    ve.settle()

                op(eng.tensor_reduce(sc_(30), g4, AX.X, ALU.max))
                ve.settle()
                tt_(R(3, 4), g4, bc(sc_(30), 4), ALU.subtract, ("group max", l))
                first_one(12, 9, g4, sc_(30), 4)
                for g in range(4):
                    tt_(g48[:, :, g, :], e32[:, :, g, :], bc(rt[:, 12:15, g], 8), M)
                ve.settle()
                tt_(R(15), g48[:, :, 0, :], g48[:, :, 1, :], A_)
                tt_(R(18), g48[:, :, 2, :], g48[:, :, 3, :], A_)
                ve.settle()
                tt_(R(15), R(15), R(18), A_)
                ve.settle()
                op(eng.tensor_reduce(sc_(33), R(15), AX.X, ALU.max))
                ve.settle()
                first_one(21, 18, R(15), sc_(33), 8)
                stt(R(24), R(21), -3e38, R(15), M, A_)
                ve.settle()
                op(eng.tensor_reduce(sc_(34), R(24), AX.X, ALU.max))
                ve.settle()
                tt_(sc_(35), sc_(34), sc_(33), ALU.subtract, ("top2", l))
                first_one(27, 18, R(24), sc_(34), 8)
                ve.wait("route exp", l)
                op(eng.tensor_reduce(sc_(37), rt[:, 6:9, 0:4], AX.X, A_))
                ts(sc_(38), sc_(36), 1.0, None, A_, ALU.bypass)
                ve.settle()
                tt_(sc_(38), sc_(38), sc_(37), M)
                ve.settle()
                op(eng.reciprocal(sc_(38), sc_(38)))
                ve.settle()
                tt_(sc_(37), sc_(38), sc_(36), M)
                ve.settle()
                tt_(R(15), R(21), bc(sc_(38), 8), M)
                tt_(R(18), R(27), bc(sc_(37), 8), M)
                tt_(R(24), R(21), R(27), A_)
                ve.settle()
                tt_(R(15), R(15), R(18), A_)
                ve.settle()
                for g in range(4):
                    tt_(cw[:, :, 8 * g:8 * g + 8], R(15), bc(rt[:, 12:15, g], 8), M)
                    tt_(msk[:, :, 8 * g:8 * g + 8], R(24), bc(rt[:, 12:15, g], 8), M)
                ve.settle()
                op(eng.memset(msk[64:128, 2, :], 0.0), ("mask", l))
                pb = pk("rank", l)
                tt_(posn[:, :, :], pb[:, 0:96].rearrange("p (j e) -> p j e", j=3), msk[:, :, :], M)
                op(eng.tensor_reduce(small[:, 0:1], pb[:, 96:96 + EXP], AX.X, ALU.max), ("read", "rank", l))
                ve.settle()
                for a in range(4):
                    ts(small[:, 1 + a:2 + a], small[:, 0:1], float(SLOTS * (a + 1)), None, ALU.is_gt, ALU.bypass)
                ve.settle()
                op(eng.tensor_reduce(small[:, 5:6], small[:, 1:5], AX.X, A_))
                ve.settle()
                ts(passes[:, 2 * l:2 * l + 1], small[:, 5:6], 1.0, None, A_, ALU.bypass)
                op(eng.tensor_copy(passes[:, 2 * l + 1:2 * l + 2], small[:, 5:6]), ("passes", l))
                ve.settle()
                eng.memset(small[:, 8:9], 0.0).then_inc(S["pos_ready"], 1)
                nb = eng.value_load(passes[0:1, 2 * l:2 * l + 1], min_val=1, max_val=5)
                eng.memset(small[:, 9:10], 0.0).then_inc(S["y_added"], 1)

                def select(e, u):
                    for v in range(2):
                        for j, (t0, kt) in enumerate(TILES):
                            a = slice(64 * v, 64 * v + 64)
                            eng.tensor_scalar(sel[0:kt, u, j, a], cst("iota", kt), posn[0:kt, j, bass.ds(e + v, 1)],
                                              None, ALU.is_equal, ALU.bypass)
                            ins = eng.tensor_scalar(selw[0:kt, u, j, a], cst("iota", kt),
                                                    posn[0:kt, j, bass.ds(e + v, 1)], cw[0:kt, j, bass.ds(e + v, 1)],
                                                    ALU.is_equal, M)
                    ins.then_inc(S["sel_ready"], 1)

                def experts(k, e_next):
                    for u in range(2):
                        eng.wait_ge(S["silu_ready"], 2 * k + u + 1)
                        eng.tensor_tensor(hid[:, u, :], silu[:, u, :], ps[3 + 4 * u][:, FE:2 * FE],
                                          M).then_inc(S["h_ready"], 1)
                        if u == 0 and e_next is not None:
                            for w in range(2):
                                select(e_next + 2 * w, w)
                        eng.wait_ge(S["hT_made"], 2 * k + u + 1)
                        eng.tensor_copy(hidT[:, u], ps[0][:, 0:2 * P].rearrange("p (f s) -> p f s", f=2)
                                        ).then_inc(S["hT_ready"], 1)
                    for c in range(C):
                        eng.wait_ge(S["y_made"], 8 * k + c + 1)
                        eng.tensor_tensor(ysum[:, c, :], ysum[:, c, :], ps[(6, 7, 3, 0)[c % 4]][:, 0:T],
                                          A_).then_inc(S["y_added"], 1)

                with eng.Fori(0, nb) as p:
                    eng.wait_ge(S["pos_ready"], p + 1)
                    for u in range(2):
                        select(2 * u, u)
                    with eng.Fori(0, EXP // 4 - 1) as k_:
                        experts(8 * p + k_, 4 * k_ + 4)
                    experts(8 * p + 7, None)
                    eng.tensor_scalar(posn[:, :, :], posn[:, :, :], -float(SLOTS), None, A_, ALU.bypass
                                      ).then_inc(S["pos_ready"], 1)
                eng.wait_ge(S["y_added"], 64 * nb + 1)
                for c in range(C):
                    for r, t0, k in SEQS:
                        stt(x[:, c, t0:t0 + k], ysum[:, c, t0:t0 + k], mod[:, l, r, 40 + c:40 + c + 1],
                            x[:, c, t0:t0 + k], M, A_, ("x moe", l), ("x for", "A1" if l == 0 else "F"))
                ve.settle()

            moe(0)
            rms("A1")
            ve.settle()
            tt_(E[0][:, :, :], x[:, :, :], bmid(rstd[:, :], C), M)
            ve.settle()
            modulated("KV", E[0], hkv, vcol("kv_norm_g", 0, C), lambda r: kvmod[:, r, :], 0, 8)
            modulated("A1", E[0], haq, vcol("norm_g", 16, C), mdl(1), 0, 8)
            for r in range(2):
                tt_(bog[:, r, :], vcol("at_b_o", 0, C), mod[:, 1, r, 16:24], M)
            eng.wait_ge(in_sems["attc_in"], 16)
            for c in range(2):
                tt_(krot[:, c, :], acst("sin"), pk("krot", c)[:, 0:T], M, ("read", "krot", c))
                tt_(kraw[:, c, :], kraw[:, c, :], acst("cos"), M)
                ve.settle()
                tt_(kT[:, c, 0:SEQ], kraw[:, c, 0:SEQ], krot[:, c, 0:SEQ], A_)
                tt_(kT[:, c, 384:448], kraw[:, c, SEQ:T], krot[:, c, SEQ:T], A_)
            ve.settle()
            ve.wait("kcache ready")
            ts(small[:, 8:9], small[:, 0:1], 0.0, None, M, ALU.bypass, ("kT whole",))
            for c in range(C):
                tt_(qt[:, c, :], acst("sin"), pk("qrot", c)[:, 0:T], M, ("read", "qrot", c))
                tt_(q[:, c, :], q[:, c, :], acst("cos"), M)
                ve.settle()
                tt_(q[:, c, :], q[:, c, :], qt[:, c, :], A_, ("q ready", c))
            eng.wait_ge(in_sems["sink_in"], 32)
            for n in range(NCH):
                W = min(n + 1, 3) * CH if n < 4 else 192
                for b in range(4):
                    cc = slice(2 * b, 2 * b + 2)
                    pb = pk("score", n, b)
                    if n:
                        ve.wait("sink exp", n - 1)
                    op(eng.tensor_reduce(att[:, 0, cc], pb[:, :].rearrange("p (c s) -> p c s", c=2)[:, :, 0:W], AX.X,
                                         ALU.max))
                    ve.settle()
                    stt(att[:, 1, cc], att[:, 0, cc], SCALE, sink[:, cc], M, ALU.max)
                    ve.settle()
                    ts(att[:, 1, cc], att[:, 1, cc], -1.0, None, M, ALU.bypass)
                    ve.settle()
                    tt_(att[:, 4, cc], sink[:, cc], att[:, 1, cc], A_, ("row max", n, b))
                ve.wait("sink exp", n)
                tt_(att[:, 5, :], att[:, 2, :], att[:, 3, :], A_)
                ve.settle()
                op(eng.reciprocal(att[:, 5, :], att[:, 5, :]))
                ve.settle()
                for c in range(C):
                    ts(prob[:, c, 0:W], prob[:, c, 0:W], att[:, 5, c:c + 1], None, M, ALU.bypass, ("prob", n, c))
            for c in range(C):
                pb = pk("ao", c)
                for r, t0, k in SEQS:
                    ts(qt[:, c, t0:t0 + k], pb[:, t0:t0 + k], mod[:, 1, r, 16 + c:17 + c], bog[:, r, c:c + 1], M, A_,
                       ("read", "ao", c))
            ve.settle()
            tt_(x[:, :, :], x[:, :, :], qt[:, :, :], A_, ("x mixed", 1), ("x for", "B1"))
            ve.settle()
            moe(1)
            rms("F")
            ve.settle()
            tt_(E[0][:, :, :], x[:, :, :], bmid(rstd[:, :], C), M)
            ve.settle()
            modulated("F", E[0], E[1], vcol("final_norm_g", 0, C), None, 0, 0)


NAMES = ['x_prompt', 'x_sample', 'state_shift', 'state_wkv', 'cache_k', 'cache_v', 'c_prompt', 'c_sample', 'ada_w',
         'ada_b', 'norm_g', 'rw_mu', 'rw_w_rkv', 'rw_w0', 'rw_w1', 'rw_w2', 'rw_a0', 'rw_a1', 'rw_a2', 'rw_g1',
         'rw_g2', 'rw_k_k', 'rw_k_a', 'rw_r_k', 'rw_lnx_w', 'rw_lnx_b', 'rw_w_o', 'kv_ada_w', 'kv_ada_b', 'kv_norm_g',
         'w_kv', 'b_kv', 'at_w_q', 'at_b_q', 'at_sinks', 'at_w_o', 'at_b_o', 'moe_w_group', 'moe_w_expert',
         'moe_w_gu', 'moe_w_down', 'final_norm_g']
OUTS = [(1, SEQ, D), (1, DEC, D), (1, 1, D), (1, 1, HEADS, HD, HD), (1, 128, NKV, HD), (1, 128, NKV, HD), (1, 1, D),
        (1, 1, HEADS, HD, HD), (1, DEC, NKV, HD), (1, DEC, NKV, HD)]


def kernel(**inputs):
    import concourse.bacc as bacc
    from concourse.bass_utils import run_bass_kernel_spmd as run

    arrays = {n: np.ascontiguousarray(inputs[n]) for n in NAMES}
    arrays.update(constants())

    def program(known):
        nc = bacc.Bacc("TRN2", target_bir_lowering=False, num_devices=1)
        i = {n: nc.dram_tensor(f"in_{n}", a.shape, mybir.dt.from_np(a.dtype), kind="ExternalInput").ap()
             for n, a in arrays.items()}
        o = [nc.dram_tensor(f"out_{k}", s, F32, kind="ExternalOutput").ap() for k, s in enumerate(OUTS)]
        seen = Counts()
        build(nc, i, o, known, seen)
        return nc, seen

    _, counts = program(None)
    nc, _ = program(counts)
    r = run(nc, [{f"in_{n}": a for n, a in arrays.items()}], core_ids=[0])
    return tuple(r.results[0][f"out_{k}"] for k in range(len(OUTS)))
```

```python
from contextlib import ExitStack

import numpy as np

import concourse.bass as bass
from concourse import mybir

F32 = mybir.dt.float32
I32 = mybir.dt.int32
BF16 = mybir.dt.bfloat16
ALU = mybir.AluOpType
ACT = mybir.ActivationFunctionType
AX = mybir.AxisListType

P = 128
D = 1024
C = D // P
SEQ, DEC = 256, 64
T = SEQ + DEC
CH = 64
NCH = T // CH
HD = 64
HEADS = D // HD
NKV = 4
ROPE = HD // 4
PAST = 512
EXP, GROUPS, EPG = 32, 4, 8
FE = D // 4
SLOTS = 64
LW, LA, LG = 64, 64, 160
RMS_EPS = 1e-6
GN_EPS = 64e-5
DECAY = float(np.exp(-0.5))
SCALE = HD ** -0.5
TILES = [(0, 128), (128, 128), (256, 64)]
SEQS = [(0, 0, SEQ), (1, SEQ, DEC)]

VEC_GROUPS = [
    [("c_prompt", 8), ("c_sample", 8), ("norm_g", 32), ("rw_mu", 48), ("rw_w0", 8), ("rw_a0", 8), ("rw_k_k", 8),
     ("rw_k_a", 8)],
    [("ada_b", 96), ("kv_ada_b", 16), ("rw_r_k", 8), ("rw_lnx_w", 8)],
    [("rw_lnx_b", 8), ("kv_norm_g", 8), ("at_b_q", 8), ("at_b_o", 8), ("final_norm_g", 8), ("b_kv", 4),
     ("state_shift", 8)],
]
VCOL = {}
for _g, _rows in enumerate(VEC_GROUPS):
    _o = P * _g
    for _n, _k in _rows:
        VCOL[_n] = _o
        _o += _k

CONST = [("ident", 128), ("ones", 128), ("triu", 128), ("selh", 128), ("iota", 64), ("i64", 64), ("down", 8)]
WKVC = [("maskA", 128), ("lev", 6 * 64), ("lev1n", 64), ("scan", T), ("selb", 1024)]
ATTC = [("cos", T), ("sin", T), ("ropep", 128), ("swap", 128)]


def offsets(table):
    out, o = {}, 0
    for n, k in table:
        out[n] = (o, k)
        o += k
    return out, o


CO, CN = offsets(CONST)
WO, WN = offsets(WKVC)
AO, AN = offsets(ATTC)


def constants():
    p = np.arange(P)
    c = np.zeros((P, CN), np.float32)

    def put(a, off, name, v):
        o, k = off[name]
        a[:v.shape[0], o:o + k] = v

    put(c, CO, "ident", np.eye(P))
    put(c, CO, "ones", np.ones((P, P)))
    put(c, CO, "triu", (p[:, None] <= p[None, :]))
    m = np.arange(P)
    put(c, CO, "selh", ((m % 16)[None, :] == 2 * (m // 16)[None, :] + (p // HD)[:, None]))
    put(c, CO, "down", np.broadcast_to(np.arange(8, 0, -1), (P, 8)))
    put(c, CO, "iota", np.broadcast_to(np.arange(1, 65), (P, 64)))
    put(c, CO, "i64", ((p % 64)[:, None] == np.arange(64)[None, :]))
    w = np.zeros((P, WN), np.float32)
    s, t = (p % 64)[:, None], np.arange(64)[None, :]
    put(w, WO, "maskA", np.concatenate([s < t, s <= t], 1))
    lev = []
    for l in range(1, 7):
        b = 1 << l
        lev.append((s // b == t // b) & (s % b < b // 2) & (t % b >= b // 2))
    put(w, WO, "lev", np.concatenate(lev, 1))
    put(w, WO, "lev1n", (s // 2 == t // 2) & (t % 2 == 0) & (s % 2 == 1))
    put(w, WO, "scan", np.broadcast_to(np.arange(T) % CH != 0, (P, T)))
    q = np.arange(1024)
    put(w, WO, "selb", (np.arange(16)[:, None] == (2 * (q // P) + (q % P) // HD)[None, :]))
    a = np.zeros((P, AN), np.float32)
    half = ROPE // 2
    inv = np.power(np.float32(500000.0), -np.arange(half, dtype=np.float32) * np.float32(2.0 / ROPE)).astype(np.float32)
    pos = np.concatenate([np.arange(SEQ), PAST + np.arange(DEC)]).astype(np.float32)
    ang = (pos[None, :] * inv[:, None]).astype(np.float32)
    d = p % HD
    cos, sin = np.ones((P, T), np.float32), np.zeros((P, T), np.float32)
    cos[d < ROPE] = np.cos(ang)[d[d < ROPE] % half]
    sin[d < ROPE] = np.sin(ang)[d[d < ROPE] % half]
    put(a, AO, "cos", cos)
    put(a, AO, "sin", sin)
    rp = np.zeros((P, P), np.float32)
    for h in (0, HD):
        for j in range(half):
            rp[h + half + j, h + j] = -1.0
            rp[h + j, h + half + j] = 1.0
    put(a, AO, "ropep", rp)
    put(a, AO, "swap", (p[:, None] == (p[None, :] + HD) % P))
    return {"const_all": c, "const_wkv": w, "const_att": a}


MODS = [("ada_w", 0, 1, "ada_b"), ("ada_w", 0, 2, "ada_b"), ("kv_ada_w", None, 0, "kv_ada_b"), ("ada_w", 1, 0, "ada_b"),
        ("ada_w", 1, 1, "ada_b"), ("ada_w", 1, 2, "ada_b")]
MSTEPS = C * len(MODS)
A_STEPS = 4
LEVEL_STEPS = (2, 0, 2, 0, 2)


def steps_of_level(l, j=None):
    first = A_STEPS * NCH + sum(LEVEL_STEPS) * (l - 2)
    if j is None:
        return range(first, first + sum(LEVEL_STEPS))
    first += sum(LEVEL_STEPS[:j])
    return range(first, first + LEVEL_STEPS[j])


def mods_done(steps):
    return [n // C for n in steps if n % C == C - 1 and n < MSTEPS]


def mods_turned(steps):
    return [n // C - 1 for n in steps if n % C == 1 and C < n <= MSTEPS + 1]


class Counts:

    def __init__(self):
        self.at, self.bank = {}, {}


class Engine:

    def __init__(self, eng, name, sems, known, seen):
        self.e, self.name, self.sems, self.known, self.seen = eng, name, sems, known, seen
        self.n, self.waited = 0, {}

    def did(self, ins, *keys):
        ins.then_inc(self.sems[self.name], 1)
        self.n += 1
        for k in keys:
            self.seen.at[k] = (self.name, self.n)

    def wait(self, *key):
        if self.known is None:
            return
        who, n = self.known.at[key]
        if self.waited.get(who, 0) < n:
            self.waited[who] = n
            self.e.wait_ge(self.sems[who], n)

    def settle(self):
        if self.n and self.waited.get(self.name, 0) < self.n:
            self.waited[self.name] = self.n
            self.e.wait_ge(self.sems[self.name], self.n)


class Banks:

    def __init__(self, pe, ps):
        self.pe, self.ps, self.n, self.owner, self.held = pe, ps, 0, [None] * 8, None

    def hold(self, *key):
        self.held = None
        pb = self.open(*key)
        self.held = (self.n - 1) % 8
        return pb

    def open(self, *key):
        if self.n % 8 == self.held:
            self.n += 1
        b = self.n % 8
        self.n += 1
        if self.owner[b] is not None:
            self.pe.wait("read", *self.owner[b])
        self.owner[b] = key
        self.pe.seen.bank[key] = b
        return self.ps[b]


def build(nc, i, o, known, seen):
    ctx = ExitStack()
    with ctx:
        def sb(name, shape, dt=F32):
            return ctx.enter_context(nc.sbuf_tensor(name, shape, dt))

        def sem(name):
            return ctx.enter_context(nc.semaphore(name))

        ps = [ctx.enter_context(nc.psum_tensor(f"bank{b}", [P, 512], F32)) for b in range(8)]
        SLOT = 6144
        B = C * T
        xt_ = sb("x_res", [P, B])
        ring = sb("ring", [P, 4 * SLOT])
        work = sb("work", [P, 8 * B])
        const = sb("const", [P, CN])
        cph = sb("const_phase", [P, max(WN, AN)])
        vec = sb("vec", [P, 3 * P])
        cs = sb("cs", [P, C, 32])
        mod = sb("mod", [P, 2, 2, 48])
        kvmod = sb("kvmod", [P, 2, 16])
        coef2 = sb("coef", [P, 2, 2, C])
        rstd = sb("rstd", [P, T])
        state = sb("state", [P, 2, C, HD])
        dend = sb("dend", [P, C, NCH])
        sink = sb("sink", [P, C])
        att2 = sb("att", [P, 2, 6, C])
        bog = sb("bog", [P, 2, C])
        passes = sb("passes", [P, 4], I32)
        small = sb("small", [P, 16])
        router = sb("router", [P, 2, C, GROUPS + EXP])

        names = ["pe_done", "act_done", "dve_done", "pool_done"]
        sems = {n: sem(n) for n in names}
        ring_in = [sem(f"ring_in{s}") for s in range(4)]
        in_sems = {n: sem(n) for n in ("const_in", "vec_in", "x_in", "wkvc_in", "attc_in", "sink_in", "cache_in",
                                       "swkv_in", "router_in0", "router_in1", "out_written", "modw_in0", "modw_in1")}
        moe_sems = [{n: sem(f"{n}{l}") for n in (
            "gu_in0", "gu_in1", "gu_in2", "gu_in3", "dn_in0", "dn_in1", "dn_in2", "dn_in3",
            "pos_ready", "sel_ready", "selT_made", "selT_ready", "xe_made", "xe_ready",
            "gu_made", "silu_ready", "h_ready", "hT_made", "hT_ready", "down_made", "hi_ready", "rest_ready",
            "mid_ready", "lo_ready0", "lo_ready1", "w_ready",
            "y_made", "y_added")} for l in range(2)]

        def cst(n, rows=P):
            a, k = CO[n]
            return const[0:rows, a:a + k]

        def wcst(n, rows=P):
            a, k = WO[n]
            return cph[0:rows, a:a + k]

        def acst(n):
            a, k = AO[n]
            return cph[:, a:a + k]

        def vcol(n, c, k=1):
            return vec[:, VCOL[n] + c:VCOL[n] + c + k]

        def slot(s, n=SLOT):
            return ring[:, s * SLOT:s * SLOT + n]

        def w512(s):
            return slot(s, 4096).rearrange("p (c n) -> p c n", c=C)

        def buf(t, off=0):
            return t[:, off:off + B].rearrange("p (c t) -> p c t", c=C)

        x = buf(xt_)
        E = [buf(work, B * n) for n in range(8)]
        Fb = [buf(ring, 2 * SLOT + B * n) for n in range(4)]
        G = [buf(ring, B * n) for n in range(4)]
        h0, diff = E[0], E[1]
        MIX = (3, 4, 5, 1, 0, 2)
        xm = [E[3 - MIX.index(n) % 2] for n in range(6)]
        sig, aa, kb, vb, gb, kk, rr, tmp = Fb[0], Fb[1], Fb[2], E[5], E[4], E[6], E[7], Fb[3]
        nrm, bonus, cum, dec = E[0], E[2], E[3], E[1]
        dinv = E[0]
        arb, aak, ark, tt, nt, tmat, wmat, nl = E[0], E[1], E[3], Fb[0], Fb[3], G[0], G[1], G[2]
        ar = work[:, 6 * B:8 * B].rearrange("p (b c t) -> p b c t", b=2, c=C)
        off = [0]

        def wk(n, dt=F32):
            a = off[0]
            off[0] += n
            return work[:, a:a + n] if dt == F32 else work[:, a:a + n].bitcast(dt)

        hT = wk(B).rearrange("p (c t) -> p c t", c=C)
        hpart = wk(3 * 3 * D // 2, BF16).rearrange("p (s j d) -> p s j d", s=3, j=3)
        ysum = wk(B).rearrange("p (c t) -> p c t", c=C)
        htok = work[:, off[0]:off[0] + 3 * D].rearrange("p (j d) -> p j d", j=3)
        xe = wk(2 * C * P).rearrange("p (u c s) -> p u c s", u=2, c=C)
        dpart = wk(3 * D, BF16).rearrange("p (u s d) -> p u s d", u=2, s=3)
        rest = wk(D).rearrange("p (n d) -> p n d", n=2)
        silu = wk(2 * FE).rearrange("p (u f) -> p u f", u=2)
        hid = wk(2 * FE).rearrange("p (u f) -> p u f", u=2)
        hidT = wk(2 * 2 * P).rearrange("p (u f s) -> p u f s", u=2, f=2)
        sel = wk(3 * P, BF16).rearrange("p (u j s) -> p u j s", u=2, j=3)
        selT = wk(T, BF16).rearrange("p (u t) -> p u t", u=2)
        lg = wk(3 * 36).rearrange("p (j n) -> p j n", j=3)
        cw = wk(3 * EXP).rearrange("p (j e) -> p j e", j=3)
        cwpart = wk(3 * 3 * EXP // 2, BF16).rearrange("p (s j e) -> p s j e", s=3, j=3)
        ident16 = wk(P // 2, BF16)
        cwrest = wk(3 * EXP).rearrange("p (j e) -> p j e", j=3)
        wslot = small[:, 10:12]
        msk = wk(3 * EXP).rearrange("p (j e) -> p j e", j=3)
        posn = wk(3 * EXP).rearrange("p (j e) -> p j e", j=3)
        rt = wk(40 * 12).rearrange("p (n k) -> p n k", n=40)
        g48 = wk(3 * 4 * 8).rearrange("p (j g e) -> p j g e", j=3, g=4)
        hkv, haq, q, qt, oT = E[1], E[5], E[6], E[7], E[5]
        kT = work[:, 2 * B:2 * B + 4 * 448].rearrange("p (v t) -> p v t", v=4)
        a3 = 3 * B
        vT = work[:, a3:a3 + 640].rearrange("p (c t) -> p c t", c=2)
        kraw = work[:, a3 + 640:a3 + 1280].rearrange("p (c t) -> p c t", c=2)
        krot = work[:, a3 + 1280:a3 + 1920].rearrange("p (c t) -> p c t", c=2)
        ktok = work[:, a3 + 1920:a3 + 2176]
        v64 = work[0:64, 4 * B:4 * B + 7 * 256].rearrange("p (n d) -> p n d", n=7)
        k64 = work[0:64, 4 * B + 1792:4 * B + 2560].rearrange("p (n d) -> p n d", n=3)
        prob2 = [work[:, a:a + 1536].rearrange("p (c s) -> p c s", c=C) for a in (0, 7 * B)]
        pT = work[0:64, 1536:1536 + 3072].rearrange("p (w c s) -> p w c s", w=3, c=C)
        ytok = work[:, 2 * B:2 * B + 3 * D].rearrange("p (j d) -> p j d", j=3)
        xtok = work[:, 0:3 * D].rearrange("p (j d) -> p j d", j=3)
        rows = work[:, 2 * B:2 * B + 3 * P].rearrange("p (g d) -> p g d", g=3)
        tail1, tail3 = 10240, 22528
        rhs_u = [ring[:, a:a + 1024].rearrange("p (b c k) -> p b c k", b=2, c=C) for a in (tail1, 4096)]
        state2 = ring[:, 5120:SLOT].rearrange("p (r c k) -> p r c k", r=2, c=C)
        swin = ring[:, tail1 + 1024:tail1 + 1536].rearrange("p (c k) -> p c k", c=C)
        shiftT = ring[:, tail1 + 1536:tail1 + 1792]
        mw = [ring[:, 3 * B:3 * B + 2048], ring[:, tail3:tail3 + 2048]]
        modrow = [ring[:, 3 * B + 2048:3 * B + 2560], work[:, 6 * B:6 * B + 512]]
        lows = {"w": ring[0:64, tail3:tail3 + T], "a": ring[0:64, tail3 + T:tail3 + 2 * T],
                "g": ring[:, tail3 + 2 * T:tail3 + 3 * T], "g1": ring[0:32, tail3 + 3 * T:tail3 + 4 * T]}
        head16 = ring[0:16, tail3 + 4 * T:tail3 + 5 * T]
        head16b = ring[0:16, tail3 + 5 * T:tail3 + 6 * T]
        swo = ring[:, 2 * SLOT + 3 * B:2 * SLOT + 3 * B + 1024].rearrange("p (r c k) -> p r c k", r=2, c=C)

        def state_at(j):
            if j == 4:
                return state[:, 1], state2[:, 1]
            return (state, state2)[j % 2][:, 0], (state2, state)[j % 2][:, 0]

        def rhs_of(j):
            return rhs_u[(0, 0, 1, 0, 1)[j]]

        def mod_of(tag):
            if tag == "KV":
                return (lambda r: kvmod[:, r, :]), 0
            return (lambda r: mod[:, int(tag[1]), r, :]), (0 if tag[0] == "A" else 24)

        ACT_CHUNKS = 3

        def sq_buf(tag):
            return E[4] if tag == "B0" else E[7]

        def seen_bank(key):
            return (known or seen).bank.get(key, 0)

        def bc(ap, n):
            return ap.unsqueeze(2).broadcast_to([ap.shape[0], ap.shape[1], n])

        def bmid(ap, n):
            return ap.unsqueeze(1).broadcast_to([ap.shape[0], n, ap.shape[1]])

        ring_plan, ring_at, got = [], {}, [0] * 4

        def plan(name, s, parts):
            got[s] += 16 * parts
            ring_at[name] = (s, got[s])
            ring_plan.append(name)

        for m in range(4):
            plan(("ada", m), m, 1)
        plan(("lora1",), 0, 3)
        plan(("lora2",), 1, 4)
        for n in (1, 0, 2):
            for hf in range(2):
                plan(("rkv", n, hf), hf, 1)
        for hf in range(2):
            plan(("wo", hf), hf, 1)
        plan(("wkv",), 0, 1)
        for hf in range(2):
            plan(("wq", hf), 1 + hf, 1)
        plan(("ao", 0), 3, 1)
        plan(("ao", 1), 2, 1)

        def arrived(en, *name):
            s, n = ring_at[name]
            en.e.wait_ge(ring_in[s], n)
            return s

        def vec_loads(eng, which):
            n = 0
            for g, group in enumerate(VEC_GROUPS):
                r = 0
                for name, k in group:
                    letters = " ".join("abcdef"[:len(i[name].shape)])
                    src = i[name].rearrange(f"{letters} -> ({letters})").rearrange("(r d) -> r d", d=P)
                    if n % 2 == which:
                        eng.dma_start(rows[r:r + k, g, :], src).then_inc(in_sems["vec_in"], 16)
                    r += k
                    n += 1

        block = ctx.enter_context(nc.Block())

        @block.sync
        def _(eng):
            sp = Engine(eng, "sp", sems, known, seen)
            mine = {}

            def load(name, pairs):
                s, _n = ring_at[name]
                if mine.get(s) is not None:
                    sp.wait("used", *mine[s])
                mine[s] = name
                for dst, src in pairs:
                    eng.dma_start(dst, src).then_inc(ring_in[s], 16)

            def half(name, w, hf):
                s, _n = ring_at[name]
                load(name, [(w512(s), w[:, 512 * hf:512 * (hf + 1)].rearrange("(c p) n -> p c n", p=P))])

            def moe_gu(l, s, e):
                eng.dma_start(slot(s, 4096).rearrange("p (c n) -> p c n", c=C),
                              i["moe_w_gu"][l, bass.ds(e, 1)].rearrange("a (c p) n -> p (a c) n", p=P)
                              ).then_inc(moe_sems[l][f"gu_in{s}"], 16)

            def moe_dn(l, s, e):
                eng.dma_start(ring[:, s * SLOT + 4096:(s + 1) * SLOT].rearrange("p (f n) -> p f n", f=2),
                              i["moe_w_down"][l, bass.ds(e, 1)].rearrange("a (f p) n -> p (a f) n", p=P)
                              ).then_inc(moe_sems[l][f"dn_in{s}"], 16)

            def moe_loads(l):
                S = moe_sems[l]
                if l == 0:
                    sp.wait("y all")
                    eng.wait_ge(in_sems["out_written"], 64)
                    moe_gu(l, 2, 2)
                    moe_dn(l, 2, 2)
                    moe_gu(l, 3, 3)
                    sp.wait("y rstd all", C - 1)
                    moe_dn(l, 3, 3)
                for s in ((0, 1) if l == 0 else (0, 1, 3, 2)):
                    if mine.get(s) is not None:
                        sp.wait("used", *mine[s])
                    moe_gu(l, s, s)
                    moe_dn(l, s, s)
                for s in range(4):
                    mine[s] = None

                def again(gu, dn, e):
                    for u in range(2):
                        eng.wait_ge(S["gu_made"], gu + u)
                        for v in range(2):
                            moe_gu(l, 2 * u + v, e + 2 * u + v)
                    for u in range(2):
                        eng.wait_ge(S["down_made"], dn + 2 * u)
                        for v in range(2):
                            moe_dn(l, 2 * u + v, e + 2 * u + v)

                with eng.Fori(0, EXP // 4 - 1) as k:
                    again(2 * k + 1, 4 * k + 2, 4 * k + 4)
                sp.wait("passes", l)
                extra = eng.value_load(passes[0:1, 2 * l + 1:2 * l + 2], min_val=0, max_val=4)
                with eng.If(extra > 0):
                    with eng.Fori(0, extra) as p:
                        with eng.Fori(0, EXP // 4) as k:
                            again(16 * p + 2 * k + 15, 32 * p + 4 * k + 30, 4 * k)
                return extra

            sp.wait("rows zeroed")
            vec_loads(eng, 0)
            for m in range(4):
                load(("ada", m), [(w512(m).rearrange("p (c k) n -> p c (k n)", c=2),
                                   i["ada_w"][0, 2 * m * P:(2 * m + 2) * P, 0:2048]
                                   .rearrange("(c p) n -> p c n", p=P))])
            load(("lora1",), [
                (slot(0, 512).rearrange("p (c n) -> p c n", c=C), i["rw_w1"][0].rearrange("(c p) n -> p c n", p=P)),
                (ring[:, 512:1024].rearrange("p (c n) -> p c n", c=C),
                 i["rw_a1"][0].rearrange("(c p) n -> p c n", p=P)),
                (ring[:, 1024:1024 + C * LG].rearrange("p (c n) -> p c n", c=C),
                 i["rw_g1"][0].rearrange("(c p) n -> p c n", p=P))])
            load(("lora2",), [
                (ring[0:64, SLOT:SLOT + 1024], i["rw_w2"][0]), (ring[0:64, SLOT + 1024:SLOT + 2048], i["rw_a2"][0]),
                (ring[:, SLOT + 2048:SLOT + 3072], i["rw_g2"][0, 0:P]),
                (ring[0:32, SLOT + 3072:SLOT + 4096], i["rw_g2"][0, P:LG])])
            for n in (1, 0, 2):
                for hf in range(2):
                    half(("rkv", n, hf), i["rw_w_rkv"][0, n], hf)
            for n in range(MSTEPS):
                w, l, blk, _b = MODS[n // C]
                src = i[w] if l is None else i[w][l]
                if n >= 2:
                    sp.wait("mod used", n - 2)
                elif n == 1:
                    sp.wait("bonus all", C - 1)
                else:
                    sp.wait("used", "rkv", 2, 1)
                eng.dma_start(mw[n % 2], src[P * (n % C):P * (n % C) + P, 2048 * blk:2048 * (blk + 1)]
                              ).then_inc(in_sems[f"modw_in{n % 2}"], 16)
            sp.wait("mod used", MSTEPS - 1)
            sp.wait("modT", len(MODS) - 1)
            sp.wait("inverses")
            for hf in range(2):
                half(("wo", hf), i["rw_w_o"][0], hf)
            extra = moe_loads(0)
            for name, w, hf, n in ((("wkv",), i["w_kv"], 0, 30), (("wq", 0), i["at_w_q"][0], 0, 30),
                                   (("wq", 1), i["at_w_q"][0], 1, 32), (("ao", 0), i["at_w_o"][0], 0, 32)):
                eng.wait_ge(moe_sems[0]["down_made"], 32 * extra + n)
                half(name, w, hf)
            half(("ao", 1), i["at_w_o"][0], 1)
            moe_loads(1)

        @block.gpsimd
        def _(eng):
            pl = Engine(eng, "pool_done", sems, known, seen)
            outs = [0]

            def put(dst, src):
                eng.dma_start(dst, src).then_inc(in_sems["out_written"], 16)
                outs[0] += 16

            pl.did(eng.memset(rows[:, 2, :], 0.0), ("rows zeroed",))
            eng.dma_start(const[:, :], i["const_all"]).then_inc(in_sems["const_in"], 16)
            for j in range(2):
                eng.dma_start(xtok[:, j, :], i["x_prompt"][0, j * P:(j + 1) * P]).then_inc(in_sems["x_in"], 16)
            eng.dma_start(xtok[0:64, 2, :], i["x_sample"][0]).then_inc(in_sems["x_in"], 16)
            eng.dma_start(cph[:, 0:WN], i["const_wkv"]).then_inc(in_sems["wkvc_in"], 16)
            for h in range(2):
                eng.dma_start(sink[64 * h:64 * h + 64, :],
                              i["at_sinks"][0].rearrange("(c h) -> h c", h=2)[h:h + 1, :].broadcast_to([64, C]),
                              allow_slow_non_contiguous=True).then_inc(in_sems["sink_in"], 16)

            def load_router(l):
                eng.dma_start(router[:, l, :, 0:GROUPS], i["moe_w_group"][l].rearrange("(c p) n -> p c n", p=P)
                              ).then_inc(in_sems[f"router_in{l}"], 16)
                eng.dma_start(router[:, l, :, GROUPS:], i["moe_w_expert"][l].rearrange("(c p) n -> p c n", p=P)
                              ).then_inc(in_sems[f"router_in{l}"], 16)

            for l in range(2):
                load_router(l)

            def split_rows(l):
                for j, (t0, k) in enumerate(TILES):
                    for hf in range(2):
                        cols = slice(512 * hf, 512 * hf + 512)
                        pl.wait("htok ready", l, j, hf)
                        pl.did(eng.tensor_tensor(htok[0:k, j, cols], htok[0:k, j, cols], hpart[0:k, 0, j, cols],
                                                 ALU.subtract), ("rest", l, j))

            def low_parts(l):
                S = moe_sems[l]
                pl.wait("passes", l)
                nb = eng.value_load(passes[0:1, 2 * l:2 * l + 1], min_val=1, max_val=5)
                with eng.Fori(0, nb) as p:
                    with eng.Fori(0, EXP // 4) as k_:
                        k = 8 * p + k_
                        for n in range(2):
                            cols = slice(512 * n, 512 * n + 512)
                            eng.wait_ge(S["mid_ready"], 4 * k + n + 1)
                            eng.tensor_tensor(dpart[:, 0, 2, cols], rest[:, n, :], dpart[:, 0, 1, cols],
                                              ALU.subtract).then_inc(S["lo_ready0"], 1)

            pl.wait("shift row")
            put(o[2][0, 0].rearrange("(c p) -> c p", p=P), shiftT[0:C, 0:P])
            put(o[6][0, 0].rearrange("(c p) -> c p", p=P), shiftT[0:C, P:2 * P])
            pl.wait("wkv ready")
            eng.dma_start(swin, i["state_wkv"][0, 0].rearrange("(c h) v k -> (h v) c k", h=2)
                          ).then_inc(in_sems["swkv_in"], 16)
            for r, n_out in ((0, 3), (1, 7)):
                pl.wait("swout ready", r)
                put(o[n_out][0, 0].rearrange("(c h) v k -> (h v) c k", h=2), swo[:, r])
            eng.dma_start(cph[:, 0:AN], i["const_att"]).then_inc(in_sems["attc_in"], 16)
            split_rows(0)
            low_parts(0)
            pl.wait("x moe", 0)
            eng.dma_start(ktok, i["cache_k"][0].rearrange("t n d -> t (n d)")).then_inc(in_sems["cache_in"], 16)
            eng.dma_start(v64[:, 4:6, :], i["cache_v"][0].rearrange("(w t) n d -> t w (n d)", w=2)
                          ).then_inc(in_sems["cache_in"], 16)
            pl.wait("k64")
            for r, (n_out, w) in enumerate(((4, 0), (4, 1), (8, 2))):
                t0 = 64 * w if n_out == 4 else 0
                put(o[n_out][0, t0:t0 + 64].rearrange("t n d -> t (n d)"), k64[:, w, :])
            pl.wait("v64")
            for n_out, w, t0 in ((5, 2, 0), (5, 3, 64), (9, 6, 0)):
                put(o[n_out][0, t0:t0 + 64].rearrange("t n d -> t (n d)"), v64[:, w, :])
            split_rows(1)
            low_parts(1)
            for j in range(3):
                pl.wait("ytok", j)
                if j < 2:
                    put(o[0][0, j * P:(j + 1) * P], ytok[:, j, :])
                else:
                    put(o[1][0], ytok[0:64, 2, :])
            eng.wait_ge(in_sems["out_written"], outs[0])

        @block.tensor
        def _(eng):
            pe = Engine(eng, "pe_done", sems, known, seen)
            bank = Banks(pe, ps)
            ident = cst("ident")

            def mm(out, l, r, start, stop, **kw):
                return eng.matmul(out, l, r, start=start, stop=stop, **kw)

            def full(ins, *key):
                pe.did(ins, key)

            def mod_rows(pb, c, w):
                for n in range(4):
                    ins = mm(pb[32 * n:32 * n + 32, :], cs[:, c, :], w[:, 512 * n:512 * n + 512], c == 0, c == C - 1,
                             tile_position=(0, 32 * n))
                return ins

            def mod_turn(g):
                pe.wait("mod rows", g)
                pb = bank.open("modT", g)
                for qd in range(4):
                    cols = slice(P * qd, P * qd + P)
                    ins = eng.transpose(pb[:, cols], modrow[g < 0][:, cols], ident)
                full(ins, "modT", g)

            def mod_step(n):
                for g in mods_turned([n]):
                    mod_turn(g)
                if n < MSTEPS:
                    g, c = divmod(n, C)
                    if c == 0:
                        bank.hold("mod", g)
                    eng.wait_ge(in_sems[f"modw_in{n % 2}"], 16 * (n // 2 + 1))
                    pe.did(mod_rows(ps[seen_bank(("mod", g))], c, mw[n % 2]), ("mod used", n), ("mod", g))
                elif n == MSTEPS:
                    bank.held = None

            def mean_square(tag):
                pb = bank.open("ms", tag)
                for c in range(C):
                    if c % 2 == 0:
                        pe.wait("squares", tag, c // 2)
                    ins = mm(pb[:, 0:T], cst("ones"), sq_buf(tag)[:, c, :], c == 0, c == C - 1)
                full(ins, "ms", tag)

            def project(tag, outs, src, wname, ready=None):
                for m in outs:
                    s = arrived(pe, *wname(m // 4))
                    pb = bank.open(tag, m)
                    for c in range(C):
                        if ready:
                            pe.wait(*ready, c)
                        ins = mm(pb[:, 0:T], w512(s)[:, c, 128 * (m % 4):128 * (m % 4) + 128], src[:, c, :], c == 0,
                                 c == C - 1)
                    keys = [(tag, m)]
                    if m % 4 == 3:
                        keys.append(("used",) + wname(m // 4))
                    pe.did(ins, *keys)

            def head_sums(tag, src, ready=None):
                pb = bank.open(tag, 0)
                for c in range(C):
                    if ready:
                        pe.wait(ready, c)
                    ins = mm(pb[0:16, 0:T], cst("selh")[:, 16 * c:16 * c + 16], src[:, c, :], c == 0, c == C - 1)
                full(ins, tag, 0)

            def head_spread(tag, src16):
                for c in range(C):
                    pb = bank.open(tag, c)
                    full(mm(pb[:, 0:T], wcst("selb", 16)[:, P * c:P * (c + 1)], src16, True, True), tag, c)

            eng.wait_ge(in_sems["const_in"], 16)
            eng.wait_ge(in_sems["vec_in"], 16 * sum(len(g) for g in VEC_GROUPS))
            pb = bank.open("vec")
            for g in range(3):
                ins = eng.transpose(pb[:, P * g:P * (g + 1)], rows[:, g, :], ident)
            full(ins, "vec")
            eng.wait_ge(in_sems["x_in"], 48)
            for c in range(C):
                pb = bank.open("xT", c)
                for j, (t0, k) in enumerate(TILES):
                    ins = eng.transpose(pb[:, t0:t0 + k], xtok[0:k, j, P * c:P * (c + 1)], ident[0:k, 0:k])
                full(ins, "xT", c)
            pe.wait("cs")
            mean_square("A0")
            pb = bank.open("mod", -1)
            for m in range(4):
                s = arrived(pe, "ada", m)
                for c in range(2):
                    ins = mod_rows(pb, 2 * m + c, slot(s, 4096)[:, 2048 * c:2048 * c + 2048])
                pe.did(ins, ("used", "ada", m), ("mod", -1))
            mod_turn(-1)

            pe.wait("h", "A0", C - 1 - ACT_CHUNKS)
            pe.wait("h", "A0", C - 1)
            pb = bank.open("shift")
            ins = eng.transpose(pb[0:C, 0:128], h0[:, :, SEQ - 1], ident)
            ins = eng.transpose(pb[0:C, 128:256], h0[:, :, T - 1], ident)
            full(ins, "shift")
            s = arrived(pe, "lora1")
            for n, (key, a, k) in enumerate((("w", 0, LW), ("a", 512, LA), ("g", 1024, LG))):
                w = ring[:, a:a + C * k].rearrange("p (c n) -> p c n", c=C)
                parts = [(0, k)] if k <= 128 else [(0, 128), (128, k - 128)]
                for m, (c0, kk_) in enumerate(parts):
                    pb = bank.open("low", key, m)
                    for c in range(C):
                        pe.wait("xm", 3 + n, c)
                        ins = mm(pb[0:kk_, 0:T], w[:, c, c0:c0 + kk_], xm[3 + n][:, c, :], c == 0, c == C - 1)
                    pe.did(ins, ("low", key, m), ("xm used", 3 + n))
            seen.at[("used", "lora1")] = seen.at[("low", "g", 1)]
            s = arrived(pe, "lora2")
            w2 = ring[0:64, SLOT:SLOT + 1024]
            a2 = ring[0:64, SLOT + 1024:SLOT + 2048]
            g2a = ring[:, SLOT + 2048:SLOT + 3072]
            g2b = ring[0:32, SLOT + 3072:SLOT + 4096]
            for key, w in (("w", w2), ("a", a2)):
                pe.wait("low ready", key, 0)
                for c in range(C):
                    pb = bank.open("up", key, c)
                    full(mm(pb[:, 0:T], w[:, P * c:P * (c + 1)], lows[key], True, True), "up", key, c)
            pe.wait("low ready", "g", 1)
            for c in range(C):
                pb = bank.open("up", "g", c)
                mm(pb[:, 0:T], g2a[:, P * c:P * (c + 1)], lows["g"], True, False)
                ins = mm(pb[:, 0:T], g2b[:, P * c:P * (c + 1)], lows["g1"], False, True)
                pe.did(ins, ("up", "g", c), ("used", "lora2"))
            for n in (1, 0):
                project(("rkv", n), range(C), xm[n], lambda hf, n=n: ("rkv", n, hf), ("xm", n))
                seen.at[("xm used", n)] = (pe.name, pe.n)
            pe.wait("kk squares")
            head_sums("kk sum", nrm)
            project(("rkv", 2), range(4), xm[2], lambda hf: ("rkv", 2, hf), ("xm", 2))
            pe.wait("kk rstd")
            head_spread("kk rstd all", head16)
            pe.wait("rk")
            head_sums("bonus sum", tmp)
            project(("rkv", 2), range(4, C), xm[2], lambda hf: ("rkv", 2, hf))
            seen.at[("xm used", 2)] = (pe.name, pe.n)
            pe.wait("bonus 16")
            head_spread("bonus all", head16b)
            pe.wait("wkv ready")
            i64 = cst("i64")

            def per_head(pb, cols, terms, c, last=True):
                for h in range(2):
                    r = slice(64 * h, 64 * h + 64)
                    for k, (l, m) in enumerate(terms):
                        ins = mm(pb[r, cols], l[r], m[r], k == 0, k == len(terms) - 1)
                return ins

            for j in range(NCH):
                t = slice(CH * j, CH * (j + 1))
                for nm, st in (("b", aa), ("k", kb)):
                    for hf in range(2):
                        pb = bank.open("A" + nm, j, hf)
                        for cc in range(4):
                            c = 4 * hf + cc
                            for h in range(2):
                                r = slice(64 * h, 64 * h + 64)
                                ins = mm(pb[r, P * cc:P * cc + P].rearrange("p (b t) -> p b t", b=2), st[r, c, t],
                                         ar[r, :, c, t], True, True)
                        full(ins, "A" + nm, j, hf)
                for n in range(A_STEPS * j, A_STEPS * j + A_STEPS // 2):
                    mod_step(n)
                pb = bank.open("N1", j)
                for c in range(C):
                    ins = per_head(pb, slice(64 * c, 64 * c + 64), [(kk[:, c, t], aa[:, c, t])], c)
                full(ins, "N1", j)
                for nm, st in (("v", vb), ("b", aa), ("k", kb)):
                    pb = bank.open("tok" + nm, j)
                    for c in range(C):
                        ins = per_head(pb, slice(64 * c, 64 * c + 64), [(st[:, c, t], i64)], c)
                    full(ins, "tok" + nm, j)
                for n in range(A_STEPS * j + A_STEPS // 2, A_STEPS * (j + 1)):
                    mod_step(n)
            for l in range(2, 7):
                for j in range(NCH):
                    t = slice(CH * j, CH * (j + 1))
                    pe.wait("level", l, j)
                    pb = bank.open("W", l, j)
                    for c in range(C):
                        ins = per_head(pb, slice(64 * c, 64 * c + 64), [(nl[:, c, t], tmat[:, c, t])], c)
                    full(ins, "W", l, j)
                for j in range(NCH):
                    t = slice(CH * j, CH * (j + 1))
                    pe.wait("W ready", l, j)
                    pb = bank.open("TT", l, j)
                    for c in range(C):
                        ins = per_head(pb, slice(64 * c, 64 * c + 64), [(wmat[:, c, t], tt[:, c, t])], c)
                    full(ins, "TT", l, j)
                    if l < 6:
                        pb = bank.open("TW", l, j)
                        for c in range(C):
                            ins = per_head(pb, slice(64 * c, 64 * c + 64), [(tt[:, c, t], wmat[:, c, t])], c)
                        full(ins, "TW", l, j)
                    for n in steps_of_level(l, j):
                        mod_step(n)
            eng.wait_ge(in_sems["swkv_in"], 16)
            pb = bank.open("s0")
            for c in range(C):
                ins = per_head(pb, slice(64 * c, 64 * c + 64), [(swin[:, c, :], i64)], c)
            full(ins, "s0")

            def heads8(name, j, cc, terms):
                pb = bank.open(name, j)
                for c in cc:
                    ins = per_head(pb, slice(64 * c, 64 * c + 64), terms(c), c)
                full(ins, name, j)

            def tk(j):
                return slice(CH * j, CH * (j + 1))

            def state_rhs(j):
                pe.wait("state", j)
                pe.wait("T ready", j)
                heads8("RHS", j, range(C), lambda c: [(kk[:, c, tk(j)], state_at(j)[0][:, c, :]),
                                                      (aak[:, c, tk(j)], vb[:, c, tk(j)])])

            def state_u(j):
                pe.wait("RHS ready", j)
                heads8("U", j, range(C), lambda c: [(tt[:, c, tk(j)], rhs_of(j)[:, 0, c, :])])

            def state_s(j):
                pe.wait("U ready", j)
                heads8("S", j, range(C), lambda c: [(aa[:, c, tk(j)], rhs_of(j)[:, 1, c, :]),
                                                    (kb[:, c, tk(j)], vb[:, c, tk(j)])])

            def state_y(j, hf):
                heads8(("Y", hf), j, range(4 * hf, 4 * hf + 4),
                       lambda c: [(state_at(j)[0][:, c, :], rr[:, c, tk(j)]), (rhs_of(j)[:, 1, c, :], arb[:, c, tk(j)]),
                                  (vb[:, c, tk(j)], ark[:, c, tk(j)])])

            state_rhs(0)
            state_rhs(4)
            state_u(0)
            state_u(4)
            state_s(0)
            state_y(0, 0)
            state_y(0, 1)
            state_s(4)
            for j, before in ((1, 4), (2, 1), (3, 2)):
                state_rhs(j)
                state_y(before, 0)
                state_u(j)
                state_y(before, 1)
                state_s(j)
            state_y(3, 0)
            state_y(3, 1)
            for r_ in range(2):
                pe.wait("final state", r_)
                pb = bank.open("sout", r_)
                for c in range(C):
                    ins = per_head(pb, slice(64 * c, 64 * c + 64), [((state, state2)[r_][:, r_, c, :], i64)], c)
                full(ins, "sout", r_)
            pe.wait("y all")
            head_sums("y sum", rr)
            pe.wait("y mean")
            head_spread("y mean all", head16)
            head_sums("yc sum", E[0], "yc squares")
            pe.wait("y rstd")
            head_spread("y rstd all", head16)
            project("wo", range(C), rr, lambda hf: ("wo", hf), ("mix out",))

            def moe(l):
                S = moe_sems[l]
                mean_square(f"B{l}")
                eng.wait_ge(in_sems[f"router_in{l}"], 32)
                pb = [bank.open("logits", l, j) for j in range(3)]
                for c in range(C):
                    pe.wait("h", f"B{l}", c)
                    for j, (t0, k) in enumerate(TILES):
                        ins = mm(pb[j][0:k, 0:36], hT[:, c, t0:t0 + k], router[:, l, c, :], c == 0,
                                 c == C - 1)
                pe.did(ins, *[("logits", l, j) for j in range(3)])
                for j, (t0, k) in enumerate(TILES):
                    for hf in range(2):
                        pb = bank.open("htok", l, j, hf)
                        for cc in range(4):
                            ins = eng.transpose(pb[0:k, P * cc:P * cc + P], hT[:, 4 * hf + cc, t0:t0 + k], ident)
                        full(ins, "htok", l, j, hf)
                pe.wait("mask", l)
                pb = bank.open("rank", l)
                for j in range(3):
                    for jj in range(j + 1):
                        ins = mm(pb[:, EXP * j:EXP * j + EXP], cst("triu") if jj == j else cst("ones"),
                                 msk[:, jj, :], jj == 0, jj == j)
                for jj in range(3):
                    ins = mm(pb[:, 96:96 + EXP], cst("ones"), msk[:, jj, :], jj == 0, jj == 2)
                full(ins, "rank", l)
                pe.wait("parts", l)
                pe.wait("passes", l)
                for b in range(8):
                    if bank.owner[b] is not None:
                        pe.wait("read", *bank.owner[b])
                nb = eng.value_load(passes[0:1, 2 * l:2 * l + 1], min_val=1, max_val=5)

                def gather(k, u):
                    eng.wait_ge(S["sel_ready"], 2 * k + u + 1)
                    for hf in range(2):
                        if u == 1:
                            eng.wait_ge(S["xe_ready"], 4 * k + hf + 1)
                        for cc in range(4):
                            c = 4 * hf + cc
                            for j, (t0, kt) in enumerate(TILES):
                                for n in range(3):
                                    ins = mm(ps[1 + hf][:, P * cc:P * cc + P], hpart[0:kt, n, j, P * c:P * c + P],
                                             sel[0:kt, u, j, :], j == 0 and n == 0, j == 2 and n == 2)
                        ins.then_inc(S["xe_made"], 1)

                def hid_turn(k, u):
                    eng.wait_ge(S["h_ready"], 2 * k + u + 1)
                    if u == 0:
                        eng.wait_ge(S["y_added"], 8 * k + 1)
                    else:
                        eng.wait_ge(S["hT_ready"], 2 * k + 1)
                    for f in range(2):
                        ins = eng.transpose(ps[0][:, P * f:P * f + P], hid[:, u, P * f:P * f + P], ident)
                    ins.then_inc(S["hT_made"], 1)

                def down(k, u):
                    eng.wait_ge(S["hT_ready"], 2 * k + u + 1)
                    for v in range(2):
                        eng.wait_ge(S[f"dn_in{2 * u + v}"], 16 * k + 16)
                    for n in range(2):
                        if u == 1:
                            eng.wait_ge(S["rest_ready"], 4 * k + n + 1)
                        for f in range(2):
                            for v in range(2):
                                s = 2 * u + v
                                w = ring[:, s * SLOT + 4096:(s + 1) * SLOT]
                                ins = mm(ps[4 + n][64 * v:64 * v + 64, :], hidT[:, u, f, 64 * v:64 * v + 64],
                                         w[:, D * f + 512 * n:D * f + 512 * n + 512], f == 0, f == 1)
                        ins.then_inc(S["down_made"], 1)

                def experts(k, e, ahead):
                    for u in range(2):
                        eng.wait_ge(S["xe_ready"], 4 * k + 3 + u)
                        for j, (t0, kt) in enumerate(TILES):
                            mm(ps[1 + u][:, t0:t0 + kt], sel[0:kt, u, j, :], ident16[0:kt, 0:kt], True, True)
                        for j, (t0, kt) in enumerate(TILES):
                            ins = mm(ps[1 + u][:, T:T + 6].rearrange("p (s v) -> p s v", s=3), sel[0:kt, u, j, :],
                                     cwpart[0:kt, :, j, bass.ds(e + 2 * u, 2)], j == 0, j == 2)
                        ins.then_inc(S["selT_made"], 1)
                    for u in range(2):
                        for v in range(2):
                            eng.wait_ge(S[f"gu_in{2 * u + v}"], 16 * k + 16)
                        if u == 0:
                            eng.wait_ge(S["y_added"], 8 * k)
                        for c in range(C):
                            for v in range(2):
                                ins = mm(ps[3 + 4 * u][64 * v:64 * v + 64, :], xe[:, u, c, 64 * v:64 * v + 64],
                                         w512(2 * u + v)[:, c, :], c == 0, c == C - 1)
                        ins.then_inc(S["gu_made"], 1)
                    hid_turn(k, 0)
                    eng.wait_ge(S["selT_ready"], 2 * k + 2)
                    if ahead:
                        gather(k + 1, 0)
                    hid_turn(k, 1)
                    down(k, 0)
                    down(k, 1)
                    if ahead:
                        gather(k + 1, 1)
                    eng.wait_ge(S["hT_ready"], 2 * k + 2)
                    for c in range(C):
                        pb = ps[(6, 7, 3, 0)[c % 4]]
                        if c % 4 == 0:
                            for u in range(2):
                                eng.wait_ge(S[f"lo_ready{u}"], 2 * k + 1 + c // 4)
                        if c >= 4:
                            eng.wait_ge(S["y_added"], 8 * k + c - 2)
                        for u in range(2):
                            for n in range(3):
                                ins = mm(pb[:, 0:T], dpart[:, u, n, P * c:P * c + P], selT[:, u, :],
                                         u == 0 and n == 0, u == 1 and n == 2)
                        ins.then_inc(S["y_made"], 1)

                with eng.Fori(0, nb) as p:
                    for u in range(2):
                        gather(8 * p, u)
                    with eng.Fori(0, EXP // 4 - 1) as k_:
                        experts(8 * p + k_, 4 * k_, True)
                    experts(8 * p + 7, EXP - 4, False)
                pe.wait("x moe", l)

            moe(0)

            mean_square("A1")
            project("kv", range(4), hkv, lambda hf: ("wkv",), ("h", "KV"))
            eng.wait_ge(in_sems["attc_in"], 16)
            for c in range(2):
                pe.wait("kraw", c)
                pb = bank.open("krot", c)
                full(mm(pb[:, 0:T], acst("ropep"), kraw[:, c, :], True, True), "krot", c)
            eng.wait_ge(in_sems["cache_in"], 32)
            pb = bank.open("kcache")
            for c in range(2):
                ins = eng.transpose(pb[:, P * c:P * c + P], ktok[:, P * c:P * c + P], ident)
            full(ins, "kcache")
            pe.wait("kT whole")
            for c in range(2):
                pb = bank.open("kswap", c)
                full(mm(pb[:, 0:448], acst("swap"), kT[:, c, :], True, True), "kswap", c)
            pe.wait("vT", 1)
            for w, t0 in enumerate((0, 64, 128, 192, 256)):
                pb = bank.open("v64", w)
                for c in range(2):
                    ins = eng.transpose(pb[0:64, P * c:P * c + P], vT[:, c, t0:t0 + 64], ident)
                full(ins, "v64", w)
            for w, t0 in enumerate((128, 192, 384)):
                pb = bank.open("k64", w)
                for c in range(2):
                    ins = eng.transpose(pb[0:64, P * c:P * c + P], kT[:, c, t0:t0 + 64], ident)
                full(ins, "k64", w)

            def q_turn(c):
                pe.wait("qraw", c)
                pb = bank.open("qrot", c)
                full(mm(pb[:, 0:T], acst("ropep"), q[:, c, :], True, True), "qrot", c)

            for c in range(C):
                project("q", [c], haq, lambda hf: ("wq", hf), ("h", "A1"))
                if c:
                    q_turn(c - 1)
            q_turn(C - 1)
            pe.wait("kswapped", 1)

            def scores(n):
                t0 = CH * n
                lo, hi = (max(0, n - 2) * CH, (n + 1) * CH) if n < 4 else (256, 448)
                for b in range(4):
                    pe.wait("q ready", 2 * b + 1)
                    pb = bank.open("score", n, b)
                    for cc in range(2):
                        c = 2 * b + cc
                        g = c // 2
                        for h in range(2):
                            var = 0 if g % 2 == h else 2
                            r = slice(64 * h, 64 * h + 64)
                            ins = mm(pb[r, 256 * cc:256 * cc + hi - lo], q[r, c, t0:t0 + CH],
                                     kT[r, var + g // 2, lo:hi], True, True)
                    full(ins, "score", n, b)

            def attended(n):
                prob = prob2[n % 2]
                parts = min(n + 1, 3) if n < 4 else 3
                for w in range(parts):
                    for hf in range(2):
                        pe.wait("prob", n, 4 * hf + 3)
                        pb = bank.open("pT", n, w, hf)
                        for cc in range(4):
                            ins = eng.transpose(pb[0:64, P * cc:P * cc + P], prob[:, 4 * hf + cc, CH * w:CH * w + CH],
                                                ident)
                        full(ins, "pT", n, w, hf)
                pe.wait("v64")
                pe.wait("pT ready", n)
                pb = bank.open("o", n)
                first = max(0, n - 2) if n < 4 else 4
                for g in range(NKV):
                    for h in range(2):
                        for w in range(parts):
                            ins = mm(pb[64 * h:64 * h + 64, P * g:P * g + P].rearrange("p (c s) -> p c s", c=2),
                                     v64[:, first + w, 64 * g:64 * g + 64],
                                     pT[:, w, 2 * g:2 * g + 2, 64 * h:64 * h + 64], w == 0, w == parts - 1)
                full(ins, "o", n)

            scores(0)
            for n in range(NCH):
                if n + 1 < NCH:
                    scores(n + 1)
                attended(n)
            pe.wait("oT", NCH - 1)
            project("ao", range(C), oT, lambda hf: ("ao", hf))
            moe(1)
            mean_square("F")
            pe.wait("h", "F")
            for j, (t0, k) in enumerate(TILES):
                for hf in range(2):
                    pb = bank.open("ytok", j, hf)
                    for cc in range(4):
                        ins = eng.transpose(pb[0:k, P * cc:P * cc + P], E[1][:, 4 * hf + cc, t0:t0 + k], ident)
                    full(ins, "ytok", j, hf)

        @block.scalar
        def _(eng):
            ac = Engine(eng, "act_done", sems, known, seen)

            def pk(*key):
                ac.wait(*key)
                return ps[seen_bank(key)]

            def act(out, in_, f, *keys, **kw):
                ac.did(eng.activation(out, in_, f, **kw), *keys)

            def squares(tag):
                for b in range(4):
                    ac.wait("x for", tag, b)
                    act(sq_buf(tag)[:, 2 * b:2 * b + 2, :], x[:, 2 * b:2 * b + 2, :], ACT.Square,
                        ("squares", tag, b))

            def root(tag):
                ac.wait("ms ready", tag)
                act(rstd[:, :], rstd[:, :], ACT.Sqrt, ("root", tag))

            def mod_copy(steps):
                for g in mods_done(steps):
                    pb = pk("mod", g)
                    ac.wait("modT", g - 1)
                    act(modrow[0], pb[:, :], ACT.Copy, ("read", "mod", g), ("mod rows", g))

            ac.wait("rows zeroed")
            vec_loads(eng, 1)
            def modulated(tag, src, dst):
                md, sh = mod_of(tag)
                ac.wait("coef", tag)
                ac.wait("normed", tag, C - ACT_CHUNKS)
                for c in range(C - ACT_CHUNKS, C):
                    for r, t0, k in SEQS:
                        act(dst[:, c, t0:t0 + k], src[:, c, t0:t0 + k], ACT.Identity, ("h", tag, c),
                            scale=coef2[:, 0, r, c:c + 1], bias=md(r)[:, sh + c:sh + c + 1])

            ac.wait("vec ready")
            act(small[:, 0:16], vcol("c_prompt", 0, 16), ACT.Silu, ("silu c",))
            squares("A0")
            root("A0")
            act(modrow[1], pk("mod", -1)[:, :], ACT.Copy, ("read", "mod", -1), ("mod rows", -1))
            modulated("A0", h0, h0)
            pb = pk("shift")
            act(shiftT[0:C, :], pb[0:C, 0:256], ACT.Copy, ("read", "shift"), ("shift row",))
            act(lows["w"], pk("low", "w", 0)[0:64, 0:T], ACT.Tanh, ("read", "low", "w", 0), ("low ready", "w", 0))
            act(lows["a"], pk("low", "a", 0)[0:64, 0:T], ACT.Copy, ("read", "low", "a", 0), ("low ready", "a", 0))
            act(lows["g"], pk("low", "g", 0)[:, 0:T], ACT.Sigmoid, ("read", "low", "g", 0), ("low ready", "g", 0))
            act(lows["g1"], pk("low", "g", 1)[0:32, 0:T], ACT.Sigmoid, ("read", "low", "g", 1), ("low ready", "g", 1))
            for key, dst, v in (("w", sig, "rw_w0"), ("a", aa, "rw_a0")):
                for c in range(C):
                    act(dst[:, c, :], pk("up", key, c)[:, 0:T], ACT.Sigmoid, ("read", "up", key, c), (key + " ready",),
                        bias=vcol(v, c))
            for c in range(C):
                act(gb[:, c, :], pk("up", "g", c)[:, 0:T], ACT.Copy, ("read", "up", "g", c))
            def projected(n, dst, cc):
                for c in cc:
                    act(dst[:, c, :], pk(("rkv", n), c)[:, 0:T], ACT.Copy, ("read", ("rkv", n), c), ("rkv ready", n))

            projected(1, kb, range(C))
            ac.wait("kk raw")
            act(nrm[:, :, :], kk[:, :, :], ACT.Square, ("kk squares",))
            projected(0, rr, range(C))
            ac.wait("cum")
            act(dec[:, :, :], cum[:, :, :], ACT.Exp, ("dec",), scale=-DECAY)
            ac.wait("kk ms")
            act(head16, head16, ACT.Sqrt, ("kk root",))
            ac.wait("dm arg")
            act(sig[:, :, :], sig[:, :, :], ACT.Exp, ("dm",), scale=-DECAY)
            projected(2, vb, range(4))
            ac.wait("kk sum", 0)
            act(dinv[:, :, :], cum[:, :, :], ACT.Exp, ("dinv",), scale=DECAY)
            projected(2, vb, range(4, C))
            for j in range(NCH):
                t = slice(CH * j, CH * (j + 1))
                for nm, dst in (("v", vb), ("b", aa), ("k", kb)):
                    pb = pk("tok" + nm, j)
                    act(dst[:, :, t], pb[:, :].rearrange("p (c t) -> p c t", c=C), ACT.Copy,
                        ("read", "tok" + nm, j), ("tok ready", j))
                mod_copy(range(A_STEPS * j, A_STEPS * (j + 1)))
            for l in range(2, 7):
                for j in range(NCH):
                    t = slice(CH * j, CH * (j + 1))
                    pb = pk("W", l, j)
                    act(wmat[:, :, t], pb[:, :].rearrange("p (c t) -> p c t", c=C), ACT.Copy,
                        ("read", "W", l, j), ("W ready", l, j))
                mod_copy(steps_of_level(l))
            pb = pk("s0")
            act(state[:, 1], pb[:, :].rearrange("p (c t) -> p c t", c=C), ACT.Copy, ("read", "s0"), ("state", 4))

            def evac(dst, *key):
                act(dst, pk(*key)[:, :].rearrange("p (c t) -> p c t", c=C), ACT.Copy, ("read",) + key,
                    (key[0] + " ready", key[1]))

            def evac_y(j, hf):
                act(rr[:, 4 * hf:4 * hf + 4, CH * j:CH * (j + 1)],
                    pk(("Y", hf), j)[:, 256 * hf:256 * hf + 256].rearrange("p (c t) -> p c t", c=4), ACT.Copy,
                    ("read", ("Y", hf), j), ("y all",))

            for name, b in (("RHS", 0), ("U", 1)):
                for j in (0, 4):
                    evac(rhs_of(j)[:, b], name, j)
            evac_y(0, 0)
            evac_y(0, 1)
            for j, before in ((1, 4), (2, 1), (3, 2)):
                evac(rhs_of(j)[:, 0], "RHS", j)
                evac_y(before, 0)
                evac(rhs_of(j)[:, 1], "U", j)
                evac_y(before, 1)
            evac_y(3, 0)
            evac_y(3, 1)
            for r_ in range(2):
                pb = pk("sout", r_)
                act(swo[:, r_], pb[:, :].rearrange("p (c t) -> p c t", c=C), ACT.Copy, ("read", "sout", r_),
                    ("swout ready", r_), ("read", "swout", r_))
            for c in range(C):
                ac.wait("yc", c)
                act(E[0][:, c, :], rr[:, c, :], ACT.Square, ("yc squares", c))
            ac.wait("y var")
            act(head16, head16, ACT.Sqrt, ("y root",))

            def moe(l):
                S = moe_sems[l]
                squares(f"B{l}")
                root(f"B{l}")
                modulated(f"B{l}", hT, hT)
                eng.wait_ge(in_sems["out_written"], (64, 160)[l])
                for j, (t0, k) in enumerate(TILES):
                    for hf in range(2):
                        cols = slice(512 * hf, 512 * hf + 512)
                        pb = pk("htok", l, j, hf)[0:k, :]
                        act(hpart[0:k, 0, j, cols], pb, ACT.Copy)
                        act(htok[0:k, j, cols], pb, ACT.Copy, ("read", "htok", l, j, hf), ("htok ready", l, j, hf))
                ac.wait("group max", l)
                ac.wait("top2", l)
                act(rt[:, 6:9, 0:4], rt[:, 3:6, 0:4], ACT.Exp)
                act(rt[:, 36, 0:3], rt[:, 35, 0:3], ACT.Exp, ("route exp", l))
                for j, (t0, k) in enumerate(TILES):
                    ac.wait("rest", l, j)
                    act(hpart[0:k, 1, j, :], htok[0:k, j, :], ACT.Copy, ("middle", l, j))
                ac.wait("passes", l)
                nb = eng.value_load(passes[0:1, 2 * l:2 * l + 1], min_val=1, max_val=5)

                def gathered(k, u):
                    for hf in range(2):
                        eng.wait_ge(S["xe_made"], 4 * k + 2 * u + hf + 1)
                        eng.activation(xe[:, u, 4 * hf:4 * hf + 4, :],
                                       ps[1 + hf][:, :].rearrange("p (c s) -> p c s", c=4),
                                       ACT.Copy).then_inc(S["xe_ready"], 1)

                def experts(k, ahead):
                    for u in range(2):
                        eng.wait_ge(S["w_ready"], 4 * k + 2 * u + 2)
                        eng.activation(selT[:, u, :], ps[1 + u][:, 0:T], ACT.Copy).then_inc(S["selT_ready"], 1)
                    for u in range(2):
                        eng.wait_ge(S["gu_made"], 2 * k + u + 1)
                        eng.activation(silu[:, u, :], ps[3 + 4 * u][:, 0:FE], ACT.Silu).then_inc(S["silu_ready"], 1)
                    if ahead:
                        gathered(k + 1, 0)
                    for u in range(2):
                        for n in range(2):
                            eng.wait_ge(S["down_made"], 4 * k + 2 * u + n + 1)
                            eng.activation(dpart[:, u, 0, 512 * n:512 * n + 512], ps[4 + n][:, :],
                                           ACT.Copy).then_inc(S["hi_ready"], 1)
                        for n in range(2):
                            eng.wait_ge(S["rest_ready"], 4 * k + 2 * u + n + 1)
                            eng.activation(dpart[:, u, 1, 512 * n:512 * n + 512], rest[:, n, :],
                                           ACT.Copy).then_inc(S["mid_ready"], 1)
                    if ahead:
                        gathered(k + 1, 1)

                with eng.Fori(0, nb) as p:
                    for u in range(2):
                        gathered(8 * p, u)
                    with eng.Fori(0, EXP // 4 - 1) as k_:
                        experts(8 * p + k_, True)
                    experts(8 * p + 7, False)
                ac.wait("x moe", l)

            moe(0)
            squares("A1")
            root("A1")
            modulated("KV", E[0], hkv)
            for c in range(4):
                dst = kraw[:, c, :] if c < 2 else vT[:, c - 2, :]
                act(dst, pk("kv", c)[:, 0:T], ACT.Identity, ("read", "kv", c), ("kraw", c) if c < 2 else ("vT", c - 2),
                    bias=vcol("b_kv", c))
            act(kT[:, 0:2, 256:384], pk("kcache")[:, 0:256].rearrange("p (c t) -> p c t", c=2), ACT.Copy,
                ("read", "kcache"), ("kcache ready",))
            for c in range(2):
                act(kT[:, 2 + c, :], pk("kswap", c)[:, 0:448], ACT.Copy, ("read", "kswap", c), ("kswapped", c))
            for w in range(5):
                act(v64[:, w if w < 4 else 6, :], pk("v64", w)[0:64, 0:256], ACT.Copy, ("read", "v64", w), ("v64",))
            for w in range(3):
                act(k64[:, w, :], pk("k64", w)[0:64, 0:256], ACT.Copy, ("read", "k64", w), ("k64",))
            for c in range(C):
                act(q[:, c, :], pk("q", c)[:, 0:T], ACT.Identity, ("read", "q", c), ("qraw", c),
                    bias=vcol("at_b_q", c))

            def exps(n):
                W = min(n + 1, 3) * CH if n < 4 else 192
                prob, att = prob2[n % 2], att2[:, n % 2]
                for b in range(4):
                    ac.wait("row max", n, b)
                    for cc in range(2):
                        c = 2 * b + cc
                        act(prob[:, c, 0:W], ps[seen_bank(("score", n, b))][:, 256 * cc:256 * cc + W], ACT.Exp,
                            ("read", "score", n, b), ("exp", n, c), bias=att[:, 1, c:c + 1], scale=SCALE,
                            accum_out=att[:, 2, c:c + 1])
                act(att[:, 3, :], att[:, 4, :], ACT.Exp, ("sink exp", n))

            exps(0)
            for n in range(NCH):
                parts = min(n + 1, 3) if n < 4 else 3
                for w in range(3):
                    if w == 2 and n + 1 < NCH:
                        exps(n + 1)
                    for hf in range(2 if w < parts else 0):
                        act(pT[:, w, 4 * hf:4 * hf + 4, :],
                            pk("pT", n, w, hf)[0:64, :].rearrange("p (c s) -> p c s", c=4), ACT.Copy,
                            ("read", "pT", n, w, hf), ("pT ready", n))
                act(oT[:, :, CH * n:CH * (n + 1)], pk("o", n)[:, :].rearrange("p (c t) -> p c t", c=C), ACT.Copy,
                    ("read", "o", n), ("oT", n))
            moe(1)
            squares("F")
            root("F")
            for j, (t0, k) in enumerate(TILES):
                for hf in range(2):
                    act(ytok[0:k, j, 512 * hf:512 * hf + 512], pk("ytok", j, hf)[0:k, :], ACT.Copy,
                        ("read", "ytok", j, hf), ("ytok", j))

        @block.vector
        def _(eng):
            ve = Engine(eng, "dve_done", sems, known, seen)

            def pk(*key):
                ve.wait(*key)
                return ps[seen_bank(key)]

            def op(ins, *keys):
                ve.did(ins, *keys)

            def tt_(out, a, b, o_, *keys):
                op(eng.tensor_tensor(out, a, b, o_), *keys)

            def ts(out, a, s1, s2, o1, o2, *keys):
                op(eng.tensor_scalar(out, a, s1, s2, o1, o2), *keys)

            def stt(out, a, s_, b, o1, o2, *keys):
                op(eng.scalar_tensor_tensor(out, a, s_, b, o1, o2), *keys)

            M, A_ = ALU.mult, ALU.add

            op(eng.memset(cs[:, :, :], 0.0))
            op(eng.memset(state[:, 0], 0.0), ("state", 0))
            op(eng.tensor_copy(vec[:, :], pk("vec")[:, 0:3 * P]), ("read", "vec"), ("vec ready",))
            ve.wait("silu c")
            for r in range(2):
                op(eng.tensor_copy(cs[:, :, r], small[:, 8 * r:8 * r + 8]), ("cs",))
            for c in range(C):
                op(eng.tensor_copy(x[:, c, :], pk("xT", c)[:, 0:T]), ("read", "xT", c), ("x for", "A0", c // 2))

            def turned(g, dst, bias):
                v = pk("modT", g)[:, :].rearrange("p (q j r) -> p r q j", q=4, j=4)
                for r in range(2):
                    tt_(dst(r).rearrange("p (j q) -> p q j", q=4), v[:, r],
                        vec[:, bias:bias + 16].rearrange("p (j q) -> p q j", q=4), A_, ("read", "modT", g),
                        ("mod ready", g))

            def mods_out(steps):
                for g in mods_turned(steps):
                    _w, l, blk, b = MODS[g]
                    if l is None:
                        turned(g, lambda r: kvmod[:, r, :], VCOL[b])
                    else:
                        turned(g, lambda r: mod[:, l, r, 16 * blk:16 * blk + 16], VCOL[b] + 48 * l + 16 * blk)

            def rms(tag):
                ts(rstd[:, :], pk("ms", tag)[:, 0:T], 1.0 / D, RMS_EPS, M, A_, ("read", "ms", tag), ("ms ready", tag))
                ve.wait("root", tag)
                op(eng.reciprocal(rstd[:, :], rstd[:, :]))

            def coefficients(tag, g):
                md, sh = mod_of(tag)
                coef = coef2[:, tag == "A1"]
                for r in range(2):
                    ts(coef[:, r, :], md(r)[:, sh + C:sh + 2 * C], 1.0, None, A_, ALU.bypass)
                ve.settle()
                for r in range(2):
                    tt_(coef[:, r, :], coef[:, r, :], g, M, ("coef", tag))
                ve.settle()

            def normed(tag, dst):
                for cc in (slice(C - ACT_CHUNKS, C), slice(0, C - ACT_CHUNKS)):
                    n = cc.stop - cc.start
                    tt_(dst[:, cc, :], x[:, cc, :], bmid(rstd[:, :], n), M, ("normed", tag, cc.start))
                ve.settle()

            def modulated(tag, src, dst, cc):
                md, sh = mod_of(tag)
                coef = coef2[:, tag == "A1"]
                for c in cc:
                    for r, t0, k in SEQS:
                        ts(dst[:, c, t0:t0 + k], src[:, c, t0:t0 + k], coef[:, r, c:c + 1],
                           md(r)[:, sh + c:sh + c + 1], M, A_, ("h", tag, c))
                ve.settle()

            def gated(tag, name, l, gate, *key):
                for c in range(C):
                    pb = pk(*key, c)
                    for r, t0, k in SEQS:
                        stt(x[:, c, t0:t0 + k], pb[:, t0:t0 + k], mod[:, l, r, gate + c:gate + c + 1],
                            x[:, c, t0:t0 + k], M, A_, ("read",) + key + (c,), name,
                            ("x for", tag, c // 2))
                ve.settle()

            rms("A0")
            ve.settle()
            normed("A0", h0)
            turned(-1, lambda r: mod[:, 0, r, 0:16], VCOL["ada_b"])
            ve.settle()
            coefficients("A0", vcol("norm_g", 0, C))
            modulated("A0", h0, h0, range(C - ACT_CHUNKS))
            ve.wait("h", "A0", C - 1)
            tt_(diff[:, :, 1:T], h0[:, :, 0:T - 1], h0[:, :, 1:T], ALU.subtract)
            ve.settle()
            ts(diff[:, :, 0], h0[:, :, 0], -1.0, None, M, ALU.bypass)
            tt_(diff[:, :, SEQ], vcol("state_shift", 0, C), h0[:, :, SEQ], ALU.subtract)
            ve.settle()
            for k, n in enumerate(MIX):
                if k >= 2:
                    ve.wait("xm used", MIX[k - 2])
                for c in range(C):
                    stt(xm[n][:, c, :], diff[:, c, :], vcol("rw_mu", 8 * n + c), h0[:, c, :], M, A_, ("xm", n, c),
                        ("xm", n))
            ve.wait("rkv ready", 1)
            ve.wait("a ready")
            eng.wait_ge(in_sems["wkvc_in"], 16)
            tt_(kk[:, :, :], kb[:, :, :], bc(vcol("rw_k_k", 0, C), T), M, ("kk raw",))
            stt(tmp[:, :, :], aa[:, :, :], -1.0, bc(vcol("rw_k_a", 0, C), T), A_, M)
            ve.settle()
            stt(kb[:, :, :], tmp[:, :, :], 1.0, kb[:, :, :], A_, M)
            ve.settle()
            ve.wait("w ready")
            ve.wait("xm used", 0)
            for c in range(C):
                op(eng.tensor_tensor_scan(cum[:, c, :], wcst("scan"), sig[:, c, :], 0.0, M, A_), ("cum",))
            ts(head16, pk("kk sum", 0)[0:16, 0:T], 1e-24, None, ALU.max, ALU.bypass, ("read", "kk sum", 0),
               ("kk ms",))
            ve.settle()
            tt_(sig[:, :, :], cum[:, :, :], sig[:, :, :], ALU.subtract, ("dm arg",))
            ve.wait("kk root")
            op(eng.reciprocal(head16, head16), ("kk rstd",))
            ve.wait("rkv ready", 0)
            tt_(tmp[:, :, :], rr[:, :, :], kb[:, :, :], M)
            ve.settle()
            tt_(tmp[:, :, :], tmp[:, :, :], bc(vcol("rw_r_k", 0, C), T), M, ("rk",))
            ve.wait("dec")
            tt_(rr[:, :, :], rr[:, :, :], dec[:, :, :], M)
            op(eng.tensor_copy(dend[:, :, :], dec[:, :, CH - 1:T:CH]))
            for c in range(C):
                tt_(kk[:, c, :], kk[:, c, :], pk("kk rstd all", c)[:, 0:T], M, ("read", "kk rstd all", c), ("kk done",))
            op(eng.tensor_copy(head16b, pk("bonus sum", 0)[0:16, 0:T]), ("read", "bonus sum", 0), ("bonus 16",))
            ve.settle()
            tt_(aa[:, :, :], kk[:, :, :], aa[:, :, :], M)
            ve.wait("dm")
            ve.settle()
            stt(kk[:, :, :], kk[:, :, :], -1.0, sig[:, :, :], M, M)
            ve.wait("dinv")
            tt_(aa[:, :, :], aa[:, :, :], dinv[:, :, :], M)
            tt_(kb[:, :, :], kb[:, :, :], dinv[:, :, :], M)
            ve.wait("rkv ready", 2)
            for c in range(C):
                tt_(bonus[:, c, :], vb[:, c, :], pk("bonus all", c)[:, 0:T], M, ("read", "bonus all", c),
                    ("wkv ready",))
            ve.settle()
            for j in range(NCH):
                t = slice(CH * j, CH * (j + 1))
                for nm, strict, incl in (("b", nt, arb), ("k", aak, ark)):
                    for hf in range(2):
                        pb = pk("A" + nm, j, hf)[:, :].rearrange("p (c b t) -> p c b t", c=4, b=2)
                        cs4 = slice(4 * hf, 4 * hf + 4)
                        tt_(strict[:, cs4, t], pb[:, :, 0, :], bmid(wcst("maskA")[:, 0:64], 4), M)
                        tt_(incl[:, cs4, t], pb[:, :, 1, :], bmid(wcst("maskA")[:, 64:128], 4), M,
                            ("read", "A" + nm, j, hf))
                pb = pk("N1", j)[:, :].rearrange("p (c t) -> p c t", c=C)
                ve.settle()
                tt_(tmat[:, :, t], pb, bmid(wcst("lev1n"), C), M, ("read", "N1", j))
                tt_(tt[:, :, t], nt[:, :, t], bmid(wcst("lev")[:, 0:64], C), M)
                ve.settle()
                tt_(tmat[:, :, t], tmat[:, :, t], bmid(cst("i64"), C), A_)
                tt_(tt[:, :, t], tt[:, :, t], bmid(cst("i64"), C), A_)
                tt_(nl[:, :, t], nt[:, :, t], bmid(wcst("lev")[:, 64:128], C), M, ("level", 2, j))
                mods_out(range(A_STEPS * j, A_STEPS * (j + 1)))
                ve.settle()
            for l in range(2, 7):
                for j in range(NCH):
                    t = slice(CH * j, CH * (j + 1))
                    pb = pk("TT", l, j)[:, :].rearrange("p (c t) -> p c t", c=C)
                    if l < 6:
                        ve.wait("TW", l, j)
                    tt_(tt[:, :, t], tt[:, :, t], pb, A_, ("read", "TT", l, j), ("T ready", j), ("inverses",))
                    if l < 6:
                        pb = pk("TW", l, j)[:, :].rearrange("p (c t) -> p c t", c=C)
                        tt_(tmat[:, :, t], tmat[:, :, t], pb, A_, ("read", "TW", l, j))
                        tt_(nl[:, :, t], nt[:, :, t], bmid(wcst("lev")[:, 64 * l:64 * l + 64], C), M,
                            ("level", l + 1, j))
                    mods_out(steps_of_level(l, j))
            ve.settle()
            for j in (0, 4, 1, 2, 3):
                old, new = state_at(j)
                tt_(new, old, pk("S", j)[:, :].rearrange("p (c t) -> p c t", c=C), A_, ("read", "S", j))
                ve.settle()
                tt_(new, new, bc(dend[:, :, j], HD), M, ("state", j + 1) if j < 3 else ("final state", j - 3))
            ve.wait("y all")
            ts(head16, pk("y sum", 0)[0:16, 0:T], 1.0 / HD, None, M, ALU.bypass, ("read", "y sum", 0), ("y mean",))
            for c in range(C):
                tt_(rr[:, c, :], rr[:, c, :], pk("y mean all", c)[:, 0:T], ALU.subtract, ("read", "y mean all", c),
                    ("yc", c))
            ts(head16, pk("yc sum", 0)[0:16, 0:T], 1.0 / HD, GN_EPS, M, A_, ("read", "yc sum", 0), ("y var",))
            ve.wait("y root")
            op(eng.reciprocal(head16, head16), ("y rstd",))
            for c in range(C):
                stt(rr[:, c, :], rr[:, c, :], vcol("rw_lnx_w", c), pk("y rstd all", c)[:, 0:T], M, M,
                    ("read", "y rstd all", c))
                ve.settle()
                stt(rr[:, c, :], rr[:, c, :], vcol("rw_lnx_b", c), bonus[:, c, :], A_, A_)
                ve.settle()
                tt_(rr[:, c, :], rr[:, c, :], gb[:, c, :], M, ("mix out", c), ("mix out",))
            gated("B0", ("x mixed", 0), 0, 16, "wo")

            def moe(l):
                S = moe_sems[l]
                coefficients(f"B{l}", vcol("norm_g", 16 * l + 8, C))
                op(eng.memset(ysum[:, :, :], 0.0))
                rms(f"B{l}")
                ve.settle()
                normed(f"B{l}", hT)
                modulated(f"B{l}", hT, hT, range(C - ACT_CHUNKS))
                op(eng.memset(lg[:, :, :], 0.0))
                op(eng.tensor_copy(ident16[:, :], cst("ident")))
                ve.settle()
                for j, (t0, k) in enumerate(TILES):
                    op(eng.tensor_copy(lg[0:k, j, :], pk("logits", l, j)[0:k, 0:36]), ("read", "logits", l, j))
                ve.settle()
                R = lambda a, n=8: rt[:, a:a + 3, 0:n]
                g4 = lg[:, :, 0:4]
                e32 = lg[:, :, 4:36].rearrange("p j (g e) -> p j g e", g=4)
                sc_ = lambda a: rt[:, a, 0:3]

                def first_one(dst, key, src, mx, n):
                    tt_(R(key, n), src, bc(mx, n), ALU.is_equal)
                    ve.settle()
                    tt_(R(key, n), R(key, n), bmid(cst("down")[:, 8 - n:8], 3), M)
                    ve.settle()
                    op(eng.tensor_reduce(sc_(39), R(key, n), AX.X, ALU.max))
                    ve.settle()
                    tt_(R(dst, n), R(key, n), bc(sc_(39), n), ALU.is_equal)
                    ve.settle()

                op(eng.tensor_reduce(sc_(30), g4, AX.X, ALU.max))
                ve.settle()
                tt_(R(3, 4), g4, bc(sc_(30), 4), ALU.subtract, ("group max", l))
                first_one(12, 9, g4, sc_(30), 4)
                for g in range(4):
                    tt_(g48[:, :, g, :], e32[:, :, g, :], bc(rt[:, 12:15, g], 8), M)
                ve.settle()
                tt_(R(15), g48[:, :, 0, :], g48[:, :, 1, :], A_)
                tt_(R(18), g48[:, :, 2, :], g48[:, :, 3, :], A_)
                ve.settle()
                tt_(R(15), R(15), R(18), A_)
                ve.settle()
                op(eng.tensor_reduce(sc_(33), R(15), AX.X, ALU.max))
                ve.settle()
                first_one(21, 18, R(15), sc_(33), 8)
                stt(R(24), R(21), -3e38, R(15), M, A_)
                ve.settle()
                op(eng.tensor_reduce(sc_(34), R(24), AX.X, ALU.max))
                ve.settle()
                tt_(sc_(35), sc_(34), sc_(33), ALU.subtract, ("top2", l))
                first_one(27, 18, R(24), sc_(34), 8)
                ve.wait("route exp", l)
                op(eng.tensor_reduce(sc_(37), rt[:, 6:9, 0:4], AX.X, A_))
                ts(sc_(38), sc_(36), 1.0, None, A_, ALU.bypass)
                ve.settle()
                tt_(sc_(38), sc_(38), sc_(37), M)
                ve.settle()
                op(eng.reciprocal(sc_(38), sc_(38)))
                ve.settle()
                tt_(sc_(37), sc_(38), sc_(36), M)
                ve.settle()
                tt_(R(15), R(21), bc(sc_(38), 8), M)
                tt_(R(18), R(27), bc(sc_(37), 8), M)
                tt_(R(24), R(21), R(27), A_)
                ve.settle()
                tt_(R(15), R(15), R(18), A_)
                ve.settle()
                for g in range(4):
                    tt_(cw[:, :, 8 * g:8 * g + 8], R(15), bc(rt[:, 12:15, g], 8), M)
                    tt_(msk[:, :, 8 * g:8 * g + 8], R(24), bc(rt[:, 12:15, g], 8), M)
                ve.settle()
                op(eng.memset(msk[64:128, 2, :], 0.0), ("mask", l))
                for j, (t0, k) in enumerate(TILES):
                    ve.wait("middle", l, j)
                    tt_(hpart[0:k, 2, j, :], htok[0:k, j, :], hpart[0:k, 1, j, :], ALU.subtract, ("parts", l))
                op(eng.tensor_copy(cwpart[:, 0], cw[:, :, :]))
                ve.settle()
                tt_(cwrest[:, :, :], cw[:, :, :], cwpart[:, 0], ALU.subtract)
                ve.settle()
                op(eng.tensor_copy(cwpart[:, 1], cwrest[:, :, :]))
                ve.settle()
                tt_(cwpart[:, 2], cwrest[:, :, :], cwpart[:, 1], ALU.subtract)
                pb = pk("rank", l)
                tt_(posn[:, :, :], pb[:, 0:96].rearrange("p (j e) -> p j e", j=3), msk[:, :, :], M)
                op(eng.tensor_reduce(small[:, 0:1], pb[:, 96:96 + EXP], AX.X, ALU.max), ("read", "rank", l))
                ve.settle()
                for a in range(4):
                    ts(small[:, 1 + a:2 + a], small[:, 0:1], float(SLOTS * (a + 1)), None, ALU.is_gt, ALU.bypass)
                ve.settle()
                op(eng.tensor_reduce(small[:, 5:6], small[:, 1:5], AX.X, A_))
                ve.settle()
                ts(passes[:, 2 * l:2 * l + 1], small[:, 5:6], 1.0, None, A_, ALU.bypass)
                op(eng.tensor_copy(passes[:, 2 * l + 1:2 * l + 2], small[:, 5:6]), ("passes", l))
                ve.settle()
                eng.memset(small[:, 8:9], 0.0).then_inc(S["pos_ready"], 1)
                nb = eng.value_load(passes[0:1, 2 * l:2 * l + 1], min_val=1, max_val=5)
                eng.memset(small[:, 9:10], 0.0).then_inc(S["y_added"], 1)

                def select(e, u):
                    for v in range(2):
                        for j, (t0, kt) in enumerate(TILES):
                            a = slice(64 * v, 64 * v + 64)
                            ins = eng.tensor_scalar(sel[0:kt, u, j, a], cst("iota", kt),
                                                    posn[0:kt, j, bass.ds(e + v, 1)], None, ALU.is_equal, ALU.bypass)
                    ins.then_inc(S["sel_ready"], 1)

                def experts(k, e_next):
                    for u in range(2):
                        eng.wait_ge(S["selT_made"], 2 * k + u + 1)
                        for v in range(2):
                            a = slice(64 * v, 64 * v + 64)
                            eng.tensor_reduce(wslot[a, u:u + 1],
                                              ps[1 + u][a, T:T + 6].rearrange("p (s v) -> p v s", s=3)[:, v, :],
                                              AX.X, A_).then_inc(S["w_ready"], 1)
                    for u in range(2):
                        eng.wait_ge(S["silu_ready"], 2 * k + u + 1)
                        if u == 0:
                            eng.wait_ge(S["w_ready"], 4 * k + 4)
                        eng.scalar_tensor_tensor(hid[:, u, :], silu[:, u, :], wslot[:, u:u + 1],
                                                 ps[3 + 4 * u][:, FE:2 * FE], M, M).then_inc(S["h_ready"], 1)
                        if u == 0 and e_next is not None:
                            for w in range(2):
                                select(e_next + 2 * w, w)
                        eng.wait_ge(S["hT_made"], 2 * k + u + 1)
                        eng.tensor_copy(hidT[:, u], ps[0][:, 0:2 * P].rearrange("p (f s) -> p f s", f=2)
                                        ).then_inc(S["hT_ready"], 1)
                    for u in range(2):
                        for n in range(2):
                            eng.wait_ge(S["hi_ready"], 4 * k + 2 * u + n + 1)
                            if u == 1:
                                eng.wait_ge(S["lo_ready0"], 2 * k + n + 1)
                            eng.tensor_tensor(rest[:, n, :], ps[4 + n][:, :], dpart[:, u, 0, 512 * n:512 * n + 512],
                                              ALU.subtract).then_inc(S["rest_ready"], 1)
                    for n in range(2):
                        eng.wait_ge(S["mid_ready"], 4 * k + 3 + n)
                        eng.tensor_tensor(dpart[:, 1, 2, 512 * n:512 * n + 512], rest[:, n, :],
                                          dpart[:, 1, 1, 512 * n:512 * n + 512],
                                          ALU.subtract).then_inc(S["lo_ready1"], 1)
                    for c in range(C):
                        eng.wait_ge(S["y_made"], 8 * k + c + 1)
                        eng.tensor_tensor(ysum[:, c, :], ysum[:, c, :], ps[(6, 7, 3, 0)[c % 4]][:, 0:T],
                                          A_).then_inc(S["y_added"], 1)

                with eng.Fori(0, nb) as p:
                    eng.wait_ge(S["pos_ready"], p + 1)
                    for u in range(2):
                        select(2 * u, u)
                    with eng.Fori(0, EXP // 4 - 1) as k_:
                        experts(8 * p + k_, 4 * k_ + 4)
                    experts(8 * p + 7, None)
                    eng.tensor_scalar(posn[:, :, :], posn[:, :, :], -float(SLOTS), None, A_, ALU.bypass
                                      ).then_inc(S["pos_ready"], 1)
                eng.wait_ge(S["y_added"], 64 * nb + 1)
                for c in range(C):
                    for r, t0, k in SEQS:
                        stt(x[:, c, t0:t0 + k], ysum[:, c, t0:t0 + k], mod[:, l, r, 40 + c:40 + c + 1],
                            x[:, c, t0:t0 + k], M, A_, ("x moe", l), ("x for", "A1" if l == 0 else "F", c // 2))
                ve.settle()

            moe(0)
            coefficients("KV", vcol("kv_norm_g", 0, C))
            coefficients("A1", vcol("norm_g", 16, C))
            rms("A1")
            ve.settle()
            normed("KV", E[0])
            modulated("KV", E[0], hkv, range(C - ACT_CHUNKS))
            modulated("A1", E[0], haq, range(C))
            for r in range(2):
                tt_(bog[:, r, :], vcol("at_b_o", 0, C), mod[:, 1, r, 16:24], M)
            eng.wait_ge(in_sems["attc_in"], 16)
            for c in range(2):
                tt_(krot[:, c, :], acst("sin"), pk("krot", c)[:, 0:T], M, ("read", "krot", c))
                tt_(kraw[:, c, :], kraw[:, c, :], acst("cos"), M)
                ve.settle()
                tt_(kT[:, c, 0:SEQ], kraw[:, c, 0:SEQ], krot[:, c, 0:SEQ], A_)
                tt_(kT[:, c, 384:448], kraw[:, c, SEQ:T], krot[:, c, SEQ:T], A_)
            ve.settle()
            ve.wait("kcache ready")
            ts(small[:, 8:9], small[:, 0:1], 0.0, None, M, ALU.bypass, ("kT whole",))
            for c in range(C):
                tt_(qt[:, c, :], acst("sin"), pk("qrot", c)[:, 0:T], M, ("read", "qrot", c))
                tt_(q[:, c, :], q[:, c, :], acst("cos"), M)
                ve.settle()
                tt_(q[:, c, :], q[:, c, :], qt[:, c, :], A_, ("q ready", c))
            eng.wait_ge(in_sems["sink_in"], 32)

            def row_maxima(n):
                W = min(n + 1, 3) * CH if n < 4 else 192
                att = att2[:, n % 2]
                banks = [pk("score", n, b)[:, :].rearrange("p (c s) -> p c s", c=2)[:, :, 0:W] for b in range(4)]
                for b in range(4):
                    op(eng.tensor_reduce(att[:, 0, 2 * b:2 * b + 2], banks[b], AX.X, ALU.max))
                ve.settle()
                stt(att[:, 1, :], att[:, 0, :], SCALE, sink[:, :], M, ALU.max)
                ve.settle()
                ts(att[:, 1, :], att[:, 1, :], -1.0, None, M, ALU.bypass)
                ve.settle()
                tt_(att[:, 4, :], sink[:, :], att[:, 1, :], A_, *[("row max", n, b) for b in range(4)])

            row_maxima(0)
            for n in range(NCH):
                W = min(n + 1, 3) * CH if n < 4 else 192
                prob, att = prob2[n % 2], att2[:, n % 2]
                ve.wait("sink exp", n)
                tt_(att[:, 5, :], att[:, 2, :], att[:, 3, :], A_)
                ve.settle()
                op(eng.reciprocal(att[:, 5, :], att[:, 5, :]))
                ve.settle()
                for c in range(C):
                    ts(prob[:, c, 0:W], prob[:, c, 0:W], att[:, 5, c:c + 1], None, M, ALU.bypass, ("prob", n, c))
                if n + 1 < NCH:
                    row_maxima(n + 1)
            for c in range(C):
                pb = pk("ao", c)
                for r, t0, k in SEQS:
                    ts(qt[:, c, t0:t0 + k], pb[:, t0:t0 + k], mod[:, 1, r, 16 + c:17 + c], bog[:, r, c:c + 1], M, A_,
                       ("read", "ao", c))
                ve.settle()
                tt_(x[:, c, :], x[:, c, :], qt[:, c, :], A_, ("x mixed", 1), ("x for", "B1", c // 2))
            ve.settle()
            moe(1)
            rms("F")
            ve.settle()
            normed("F", E[0])
            for c in range(C):
                ts(E[1][:, c, :], E[0][:, c, :], vcol("final_norm_g", c), None, M, ALU.bypass, ("h", "F"))


NAMES = ['x_prompt', 'x_sample', 'state_shift', 'state_wkv', 'cache_k', 'cache_v', 'c_prompt', 'c_sample', 'ada_w',
         'ada_b', 'norm_g', 'rw_mu', 'rw_w_rkv', 'rw_w0', 'rw_w1', 'rw_w2', 'rw_a0', 'rw_a1', 'rw_a2', 'rw_g1',
         'rw_g2', 'rw_k_k', 'rw_k_a', 'rw_r_k', 'rw_lnx_w', 'rw_lnx_b', 'rw_w_o', 'kv_ada_w', 'kv_ada_b', 'kv_norm_g',
         'w_kv', 'b_kv', 'at_w_q', 'at_b_q', 'at_sinks', 'at_w_o', 'at_b_o', 'moe_w_group', 'moe_w_expert',
         'moe_w_gu', 'moe_w_down', 'final_norm_g']
OUTS = [(1, SEQ, D), (1, DEC, D), (1, 1, D), (1, 1, HEADS, HD, HD), (1, 128, NKV, HD), (1, 128, NKV, HD), (1, 1, D),
        (1, 1, HEADS, HD, HD), (1, DEC, NKV, HD), (1, DEC, NKV, HD)]


def kernel(**inputs):
    import concourse.bacc as bacc
    from concourse.bass_utils import run_bass_kernel_spmd as run

    arrays = {n: np.ascontiguousarray(inputs[n]) for n in NAMES}
    arrays.update(constants())

    def program(known):
        nc = bacc.Bacc("TRN2", target_bir_lowering=False, num_devices=1)
        i = {n: nc.dram_tensor(f"in_{n}", a.shape, mybir.dt.from_np(a.dtype), kind="ExternalInput").ap()
             for n, a in arrays.items()}
        o = [nc.dram_tensor(f"out_{k}", s, F32, kind="ExternalOutput").ap() for k, s in enumerate(OUTS)]
        seen = Counts()
        build(nc, i, o, known, seen)
        return nc, seen

    _, counts = program(None)
    nc, _ = program(counts)
    r = run(nc, [{f"in_{n}": a for n, a in arrays.items()}], core_ids=[0])
    return tuple(r.results[0][f"out_{k}"] for k in range(len(OUTS)))
```
